# Optimizing a Trainium2 kernel written in Bass

```python
import math
import jax, jax.numpy as jnp
from jax import lax
import numpy as np

D_MODEL = 1024
BATCH = 1
SEQ = 512
DEPTH = 1

CHUNK = 64
EPS = 1e-6
A_HEADS = 8
A_DK = 128
A_DV = 256
CONV_W = 4
B_HEADS = 4
B_DK = 256
B_DV = 512
ROPE_BASE = 10000.0
D_FF = 4 * D_MODEL

A_QK = A_HEADS * A_DK
A_V = A_HEADS * A_DV
B_QK = B_HEADS * B_DK
B_V = B_HEADS * B_DV
IN_SIZES = (A_QK, A_QK, A_V, A_V, A_HEADS, A_HEADS, B_QK, B_QK, B_V, B_V, D_MODEL, D_MODEL)
D_IN = sum(IN_SIZES)


def rmsnorm(x, w):
    xf = x.astype(jnp.float32)
    y = xf * lax.rsqrt(jnp.mean(xf * xf, axis=-1, keepdims=True) + EPS)
    return (y * w.astype(jnp.float32)).astype(x.dtype)

def l2norm(x):
    xf = x.astype(jnp.float32)
    return (xf * lax.rsqrt(jnp.sum(xf * xf, axis=-1, keepdims=True) + EPS)).astype(x.dtype)

def _split_cols(t, sizes):
    out, start = [], 0
    for s in sizes:
        out.append(t[..., start:start + s])
        start += s
    return out

def causal_depthwise_conv(x, w):
    k_taps, s = w.shape[0], x.shape[1]
    xp = jnp.pad(x, ((0, 0), (k_taps - 1, 0), (0, 0)))
    y = xp[:, 0:s] * w[0]
    for j in range(1, k_taps):
        y = y + xp[:, j:j + s] * w[j]
    return y

def rotary(t, positions):
    d = t.shape[-1]
    inv_freq = ROPE_BASE ** (-jnp.arange(0, d, 2, dtype=jnp.float32) / d)
    ang = positions.astype(jnp.float32)[:, None] * inv_freq[None, :]
    cos = jnp.cos(ang)[None, :, None, :]
    sin = jnp.sin(ang)[None, :, None, :]
    t1, t2 = t[..., :d // 2], t[..., d // 2:]
    return jnp.concatenate([t1 * cos - t2 * sin, t1 * sin + t2 * cos], axis=-1).astype(t.dtype)

def to_chunks(t):
    b, s, h = t.shape[:3]
    t = t.reshape(b, s // CHUNK, CHUNK, h, *t.shape[3:])
    return jnp.moveaxis(t, 3, 1)

def from_chunks(t):
    t = jnp.moveaxis(t, 1, 3)
    return t.reshape(t.shape[0], t.shape[1] * t.shape[2], *t.shape[3:])

def chunk_gated_delta_rule(q, k, v, beta, g):
    dtype = v.dtype
    q, k, v = (to_chunks(t.astype(jnp.float32)) for t in (q, k, v))
    beta, g = (to_chunks(t.astype(jnp.float32)) for t in (beta, g))
    g_cum = jnp.cumsum(g, axis=-1)
    idx = jnp.arange(CHUNK)
    causal = idx[:, None] >= idx[None, :]
    strict = idx[:, None] > idx[None, :]
    decay = jnp.exp(jnp.where(causal, g_cum[..., :, None] - g_cum[..., None, :], -jnp.inf))
    k_beta = k * beta[..., None]
    lower = jnp.where(strict, jnp.einsum('bhncd,bhnmd->bhncm', k_beta, k) * decay, 0.0)
    eye = jnp.broadcast_to(jnp.eye(CHUNK, dtype=jnp.float32), lower.shape)
    t_inv = lax.linalg.triangular_solve(lower, eye, left_side=True, lower=True, unit_diagonal=True)
    u = jnp.einsum('bhncm,bhnme->bhnce', t_inv, v * beta[..., None])
    w = jnp.einsum('bhncm,bhnmd->bhncd', t_inv, k_beta * jnp.exp(g_cum)[..., None])
    attn = jnp.where(causal, jnp.einsum('bhncd,bhnmd->bhncm', q, k) * decay, 0.0)
    q_exp = q * jnp.exp(g_cum)[..., None]
    g_last = g_cum[..., -1:]
    k_dec = k * jnp.exp(g_last - g_cum)[..., None]
    last_dec = jnp.exp(g_last[..., 0])

    def step(state, inp):
        qe, ww, uu, aqk, kd, ld = inp
        v_new = uu - jnp.einsum('bhck,bhkv->bhcv', ww, state)
        o = jnp.einsum('bhck,bhkv->bhcv', qe, state) + jnp.einsum('bhcm,bhmv->bhcv', aqk, v_new)
        state = state * ld[..., None, None] + jnp.einsum('bhck,bhcv->bhkv', kd, v_new)
        return state, o

    b, h = q.shape[0], q.shape[1]
    state0 = jnp.zeros((b, h, q.shape[-1], v.shape[-1]), jnp.float32)
    xs = tuple(jnp.moveaxis(t, 2, 0) for t in (q_exp, w, u, attn, k_dec, last_dec))
    _, o = lax.scan(step, state0, xs)
    return from_chunks(jnp.moveaxis(o, 0, 2)).astype(dtype)

def chunk_retention(q, k, v):
    dtype = v.dtype
    q, k, v = (to_chunks(t.astype(jnp.float32)) for t in (q, k, v))
    h = q.shape[1]
    log_gamma = jnp.log1p(-jnp.exp2(-5.0 - jnp.arange(h, dtype=jnp.float32)))
    pos = jnp.arange(CHUNK, dtype=jnp.float32)
    dist = jnp.abs(pos[:, None] - pos[None, :])
    intra = jnp.exp(log_gamma[:, None, None] * dist)
    scores = jnp.einsum('bhncd,bhnmd->bhncm', q, k) * intra[None, :, None]
    o_intra = jnp.einsum('bhncm,bhnme->bhnce', scores, v)
    q_dec = jnp.exp(log_gamma[:, None] * (pos + 1.0))[None, :, :, None]
    k_dec = jnp.exp(log_gamma[:, None] * (CHUNK - 1.0 - pos))[None, :, :, None]
    chunk_dec = jnp.exp(log_gamma * CHUNK)[None, :, None, None]

    def step(state, inp):
        qc, kc, vc = inp
        o = jnp.einsum('bhcd,bhde->bhce', qc * q_dec, state)
        state = state * chunk_dec + jnp.einsum('bhcd,bhce->bhde', kc * k_dec, vc)
        return state, o

    state0 = jnp.zeros((q.shape[0], h, q.shape[-1], v.shape[-1]), jnp.float32)
    xs = tuple(jnp.moveaxis(t, 2, 0) for t in (q, k, v))
    _, o_inter = lax.scan(step, state0, xs)
    o = o_intra + jnp.moveaxis(o_inter, 0, 2)
    return from_chunks(o).astype(dtype)

def hybrid_layer(x, n_mix_pre, n_mix_post, n_mlp_pre, n_mlp_post, w_in, conv_a, a_log, dt_bias,
                 norm_a, norm_b, w_br_a, w_br_b, w_out, w_up, w_down):
    b, s, _ = x.shape
    xn = rmsnorm(x, n_mix_pre)
    proj = xn @ w_in
    qa, ka, va, za, beta_logit, a_dt, qb, kb, vb, gb, gate_a, gate_b = _split_cols(proj, IN_SIZES)

    qkv = jax.nn.silu(causal_depthwise_conv(jnp.concatenate([qa, ka, va], axis=-1), conv_a))
    qa, ka, va = _split_cols(qkv, (A_QK, A_QK, A_V))
    qa = l2norm(qa.reshape(b, s, A_HEADS, A_DK)) * (A_DK ** -0.5)
    ka = l2norm(ka.reshape(b, s, A_HEADS, A_DK))
    va = va.reshape(b, s, A_HEADS, A_DV)
    beta = jax.nn.sigmoid(beta_logit)
    g = -jnp.exp(a_log) * jax.nn.softplus(a_dt + dt_bias)
    oa = chunk_gated_delta_rule(qa, ka, va, beta, g)
    oa = rmsnorm(oa, norm_a) * jax.nn.silu(za.reshape(b, s, A_HEADS, A_DV))
    ya = oa.reshape(b, s, A_V) @ w_br_a

    positions = jnp.arange(s)
    qb = rotary(qb.reshape(b, s, B_HEADS, B_DK), positions)
    kb = rotary(kb.reshape(b, s, B_HEADS, B_DK), positions) * (B_DK ** -0.5)
    vb = vb.reshape(b, s, B_HEADS, B_DV)
    ob = chunk_retention(qb, kb, vb)
    ob = rmsnorm(ob, norm_b.reshape(B_HEADS, B_DV)) * jax.nn.silu(gb.reshape(b, s, B_HEADS, B_DV))
    yb = ob.reshape(b, s, B_V) @ w_br_b

    mix = (jax.nn.sigmoid(gate_a) * ya + jax.nn.sigmoid(gate_b) * yb) @ w_out
    x = x + rmsnorm(mix, n_mix_post)

    hn = rmsnorm(x, n_mlp_pre)
    ff = jnp.square(jax.nn.relu(hn @ w_up)) @ w_down
    return x + rmsnorm(ff, n_mlp_post)

def first_inputs(seed: int = 0) -> dict:
    key = jax.random.key(seed)
    ks = jax.random.split(key, 16)
    L = DEPTH

    def nrm(k, shape, fan_in):
        return jax.random.normal(k, shape, jnp.float32) * fan_in ** -0.5

    def gain(k, shape):
        return 1.0 + 0.05 * jax.random.normal(k, shape, jnp.float32)

    x = jax.random.normal(ks[0], (BATCH, SEQ, D_MODEL), jnp.float32)
    dt = jnp.exp(jax.random.uniform(ks[8], (L, A_HEADS), jnp.float32,
                                    minval=math.log(1e-3), maxval=math.log(1e-1)))
    dt_bias = dt + jnp.log(-jnp.expm1(-dt))
    a_log = jnp.log(jax.random.uniform(ks[9], (L, A_HEADS), jnp.float32, minval=1.0, maxval=16.0))
    return {
        "x": x,
        "norm_mix_pre": gain(ks[1], (L, D_MODEL)),
        "norm_mix_post": gain(ks[2], (L, D_MODEL)),
        "norm_mlp_pre": gain(ks[3], (L, D_MODEL)),
        "norm_mlp_post": gain(ks[4], (L, D_MODEL)),
        "w_in": nrm(ks[5], (L, D_MODEL, D_IN), D_MODEL),
        "conv_a": nrm(ks[6], (L, CONV_W, 2 * A_QK + A_V), CONV_W),
        "a_log": a_log,
        "dt_bias": dt_bias,
        "norm_a": gain(ks[7], (L, A_DV)),
        "norm_b": gain(ks[10], (L, B_V)),
        "w_br_a": nrm(ks[11], (L, A_V, D_MODEL), A_V),
        "w_br_b": nrm(ks[12], (L, B_V, D_MODEL), B_V),
        "w_out": nrm(ks[13], (L, D_MODEL, D_MODEL), D_MODEL),
        "w_up": nrm(ks[14], (L, D_MODEL, D_FF), D_MODEL),
        "w_down": nrm(ks[15], (L, D_FF, D_MODEL), D_FF),
    }

def first_block(x, norm_mix_pre, norm_mix_post, norm_mlp_pre, norm_mlp_post, w_in, conv_a, a_log,
              dt_bias, norm_a, norm_b, w_br_a, w_br_b, w_out, w_up, w_down):
    for l in range(DEPTH):
        x = hybrid_layer(x, norm_mix_pre[l], norm_mix_post[l], norm_mlp_pre[l], norm_mlp_post[l],
                         w_in[l], conv_a[l], a_log[l], dt_bias[l], norm_a[l], norm_b[l],
                         w_br_a[l], w_br_b[l], w_out[l], w_up[l], w_down[l])
    return x


GRID_W = 64
HEAD_DIM = 64
NA_HEADS = 8
NA_KH_MAX = 8
NA_KW = 16
NA_QBLK = 16
NA_BAND = 2 * NA_KW
NA_W = NA_HEADS * HEAD_DIM
GQA_HEADS = 8
GQA_KV_HEADS = 2
GQA_QBLK = 128
ROPE_THETA = 10000.0
GQA_Q_W = GQA_HEADS * HEAD_DIM
GQA_KV_W = GQA_KV_HEADS * HEAD_DIM
MEM_TOKENS = 256
MEM_HEADS = 4
MEM_HEAD_DIM = 128
MEM_W = MEM_HEADS * MEM_HEAD_DIM
N_BRANCH = 3
BRANCH_WIDTH = 512
GATE_W = N_BRANCH * D_MODEL
IN_W = 3 * NA_W + GQA_Q_W + 2 * GQA_KV_W + MEM_W + GATE_W
N_EXPERTS = 16
EC_CAPACITY_FACTOR = 2
D_FF_EXPERT = 1024
LN_EPS = 1e-5
RMS_EPS = 1e-6
DN_ALPHA = (2 * DEPTH) ** 0.25
DN_BETA = (8 * DEPTH) ** -0.25
NEG_INF = -1e30


def _split_points():
    sizes = (NA_W, NA_W, NA_W, GQA_Q_W, GQA_KV_W, GQA_KV_W, MEM_W)
    return tuple(int(v) for v in np.cumsum(sizes))

def layer_norm(x, g, b):
    xf = x.astype(jnp.float32)
    mu = jnp.mean(xf, axis=-1, keepdims=True)
    var = jnp.mean(jnp.square(xf - mu), axis=-1, keepdims=True)
    return ((xf - mu) * lax.rsqrt(var + LN_EPS) * g.astype(jnp.float32) + b.astype(jnp.float32)).astype(x.dtype)

def rms_norm(x, g):
    xf = x.astype(jnp.float32)
    ms = jnp.mean(jnp.square(xf), axis=-1, keepdims=True)
    return (xf * lax.rsqrt(ms + RMS_EPS) * g.astype(jnp.float32)).astype(x.dtype)

def axial_rope_tables(seq_len):
    t = jnp.arange(seq_len)
    row = (t // GRID_W).astype(jnp.float32)
    col = (t % GRID_W).astype(jnp.float32)
    half = HEAD_DIM // 2
    inv = ROPE_THETA ** (-jnp.arange(0, half, 2, dtype=jnp.float32) / half)
    ang = jnp.concatenate([row[:, None] * inv, col[:, None] * inv], axis=-1)
    return jnp.cos(ang), jnp.sin(ang)

def apply_rope(x, cos, sin):
    xf = x.astype(jnp.float32)
    x1, x2 = xf[..., 0::2], xf[..., 1::2]
    c, s = cos[None, :, None, :], sin[None, :, None, :]
    out = jnp.stack([x1 * c - x2 * s, x1 * s + x2 * c], axis=-1).reshape(x.shape)
    return out.astype(x.dtype)

def neighbourhood_attention(q, k, v, rpb):
    S, H, dh = q.shape
    rows = S // GRID_W
    kh = min(NA_KH_MAX, rows)
    ncb = GRID_W // NA_QBLK
    qg = q.reshape(rows, ncb, NA_QBLK, H, dh)
    kg = k.reshape(rows, GRID_W, H, dh)
    vg = v.reshape(rows, GRID_W, H, dh)
    r = jnp.arange(rows)
    row_start = jnp.clip(r - kh // 2, 0, rows - kh)
    key_rows = row_start[:, None] + jnp.arange(kh)
    cb = jnp.arange(ncb)
    band_start = jnp.clip(cb * NA_QBLK - NA_KW // 2, 0, GRID_W - NA_BAND)
    key_cols = band_start[:, None] + jnp.arange(NA_BAND)
    ri = key_rows[:, None, :, None]
    ci = key_cols[None, :, None, :]
    k_blk = kg[ri, ci]
    v_blk = vg[ri, ci]
    qcol = cb[:, None] * NA_QBLK + jnp.arange(NA_QBLK)
    col_start = jnp.clip(qcol - NA_KW // 2, 0, GRID_W - NA_KW)
    kc = key_cols[:, None, :]
    in_win = (kc >= col_start[:, :, None]) & (kc < col_start[:, :, None] + NA_KW)
    dr = key_rows - r[:, None]
    dc = jnp.clip(kc - qcol[:, :, None] + NA_KW - 1, 0, 2 * NA_KW - 2)
    bias = rpb[:, (dr + NA_KH_MAX - 1)[:, None, None, :, None], dc[None, :, :, None, :]]
    scores = jnp.einsum('rcqhd,rckwhd->hrcqkw', qg, k_blk,
                        preferred_element_type=jnp.float32) * (1.0 / math.sqrt(dh))
    scores = jnp.where(in_win[None, None, :, :, None, :], scores + bias.astype(jnp.float32), NEG_INF)
    p = jax.nn.softmax(scores, axis=(-2, -1))
    out = jnp.einsum('hrcqkw,rckwhd->rcqhd', p.astype(v.dtype), v_blk)
    return out.reshape(S, H * dh)

def gqa_attention(q, k, v, q_gain, k_gain, cos, sin):
    q = apply_rope(rms_norm(q, q_gain), cos, sin)
    k = apply_rope(rms_norm(k, k_gain), cos, sin)
    B, S, Hq, dh = q.shape
    hkv = k.shape[2]
    grp = Hq // hkv
    nblk = S // GQA_QBLK
    qb = q.reshape(B, nblk, GQA_QBLK, hkv, grp, dh).transpose(1, 0, 3, 4, 2, 5)
    scale = 1.0 / math.sqrt(dh)

    def block(qi):
        s = jnp.einsum('bkgqd,bskd->bkgqs', qi, k, preferred_element_type=jnp.float32) * scale
        p = jax.nn.softmax(s, axis=-1)
        return jnp.einsum('bkgqs,bskd->bqkgd', p.astype(v.dtype), v)

    out = lax.map(block, qb)
    return out.transpose(1, 0, 2, 3, 4, 5).reshape(B, S, Hq * dh)

def memory_attention(q, mk, mv):
    B, S, H, dm = q.shape
    s = jnp.einsum('bshd,bmhd->bhsm', q, mk, preferred_element_type=jnp.float32) * (1.0 / math.sqrt(dm))
    p = jax.nn.softmax(s, axis=-1)
    return jnp.einsum('bhsm,bmhd->bshd', p.astype(mv.dtype), mv).reshape(B, S, H * dm)

def expert_choice_ffn(x, w_router, w_gate_up, w_down):
    B, T, D = x.shape
    cap = EC_CAPACITY_FACTOR * T // N_EXPERTS
    logits = jnp.einsum('btd,de->bte', x, w_router, preferred_element_type=jnp.float32)
    aff = jax.nn.softmax(logits, axis=-1)
    gate, idx = lax.top_k(jnp.swapaxes(aff, 1, 2), cap)
    bidx = jnp.arange(B)[:, None, None]
    xs = x[bidx, idx]
    h = jnp.einsum('becd,edf->becf', xs, w_gate_up)
    hg, hu = jnp.split(h, 2, axis=-1)
    ye = jnp.einsum('becf,efd->becd', jax.nn.silu(hg) * hu, w_down)
    ye = ye * gate[..., None].astype(ye.dtype)
    return jnp.zeros_like(x).at[bidx, idx].add(ye)

def second_inputs(seed: int = 0) -> dict:
    key = jax.random.key(seed)
    ks = jax.random.split(key, 20)

    def nrm(k, shape, scale):
        return jax.random.normal(k, shape, jnp.float32) * scale

    return {
        "x": nrm(ks[0], (BATCH, SEQ, D_MODEL), 1.0),
        "mem": nrm(ks[1], (BATCH, MEM_TOKENS, D_MODEL), 1.0),
        "w_in": nrm(ks[2], (DEPTH, D_MODEL, IN_W), D_MODEL ** -0.5),
        "b_gate": nrm(ks[3], (DEPTH, GATE_W), 0.1),
        "na_rpb": nrm(ks[4], (DEPTH, NA_HEADS, 2 * NA_KH_MAX - 1, 2 * NA_KW - 1), 0.05),
        "gqa_q_gain": 1.0 + nrm(ks[5], (DEPTH, HEAD_DIM), 0.1),
        "gqa_k_gain": 1.0 + nrm(ks[6], (DEPTH, HEAD_DIM), 0.1),
        "w_mem_kv": nrm(ks[7], (DEPTH, D_MODEL, 2 * MEM_W), D_MODEL ** -0.5),
        "w_branch": nrm(ks[8], (DEPTH, N_BRANCH, BRANCH_WIDTH, D_MODEL), BRANCH_WIDTH ** -0.5),
        "w_out": nrm(ks[9], (DEPTH, D_MODEL, D_MODEL), D_MODEL ** -0.5 * DN_BETA),
        "ln1_g": 1.0 + nrm(ks[10], (DEPTH, D_MODEL), 0.1),
        "ln1_b": nrm(ks[11], (DEPTH, D_MODEL), 0.02),
        "w_router": nrm(ks[12], (DEPTH, D_MODEL, N_EXPERTS), D_MODEL ** -0.5),
        "w_gate_up": nrm(ks[13], (DEPTH, N_EXPERTS, D_MODEL, 2 * D_FF_EXPERT), D_MODEL ** -0.5),
        "w_down": nrm(ks[14], (DEPTH, N_EXPERTS, D_FF_EXPERT, D_MODEL), D_FF_EXPERT ** -0.5 * DN_BETA),
        "ln2_g": 1.0 + nrm(ks[15], (DEPTH, D_MODEL), 0.1),
        "ln2_b": nrm(ks[16], (DEPTH, D_MODEL), 0.02),
    }

def second_block(x, mem, w_in, b_gate, na_rpb, gqa_q_gain, gqa_k_gain, w_mem_kv, w_branch, w_out,
              ln1_g, ln1_b, w_router, w_gate_up, w_down, ln2_g, ln2_b):
    B, S, D = x.shape
    M = mem.shape[1]
    cos, sin = axial_rope_tables(S)
    for l in range(DEPTH):
        z = jnp.einsum('bsd,df->bsf', x, w_in[l])
        q_na, k_na, v_na, q_g, k_g, v_g, q_m, gate_logits = jnp.split(z, _split_points(), axis=-1)
        rpb = na_rpb[l]
        y_na = lax.map(lambda qkv: neighbourhood_attention(qkv[0], qkv[1], qkv[2], rpb),
                       (q_na.reshape(B, S, NA_HEADS, HEAD_DIM),
                        k_na.reshape(B, S, NA_HEADS, HEAD_DIM),
                        v_na.reshape(B, S, NA_HEADS, HEAD_DIM)))
        y_gqa = gqa_attention(q_g.reshape(B, S, GQA_HEADS, HEAD_DIM),
                              k_g.reshape(B, S, GQA_KV_HEADS, HEAD_DIM),
                              v_g.reshape(B, S, GQA_KV_HEADS, HEAD_DIM),
                              gqa_q_gain[l], gqa_k_gain[l], cos, sin)
        mkv = jnp.einsum('bmd,df->bmf', mem, w_mem_kv[l])
        mk, mv = jnp.split(mkv, 2, axis=-1)
        y_mem = memory_attention(q_m.reshape(B, S, MEM_HEADS, MEM_HEAD_DIM),
                                 mk.reshape(B, M, MEM_HEADS, MEM_HEAD_DIM),
                                 mv.reshape(B, M, MEM_HEADS, MEM_HEAD_DIM))
        branches = jnp.stack([y_na, y_gqa, y_mem], axis=2)
        proj = jnp.einsum('bsgk,gkd->bsgd', branches, w_branch[l])
        gates = jax.nn.sigmoid(gate_logits + b_gate[l]).reshape(B, S, N_BRANCH, D)
        merged = jnp.sum(gates * proj, axis=2)
        mix = jnp.einsum('bsd,de->bse', merged, w_out[l])
        x = layer_norm(DN_ALPHA * x + mix, ln1_g[l], ln1_b[l])
        ffn = expert_choice_ffn(x, w_router[l], w_gate_up[l], w_down[l])
        x = layer_norm(DN_ALPHA * x + ffn, ln2_g[l], ln2_b[l])
    return x


def setup_inputs(seed=0):
    out = dict(first_inputs(seed))
    for name, value in second_inputs(seed + 1).items():
        if name != "x":
            out[name + "_2"] = value
    return out


def reference(
    x, norm_mix_pre, norm_mix_post, norm_mlp_pre, norm_mlp_post, w_in, conv_a, a_log, dt_bias,
    norm_a, norm_b, w_br_a, w_br_b, w_out, w_up, w_down, mem_2, w_in_2, b_gate_2, na_rpb_2,
    gqa_q_gain_2, gqa_k_gain_2, w_mem_kv_2, w_branch_2, w_out_2, ln1_g_2, ln1_b_2, w_router_2,
    w_gate_up_2, w_down_2, ln2_g_2, ln2_b_2,
):
    x = first_block(
        x, norm_mix_pre, norm_mix_post, norm_mlp_pre, norm_mlp_post, w_in, conv_a, a_log,
        dt_bias, norm_a, norm_b, w_br_a, w_br_b, w_out, w_up, w_down,
    )
    return second_block(
        x, mem_2, w_in_2, b_gate_2, na_rpb_2, gqa_q_gain_2, gqa_k_gain_2, w_mem_kv_2,
        w_branch_2, w_out_2, ln1_g_2, ln1_b_2, w_router_2, w_gate_up_2, w_down_2, ln2_g_2,
        ln2_b_2,
    )


_drawn_inputs = setup_inputs


def setup_inputs(seed=0):
    import zlib

    import numpy as np

    out = dict(_drawn_inputs(seed))
    spreads = {}
    factors = {'b_gate_2': 8.0,
     'na_rpb_2': 8.0,
     'gqa_q_gain_2': 8.0,
     'gqa_k_gain_2': 8.0,
     'ln2_b_2': 2.75}
    for name, (base, spread) in spreads.items():
        noise = np.random.default_rng([zlib.crc32(name.encode()), seed]).standard_normal(out[name].shape)
        drawn = base * np.exp(spread * noise) if base else spread * noise
        out[name] = __import__('jax').numpy.asarray(drawn.astype(out[name].dtype))
    for name, factor in factors.items():
        out[name] = (out[name] * factor).astype(out[name].dtype)
    return out
```

```python
import concourse.bass as bass
from concourse import mybir
from contextlib import ExitStack
import numpy as np

F32, F32R = mybir.dt.float32, mybir.dt.float32r
ALU = mybir.AluOpType
ACT = mybir.ActivationFunctionType
AX = mybir.AxisListType.X

SEQ, DM, P = 512, 1024, 128
NT = SEQ // P
KB = DM // P
EPS = 1e-6
A_HEADS, A_DK, A_DV = 8, 128, 256
B_HEADS, B_DK, B_DV = 4, 256, 512
A_QK, A_V, B_QK, B_V = 1024, 2048, 1024, 2048
C_QA, C_KA, C_VA, C_ZA = 0, 1024, 2048, 4096
C_BETA = 6144
C_QB = 6160
C_KB, C_VB, C_GB = C_QB + 1024, C_QB + 2048, C_QB + 4096
C_GA = C_GB + 2048
C_GBT = C_GA + 1024
ALPHA = 2 ** 0.25
NE, EC = 16, 64
LEVELS = 7
PAIRS = A_HEADS // 2
TURNS = (("ring", 4 * 4096), ("activations_T", 4096), ("work", 26500))
A_EARLY = 16

V_MIXPRE, V_MLPPRE, V_CONV, V_NA, V_NB, V_BG, V_ALOG, V_DT = 0, 8, 16, 144, 146, 162, 186, 187
V_HALF, V_N = 188, 190


class Sig:

    known = {}

    def __init__(self, nc, ctx, name, step=1):
        self.sem, self.name, self.step = ctx.enter_context(nc.semaphore(name)), name, step
        self.seen, self.was, self.k = {}, Sig.known.get(name, {}), 0

    def start(self):
        self.k = 0

    def mark(self, ins, what):
        self.k += 1
        assert self.seen.setdefault(what, self.k) == self.k, (self.name, what)
        Sig.known[self.name] = self.seen
        ins.then_inc(self.sem, self.step)

    def __call__(self, what, i=0):
        per = len(self.was) or 1
        if self.was and what not in self.was:
            raise KeyError((self.name, what))
        return self.sem, (i * per + self.was.get(what, 1)) * self.step

    def link(self, eng, ins, i=0):
        what = f"link{self.k}"
        self.mark(ins, what)
        eng.wait_ge(*self(what, i))


TWINS = {}


def R(x):
    return bass.AP(tensor=TWINS[x.tensor.name], offset=x.offset, ap=[list(a) for a in x.ap])


def high(act, s, dst, src, what):
    s.mark(act.activation(R(dst), src, ACT.Copy), what)


def low(dve, s, dst, src, hi, what):
    s.mark(dve.tensor_tensor(R(dst), src, R(hi).bitcast(F32), ALU.subtract), what)


def product(pe, out, lhs, rhs, start, stop):
    (lh, ll), (rh, rl) = lhs, rhs
    pe.matmul(out, R(ll), R(rh), start=start, stop=False)
    pe.matmul(out, R(lh), R(rh), start=False, stop=False)
    return pe.matmul(out, R(lh), R(rl), start=False, stop=stop)


def build(nc, T, out):
    with ExitStack() as ctx:
        def sb(name, words):
            return ctx.enter_context(nc.sbuf_tensor(name, [P, words], F32))

        def sig(name, step=1):
            return Sig(nc, ctx, name, step)

        xr_t = sb("residual", 4096)
        const = sb("const", 2048)
        with ExitStack() as over:
            plain = [over.enter_context(nc.sbuf_tensor(n, [P, w], F32)) for n, w in TURNS]
        for n, w in TURNS:
            TWINS[n] = ctx.enter_context(nc.sbuf_tensor(n + "_split", [P, w], F32R))
        ring_t, at_t, work = plain
        ps_all = ctx.enter_context(nc.psum_tensor("banks", [P, 8, 512], F32))
        psum = [ps_all[:, b, :] for b in range(8)]

        ring = [ring_t[:, s * 4096:(s + 1) * 4096].rearrange("p (k n) -> p k n", k=8) for s in range(4)]
        hq = [ring_t[:, 3 * 4096 + n * 1024:3 * 4096 + (n + 1) * 1024] for n in range(4)]
        h_col = [h.rearrange("p (k n) -> p k n", k=8) for h in hq]
        h_row = [h.rearrange("p (k n) -> p k n", k=2) for h in hq]
        XR = xr_t[:, :].rearrange("p (t d) -> p t d", t=NT)
        AT = at_t[:, :].rearrange("p (k n) -> p k n", k=KB)

        def carve(t, start, shapes):
            got, at = [], start
            for s in shapes:
                n = int(np.prod(s))
                v = t[:, at:at + n]
                if len(s) == 2:
                    v = v.rearrange("p (a b) -> p a b", a=s[0])
                if len(s) == 3:
                    v = v.rearrange("p (a b c) -> p a b c", a=s[0], b=s[1])
                got.append(v)
                at += n
            return got, at

        (ident, ones, m_incl, m_lvl, cols, stat, eps, one), at_c = carve(
            const, 0, [(P,), (P,), (P,), (LEVELS, P), (192,), (16,), (1,), (1,)])

        (at_hi,), _ = carve(work, 0, [(KB, 512)])
        a, at_w = carve(work, 8192, [(512,), (NT, P), (NT, 8), (8, 516), (NT, 512), (2, 3, 512), (512,), (512,),
                                     (512,), (512,), (1024,), (NT, P)])
        ST, stN, begN, pre, zs, bc, kT, qT, kbT, qeT, dl, ATT = a
        o_st = work[:, at_w:at_w + 1024].rearrange("p (d n) -> p d n", d=2)
        a, at_w = carve(work, at_w, [(NT, P), (NT, P), (NT, P), (1024,), (NT, A_DV), (A_DV,), (A_DV,)])
        X, PP, Y, kk, vb, S, vnew = a
        assert at_w <= 26500, at_w
        (zraw, NM, nwT, wsm), at_z = carve(work, 4096, [(NT, 512), (2, 512), (512,), (KB, 40)])
        assert at_z <= 8192
        D = dl[:, 0:512].rearrange("p (t c) -> p t c", t=NT)
        LT = dl[:, 512:1024].rearrange("p (t c) -> p t c", t=NT)
        oN = dl.rearrange("p (t c) -> p t c", t=NT)
        kbeg = kk[:, 0:512].rearrange("p (t c) -> p t c", t=NT)
        kdN = kk[:, 512:1024].rearrange("p (t c) -> p t c", t=NT)
        sq = kk.rearrange("p (a c) -> p a c", a=2)
        oj = kk.rearrange("p (t c) -> p t c", t=NT)
        rinv = vb.rearrange("p t d -> p (t d)").rearrange("p (a c) -> p a c", a=2)
        u8 = work[:, 4096 + 2048:4096 + 2048 + 1536].rearrange("p (a n) -> p a n", a=3)
        y = xr_t[:, :].rearrange("p (b n) -> p b n", b=8)

        (mixT, qkr, qkT, bv, bg, PT, bo, cosT, sinT, dmask, rk, rt), at_b = carve(work, 4096, [
            (KB, 512), (4, 512), (4, 512), (NT, 512), (NT, 512), (NT, 512), (NT, 512), (512,), (512,),
            (B_HEADS, 512), (2, 512), (2, 512)])
        (oT, oT_hi, ytmp), at_o = carve(work, 8192, [(16, 512), (16, 512), (2, 512)])
        assert max(at_b, at_o) <= 26500
        ob_st = xr_t[:, 0:2048].rearrange("p (d n) -> p d n", d=4)
        sg = xr_t[:, 2048:4096].rearrange("p (b n) -> p b n", b=4)
        oT_rows = [nc.dram_tensor(f"o_{x}", (16, P, SEQ), F32).ap() for x in "ab"]
        (pt_tmp, hN), _ = carve(work, 0, [(NT, DM), (NT, DM)])
        (o_tmp, o_hN), _ = carve(work, 12288, [(NT, DM), (NT, DM)])
        (ffT, row), at_m = carve(work, 8192, [(32, 512), (DM,)])
        (mix_hi,), _ = carve(work, 8192, [(KB, 512)])
        (ff_hi, ff_lo), _ = carve(work, 0, [(4, 2, 512), (4, 2, 512)])
        (yT, area, qmT, mkT, mvN, bias, bmask, qz, vst), at_2 = carve(work, 0, [
            (12, 512), (11392,), (4, 512), (4, 256), (2, 512), (2, 3, 256), (3, 256), (2, 512), (8, P)])
        assert at_2 <= 26500, at_2
        A0 = 12 * 512
        (memN, memT), _ = carve(work, A0, [(2, DM), (KB, 256)])
        (qnT, knT, vnN, vband), _ = carve(work, A0, [(4, 512), (4, 512), (NT, 512), (8, 512)])
        (qkN, ro, kdup, ra, rb, qgT, kgT), at_g = carve(work, A0, [
            (NT, 768), (NT, 640), (NT, 2, P), (320,), (320,), (4, 512), (4, 512)])
        (mgT, v2, sg2, mtmp), at_g2 = carve(work, A0, [(KB, 512), (NT, DM), (4, 512), (2, 512)])
        assert max(at_g, at_g2) <= A0 + 11392
        vdup = bias.rearrange("p e v n -> p (e v n)")[:, 0:1024].rearrange("p (t n) -> p t n", t=NT)
        qst = qz[:, 0, :]
        (lnrow,), _ = carve(work, A0 + 11392, [(2, DM)])
        (sc, pr, pT, gain), _ = carve(ring_t, 3 * 4096, [(2, 512), (3, 512), (2, 512), (2, 64)])
        (cosN, sinN, nmax, psums, pinv, gst, eps5), at_c = carve(const, at_c, [
            (NT, 32), (NT, 32), (8,), (8,), (8,), (NT, 10), (1,)])
        assert at_c <= 2048
        (slot4, SP, SG, SGT, xst, ga, actT, ye, acc, affT, wrk, cum, iota, posN, affN, wr, m8, lmax, lsum), at_e = carve(work, 0, [
            (KB, 512), (NT, P), (NT, P), (512,), (KB, P), (2, 512), (KB, P), (2, 512), (NT, DM),
            (512,), (512,), (512,), (EC,), (NT, NE), (NT, NE), (KB, NE), (8,), (NT,), (NT,)])
        assert at_e <= A0 + 11392 and 8 * 512 + 6144 == A0 + 4096
        (slot5,), _ = carve(work, A0 + 11392 + 2 * DM, [(KB, 512)])
        eslot = ring + [slot4, slot5]
        v_rows = nc.dram_tensor("v_rows", (SEQ, 512), F32).ap()

        scratch = nc.dram_tensor("stat_rows", (P, SEQ), F32).ap()
        W = T["w_in"].rearrange("(k p) n -> p k n", p=P)

        ld_const, ld_small = sig("loaded_const", 16), sig("loaded_small", 16)
        ld_x = sig("loaded_x", 16)
        z_pool = sig("pool_setup")
        n_act, n_vec, n_pe = sig("norm_act"), sig("norm_vec"), sig("norm_pe")
        s_pe, s_act, s_vec, s_dma = sig("stats_pe"), sig("stats_act"), sig("stats_vec"), sig("stats_stored", 16)
        a_w = [sig(f"a_weights{s}", 16) for s in range(3)]
        a_bc = [sig(f"a_rows{j}", 16) for j in range(2)]
        g_pe, g_act = sig("a_gemm_pe"), sig("a_gemm_act")
        c_pe, c_act, c_vec, c_pool = sig("a_chain_pe"), sig("a_chain_act"), sig("a_chain_vec"), sig("a_chain_pool")
        ga_vec, bs_vec = sig("a_split_vec"), sig("b_split_vec")
        oa_st, ob_st_s = [sig(f"a_stored{j}", 16) for j in range(2)], sig("b_stored", 16)
        ot_ld, ot_act, ot_vec = [[sig(f"merge{x}_o_{e}", n) for x in "ab"] for e, n in (("loaded", 16), ("act", 1), ("vec", 1))]
        b_rope = sig("b_rope_vec")
        done = sig("done", 16)
        m_w = [[sig(f"merge{x}_weights{q}", 16) for q in range(3)] for x in "ab"]
        m_pe, m_act, m_vec = [[sig(f"merge{x}_{e}") for x in "ab"] for e in ("pe", "act", "vec")]
        t2_pe, t2_vec = sig("x2_turn_pe"), sig("x2_turn_vec")
        mem_ld, n2_tab, bias_ld = sig("memory_loaded", 16), sig("attn_tables", 16), sig("bias_loaded", 16)
        w2 = [sig(f"proj_weights{q}", 16) for q in range(3)]
        p_pe, p_act, p_vec = sig("proj_pe"), sig("proj_act"), sig("proj_vec")
        v_st, v_ld = sig("v_stored", 16), sig("v_bands", 16)
        at_pe, at_act, at_vec, at_pool = [{k: sig(f"attn{k}_{e}") for k in "nmg"} for e in ("pe", "act", "vec", "pool")]
        r_pe, r_act, r_vec, r_pool = sig("rope_pe"), sig("rope_act"), sig("rope_vec"), sig("rope_pool")
        mg_w = [sig(f"merge2_weights{q}", 16) for q in range(4)]
        mg_pe, mg_act, mg_vec = sig("merge2_pe"), sig("merge2_act"), sig("merge2_vec")
        l_w, l_row = [sig(f"out2_weights{q}", 16) for q in range(2)], sig("ln1_rows", 16)
        l_pe, l_act, l_vec, l_pool = sig("ln1_pe"), sig("ln1_act"), sig("ln1_vec"), sig("ln1_pool")
        q_ld, q_pe, q_act, q_vec = sig("route_loaded", 16), sig("route_pe"), sig("route_act"), sig("route_vec")
        e_w = [sig(f"expert_weights{q}", 16) for q in range(6)]
        e_pe, e_act, e_vec = sig("expert_pe"), sig("expert_act"), sig("expert_vec")
        f_rowl, f_act, f_vec, f_pool = sig("ln2_rows", 16), sig("ln2_act"), sig("ln2_vec"), sig("ln2_pool")
        b_w = [sig(f"b_weights{q}", 16) for q in range(3)]
        b_tab = sig("b_tables", 16)
        bg_pe, bg_act = sig("b_gemm_pe"), sig("b_gemm_act")
        b_pe, b_act, b_vec, b_pool = sig("b_attn_pe"), sig("b_attn_act"), sig("b_attn_vec"), sig("b_attn_pool")
        x_back, o_row, f_row = sig("x_again", 16), sig("mix_row", 16), sig("ff_row", 16)
        o_w = [sig(f"out_weights{q}", 16) for q in range(2)]
        o_pe, o_act, o_vec = sig("out_pe"), sig("out_act"), sig("out_vec")
        u_w = [sig(f"up_weights{q}", 16) for q in range(4)]
        u_pe, u_act, u_vec = sig("up_pe"), sig("up_act"), sig("up_vec")
        d_w = [sig(f"down_weights{q}", 16) for q in range(4)]
        dn_act, dn_vec = sig("down_split_act"), sig("down_split_vec")
        d_pe, d_act, d_vec = sig("down_pe"), sig("down_act"), sig("down_vec")

        def only(i):
            return isinstance(i, int) and i == 0

        block = ctx.enter_context(nc.Block())

        @block.sync
        def _(sp):
            ld_x.mark(sp.dma_start(XR, T["x"].rearrange("(t p) d -> p t d", p=P)), "x")
            ld_const.mark(sp.dma_start(const[:, 0:T["consts"].shape[1]], T["consts"]), "consts")
            ld_const.mark(sp.dma_start(cols[:, 0:V_N], T["cols"]), "cols")
            sp.wait_ge(*z_pool("wsm"))
            ld_small.mark(sp.dma_start(wsm[:, :, 0:8], W[:, :, C_BETA + 8:C_BETA + 16]), "steps")
            ld_small.mark(sp.dma_start(wsm[:, :, 32:40], W[:, :, C_BETA:C_BETA + 8]), "w")

            def load_a(p):
                last = not (only(p) and p == 0)
                if last:
                    sp.wait_ge(*g_pe("g3", p - 1))
                a_w[0].start()
                a_w[0].mark(sp.dma_start(ring[0][:, :, 0:256], W[:, :, bass.ds(p * 256 + C_QA, 256)]), "q")
                a_w[0].mark(sp.dma_start(ring[0][:, :, 256:512], W[:, :, bass.ds(p * 256 + C_KA, 256)]), "k")
                if last:
                    sp.wait_ge(*g_pe("g7", p - 1))
                a_w[1].start()
                a_w[1].mark(sp.dma_start(ring[1], W[:, :, bass.ds(p * 512 + C_VA, 512)]), "v")
                if last:
                    sp.wait_ge(*g_pe("g11", p - 1))
                a_w[2].start()
                a_w[2].mark(sp.dma_start(ring[2], W[:, :, bass.ds(p * 512 + C_ZA, 512)]), "z")

            load_a(0)
            sp.wait_ge(*s_act("eg"))
            sp.wait_ge(*s_vec("gcum"))
            s_dma.mark(sp.dma_start(scratch, ST), "rows")
            with sp.Fori(1, PAIRS) as p:
                load_a(p)

            def load_merge(x, c, before=None):
                col, wb = (C_GA, T["w_br_a"]) if x == 0 else (C_GBT, T["w_br_b"])
                wb = wb.rearrange("(a k p) n -> a p k n", p=P, a=2)
                srcs = (W[:, :, bass.ds(c * 512 + col, 512)], wb[0][:, :, bass.ds(c * 512, 512)], wb[1][:, :, bass.ds(c * 512, 512)])
                for q in range(3):
                    sp.wait_ge(*(before[q] if before else m_pe[x](("gate3", "lo3", "y3")[q], c - 1)))
                    m_w[x][q].start()
                    m_w[x][q].mark(sp.dma_start(ring[q], srcs[q]), "w")

            load_merge(0, 0, [g_pe(f"g{g}", PAIRS - 1) for g in (3, 7, 11)])

            def load_o(x):
                ot_ld[x].mark(sp.dma_start(oT, oT_rows[x].rearrange("k p n -> p k n")), "o")
            sp.wait_ge(*c_vec("oT11", PAIRS - 1))
            sp.wait_ge(*c_act("wT1", PAIRS - 1))
            for j in range(2):
                sp.wait_ge(*oa_st[j]("o", PAIRS - 1))
            load_o(0)
            with sp.Fori(1, 2) as c:
                load_merge(0, c)

            def load_b(h, before=None):
                for q in range(3):
                    sp.wait_ge(*(before[q] if before else bg_pe(f"g{4 * q + 3}", h - 1)))
                    b_w[q].start()
                    if q == 0:
                        b_w[0].mark(sp.dma_start(ring[0][:, :, 0:256], W[:, :, bass.ds(h * 256 + C_QB, 256)]), "q")
                        b_w[0].mark(sp.dma_start(ring[0][:, :, 256:512], W[:, :, bass.ds(h * 256 + C_KB, 256)]), "k")
                    else:
                        b_w[q].mark(sp.dma_start(ring[q], W[:, :, bass.ds(h * 512 + (C_VB if q == 1 else C_GB), 512)]), "k")

            load_b(0, [m_pe[0](n, 1) for n in ("gate3", "lo3", "y3")])
            sp.wait_ge(*m_vec[0]("mix3", 1))
            b_tab.mark(sp.dma_start(work[:, 8192 + 6 * 2048:8192 + 6 * 2048 + 1024], T["rope_b"]), "rope")
            b_tab.mark(sp.dma_start(dmask, T["decay_b"].rearrange("p (h c) -> p h c", h=B_HEADS)), "decay")
            with sp.Fori(1, B_HEADS) as h:
                load_b(h)
            load_merge(1, 0, [bg_pe(f"g{g}", B_HEADS - 1) for g in (3, 7, 11)])
            sp.wait_ge(*b_vec("oT3", B_HEADS - 1))
            sp.wait_ge(*ob_st_s("o", B_HEADS - 1))
            load_o(1)
            with sp.Fori(1, 2) as c:
                load_merge(1, c)

            WO = T["w_out"].rearrange("(k p) n -> p k n", p=P)
            for q in range(2):
                sp.wait_ge(*m_pe[1](("gate3", "lo3")[q], 1))
                o_w[q].mark(sp.dma_start(ring[q], WO[:, :, q * 512:(q + 1) * 512]), "w")
            sp.wait_ge(*m_vec[1]("mix3", 1))
            x_back.mark(sp.dma_start(XR, T["x"].rearrange("(t p) d -> p t d", p=P)), "x")
            o_row.mark(sp.dma_start(row, T["norm_mix_post"].broadcast_to([P, DM])), "row")
            WU = T["w_up"].rearrange("(k p) n -> p k n", p=P)
            WD = T["w_down"].rearrange("(a k p) n -> a p k n", p=P, a=4)

            def load_up(i, before=None):
                for q in range(4):
                    sp.wait_ge(*(u_pe(f"g{4 * q - 5}", i) if q >= 2 else before[q] if before else u_pe(f"g{4 * q + 11}", i - 1)))
                    u_w[q].start()
                    u_w[q].mark(sp.dma_start(ring[q % 2], WU[:, :, bass.ds(i * 2048 + q * 512, 512)]), "w")
            load_up(0, [o_pe("m31"), o_pe("m31")])
            with sp.Fori(1, 2) as i:
                load_up(i)

            def load_down(c, before=None):
                for q in range(4):
                    sp.wait_ge(*(d_pe(f"p{4 * q - 5}", c) if q >= 2 else before[q] if before else d_pe(("p11", "m3")[q], c - 1)))
                    d_w[q].start()
                    d_w[q].mark(sp.dma_start(ring[q % 2], WD[q][:, :, bass.ds(c * 512, 512)]), "w")
            load_down(0, [u_pe(f"g{4 * q + 11}", 1) for q in range(2)])
            with sp.Fori(1, 2) as c:
                load_down(c)
            sp.wait_ge(*o_vec("x3"))
            f_row.mark(sp.dma_start(row, T["norm_mlp_post"].broadcast_to([P, DM])), "row")
            sp.wait_ge(*d_vec("x3"))
            mem_ld.mark(sp.dma_start(memN, T["mem_2"].rearrange("(t p) d -> p t d", p=P)), "mem")
            n2_tab.mark(sp.dma_start(const[:, 1490:1490 + 256], T["rope_g"]), "rope")
            n2_tab.mark(sp.dma_start(bmask, T["na_mask"].rearrange("p (v n) -> p v n", v=3)), "mask")
            n2_tab.mark(sp.dma_start(gain, T["gains"].rearrange("o (a n) -> o a n", a=2).broadcast_to([P, 2, 64])), "gain")
            W2 = T["w_in_2"].rearrange("(k p) n -> p k n", p=P)
            WM = T["w_mem_kv_2"].rearrange("(k p) n -> p k n", p=P)
            order = [(WM, 0, 512), (WM, 512, 512), (W2, 1536 + 768, 512), (W2, 0, 512), (W2, 512, 512), (W2, 1024, 512),
                     (W2, 1536, 512), (W2, 2048, 256)]
            last_group = [3, 5, 9, 13, 17, 21, 25, 29]
            for n, (src, col, width) in enumerate(order):
                q = n % 3
                sp.wait_ge(*(d_pe(("p11", "m3", "m3")[q], 1) if n < 3 else p_pe(f"g{last_group[n - 3]}")))
                w2[q].mark(sp.dma_start(ring[q][:, :, 0:width], src[:, :, col:col + width]), f"w{n}")
                if n == 6:
                    sp.wait_ge(*p_act("e21"))
                    v_st.mark(sp.dma_start(v_rows.rearrange("(t p) d -> p t d", p=P), vnN), "v")
                    sp.wait_ge(*v_st("v"))
                    for cb, start in enumerate((0, 8, 24, 32)):
                        for half in range(2):
                            rows = v_rows.rearrange("(r c) d -> r c d", c=64)[4 * half:4 * half + 4, start:start + 32, :]
                            v_ld.mark(sp.dma_start(vband[:, cb * 2 + half, :], rows), f"v{cb}{half}")

                    def load_bias(b):
                        if not only(b):
                            sp.wait_ge(*at_vec["n"]("s7", b - 1))
                        bias_ld.start()
                        bias_ld.mark(sp.dma_start(bias, T["na_bias"][bass.ds(b, 1), :, :].rearrange("a p (e v n) -> (a p) e v n", e=2, v=3)), "bias")
                    load_bias(0)
                    with sp.Fori(1, 4) as b:
                        load_bias(b)

            WB2 = T["w_branch_2"].rearrange("(g k p) n -> g p k n", p=P, k=4)

            def load_merge2(c, first=False):
                for q in range(4):
                    mg_w[q].start()
                for g in range(3):
                    q = g % 2
                    sp.wait_ge(*((p_pe("g25"), p_pe("g29"), mg_pe("gate03", 0))[g] if first
                                 else mg_pe(("gate23", "gate13")[g], c - 1) if g < 2 else mg_pe("gate03", c)))
                    mg_w[q].mark(sp.dma_start(ring[q], W2[:, :, bass.ds(c * 512 + 2816 + g * DM, 512)]), f"w{g}")
                    sp.wait_ge(*((p_pe("g21"), at_pe["g"]("AV7", 3), mg_pe("br03", 0))[g] if first
                                 else mg_pe(("br23", "br13")[g], c - 1) if g < 2 else mg_pe("br03", c)))
                    if first and g == 1:
                        sp.wait_ge(*at_vec["g"]("n7", 3))
                        sp.wait_ge(*r_pool("dup"))
                    mg_w[2 + q].mark(sp.dma_start(ring[2 + q][:, 0:4, :], WB2[g][:, :, bass.ds(c * 512, 512)]), f"w{g}")
            load_merge2(0, True)
            with sp.Fori(1, 2) as c:
                load_merge2(c)
            WO2 = T["w_out_2"].rearrange("(k p) n -> p k n", p=P)
            for q in range(2):
                sp.wait_ge(*mg_pe(("gate23", "gate13")[q], 1))
                l_w[q].mark(sp.dma_start(ring[q], WO2[:, :, q * 512:(q + 1) * 512]), "w")
            sp.wait_ge(*at_pe["g"]("AV7", 3))
            for n, name in enumerate(("ln1_g_2", "ln1_b_2")):
                l_row.mark(sp.dma_start(lnrow[:, n, :], T[name].broadcast_to([P, DM])), name)
            sp.wait_ge(*l_vec("n3"))
            q_ld.mark(sp.dma_start(iota, T["iota"]), "iota")
            q_ld.mark(sp.dma_start(wr, T["w_router_2"].rearrange("(k p) e -> p k e", p=P)), "wr")
            WGU = T["w_gate_up_2"].rearrange("e (k p) n -> e p k n", p=P)
            WDN = T["w_down_2"].rearrange("e (k p) n -> e p k n", p=P)

            def load_experts(p):
                for q in range(6):
                    e_w[q].start()
                for n in range(12):
                    q, e = n // 2, n % 2
                    if q >= 3:
                        sp.wait_ge(*e_pe(f"group{q - 3}", p))
                    elif not only(p):
                        sp.wait_ge(*e_pe(f"group{q + 3}", p - 1))
                    else:
                        sp.wait_ge(*(l_pe("m31") if q == 0 else mg_pe("br23", 1)))
                    src, col = (WGU, q // 2 * 512 + q % 2 * DM) if q < 4 else (WDN, (q - 4) * 512)
                    e_w[n % 6].mark(sp.dma_start(eslot[n % 6], src[bass.ds(p * 2 + e, 1), :, :, col:col + 512].rearrange("a p k n -> (a p) k n")), f"w{n // 6}")
            load_experts(0)
            sp.wait_ge(*l_pool("x3"))
            for n, name in enumerate(("ln2_g_2", "ln2_b_2")):
                f_rowl.mark(sp.dma_start(lnrow[:, n, :], T[name].broadcast_to([P, DM])), name)
            with sp.Fori(1, NE // 2) as p:
                load_experts(p)
            for t in range(NT):
                sp.wait_ge(*f_pool(f"x{t}"))
                done.mark(sp.dma_start(out[t * P:(t + 1) * P, :], XR[:, t, :]), f"out{t}")
            sp.wait_ge(*done("out3"))

        @block.gpsimd
        def _(pool):
            z_pool.mark(pool.memset(eps, EPS), "eps")
            z_pool.mark(pool.memset(one, 1.0), "one")
            z_pool.mark(pool.memset(eps5, 1e-5), "eps5")
            z_pool.mark(pool.memset(wsm, 0.0), "wsm")
            z_pool.mark(pool.memset(ST, 0.0), "ST")
            z_pool.mark(pool.memset(pre[:, :, 0:4], 0.0), "pads")
            pool.wait_ge(*s_dma("rows"))

            def rows(p, j):
                h = p * 2 + j
                if not only(p):
                    pool.wait_ge(*c_vec(f"S{NT - 2}_{j}", p - 1))
                    pool.wait_ge(*c_vec(f"Dpre{j}", p - 1))
                    pool.wait_ge(*c_pool(f"qeT{j}", p - 1))
                a_bc[j].start()
                for n, r in enumerate((0, 32, 96)):
                    a_bc[j].mark(pool.dma_start(bc[:, j, n, :], scratch[bass.ds(h + r, 1), :].broadcast_to([P, SEQ])), f"r{n}")

            def store_a(p, j):
                pool.wait_ge(*c_vec(f"oT1{j}", p))
                oa_st[j].start()
                oa_st[j].mark(pool.dma_start(oT_rows[0][bass.ds((p * 2 + j) * 2, 2), :, :].rearrange("d p n -> p d n"), o_st), "o")

            def chain_a(p):
                c_pool.start()
                for j in range(2):
                    rows(p, j)
                for j in range(2):
                    before = (lambda what: c_vec(what + "0", p)) if j else (lambda what: c_vec(what + "1", p - 1))
                    pbefore = (lambda what: c_pe(what + "0", p)) if j else (lambda what: c_pe(what + "1", p - 1))
                    first = only(p) and j == 0
                    if not first:
                        store_a(*((p, 0) if j else (p - 1, 1)))
                    pool.wait_ge(*a_bc[j]("r2", p))
                    pool.wait_ge(*c_vec(f"kT{j}", p))
                    if not first:
                        pool.wait_ge(*pbefore("KK"))
                    c_pool.mark(pool.tensor_tensor(kbT, kT, bc[:, j, 1, :], ALU.mult), f"kbT{j}")
                    pool.wait_ge(*c_vec(f"qT{j}", p))
                    if not first:
                        pool.wait_ge(*pbefore("O3"))
                    c_pool.mark(pool.tensor_tensor(qeT, qT, bc[:, j, 2, :], ALU.mult), f"qeT{j}")
                    pool.wait_ge(*c_act(f"D{j}", p))
                    c_pool.mark(pool.tensor_tensor(D, D, m_incl.unsqueeze(1).broadcast_to([P, NT, P]), ALU.mult), f"D{j}")
                    pool.wait_ge(*c_vec(f"LT{j}", p))
                    for s in range(LEVELS):
                        if s >= 2:
                            pool.wait_ge(*c_pe(f"P{s - 2}_{j}", p))
                        elif not first:
                            pool.wait_ge(*pbefore(f"P{LEVELS - 2 + s}_" if LEVELS % 2 == 0 else f"P{LEVELS - 1 if s == 0 else LEVELS - 2}_"))
                        if s == 2:
                            pool.wait_ge(*c_vec(f"Y0_{j}", p))
                        c_pool.mark(pool.tensor_tensor(
                            NM[:, s % 2, :].rearrange("p (t c) -> p t c", t=NT), LT,
                            m_lvl[:, s, :].unsqueeze(1).broadcast_to([P, NT, P]), ALU.mult), f"NM{s}_{j}")

            chain_a(0)
            with pool.Fori(1, PAIRS) as p:
                chain_a(p)
            store_a(PAIRS - 1, 1)

            def rope_k(h):
                b_pool.start()
                if only(h) and h == 0:
                    pool.wait_ge(*b_tab("decay"))
                else:
                    pool.wait_ge(*b_pe("S3", h - 1))
                pool.wait_ge(*bg_act("e3", h))
                for o, (c0, c1, op) in enumerate(((cosT, sinT, ALU.subtract), (sinT, cosT, ALU.add))):
                    pool.tensor_tensor(rk[:, 0, :], qkr[:, 2, :], c0, ALU.mult)
                    b_pool.link(pool, pool.tensor_tensor(rk[:, 1, :], qkr[:, 3, :], c1, ALU.mult), h)
                    i = pool.tensor_tensor(qkT[:, 2 + o, :], rk[:, 0, :], rk[:, 1, :], op)
                    if o == 0:
                        b_pool.link(pool, i, h)
                b_pool.mark(i, "ropek")
            def store_b(h):
                pool.wait_ge(*b_vec("oT3", h))
                ob_st_s.start()
                ob_st_s.mark(pool.dma_start(oT_rows[1][bass.ds(h * 4, 4), :, :].rearrange("d p n -> p d n"), ob_st), "o")
            rope_k(0)
            with pool.Fori(1, B_HEADS) as h:
                rope_k(h)
                store_b(h - 1)
            store_b(B_HEADS - 1)

            pool.wait_ge(*d_vec("x3"))

            def stage(kind, b):
                S = at_pool[kind]
                S.start()
                flat = lambda x: x.rearrange("p a n -> p (a n)")
                if not only(b):
                    pool.wait_ge(*at_pe[kind]("AV7" if kind != "m" else "AV3", b - 1))
                elif kind == "m":
                    pool.wait_ge(*at_pe["n"]("AV7", 3))
                elif kind == "g":
                    pool.wait_ge(*at_pe["m"]("AV3", 3))
                if kind == "n":
                    if only(b):
                        pool.wait_ge(*p_act("e17"))
                        pool.wait_ge(*n2_tab("gain"))
                        pool.wait_ge(*v_ld("v31"))
                    for e in range(2):
                        for cb in range(4):
                            i = pool.tensor_tensor(qz[:, e, cb * P:(cb + 1) * P].rearrange("p (r q) -> p r q", r=8),
                                                   flat(qnT[:, bass.ds(b, 1), :]).rearrange("p (r c) -> p r c", r=8)[:, :, cb * 16:cb * 16 + 16],
                                                   cols[:, V_HALF + e:V_HALF + e + 1].unsqueeze(2).broadcast_to([P, 8, 16]), ALU.mult)
                        S.mark(i, f"q{e}")
                    S.mark(pool.tensor_copy(vst, vband[:, :, bass.ds(b * P, P)]), "v")
                    pool.wait_ge(*bias_ld("bias", b))
                    S.mark(pool.tensor_tensor(bias, bias, bmask.unsqueeze(1).broadcast_to([P, 2, 3, 256]), ALU.add), "bias")
                elif kind == "m":
                    S.mark(pool.tensor_copy(qst, flat(qmT[:, bass.ds(b, 1), :])), "q0")
                    S.mark(pool.tensor_copy(vst[:, 0:2, :], mvN[:, :, bass.ds(b * P, P)]), "v")
                else:
                    if only(b):
                        pool.wait_ge(*r_act("kT1"))
                    for e in range(2):
                        S.mark(pool.tensor_tensor(qz[:, e, :], flat(qgT[:, bass.ds(b, 1), :]),
                                                  cols[:, V_HALF + e:V_HALF + e + 1].broadcast_to([P, 512]), ALU.mult), f"q{e}")
                    S.mark(pool.tensor_copy(vst[:, 0:4, 0:64], vdup[:, :, bass.ds(b * 64, 64)]), "v")

            def staged(kind):
                stage(kind, 0)
                with pool.Fori(1, 4) as b:
                    stage(kind, b)
            staged("n")

            for t in range(NT):
                pool.wait_ge(*p_act(f"e{26 + t}"))
                r_pool.mark(pool.tensor_tensor(ro[:, t, :], qkN[:, t, 0:640], qkN[:, t, 0:640], ALU.mult), f"sq{t}")
            staged("m")
            for t in range(NT):
                pool.wait_ge(*r_vec(f"scaled{t}"))
                x = qkN[:, t, 0:640].rearrange("p (h d) -> p h d", h=10)
                pool.tensor_tensor(x[:, 0:8, :], x[:, 0:8, :], gain[:, 0:1, :].broadcast_to([P, 8, 64]), ALU.mult)
                r_pool.mark(pool.tensor_tensor(x[:, 8:10, :], x[:, 8:10, :], gain[:, 1:2, :].broadcast_to([P, 2, 64]), ALU.mult), f"gain{t}")
            pool.wait_ge(*r_vec("rope3"))
            k3 = ro[:, :, 512:640].rearrange("p t (a d) -> p t a d", a=2)
            for e in range(2):
                i = pool.tensor_copy(kdup[:, :, :, 64 * e:64 * e + 64], k3)
            r_pool.mark(i, "dup")
            for n in range(4):
                i = pool.tensor_copy(vdup[:, :, n * 64:(n + 1) * 64], qkN[:, :, 640 + n // 2 * 64:704 + n // 2 * 64])
            r_pool.mark(i, "vdup")
            pool.wait_ge(*r_pool("vdup"))
            staged("g")

            for t in range(NT):
                pool.wait_ge(*l_vec(f"n{t}"))
                if t == 0:
                    pool.wait_ge(*l_row("ln1_b_2"))
                l_pool.mark(pool.tensor_tensor(v2[:, t, :], v2[:, t, :], lnrow[:, 0, :], ALU.mult), f"g{t}")
                pool.wait_ge(*l_pool(f"g{t}"))
                l_pool.mark(pool.tensor_tensor(XR[:, t, :], v2[:, t, :], lnrow[:, 1, :], ALU.add), f"x{t}" if t < 3 else "x3")
            for t in range(NT):
                pool.wait_ge(*f_vec(f"n{t}"))
                if t == 0:
                    pool.wait_ge(*f_rowl("ln2_b_2"))
                f_pool.mark(pool.tensor_tensor(acc[:, t, :], acc[:, t, :], lnrow[:, 0, :], ALU.mult), f"g{t}")
                pool.wait_ge(*f_pool(f"g{t}"))
                f_pool.mark(pool.tensor_tensor(XR[:, t, :], acc[:, t, :], lnrow[:, 1, :], ALU.add), f"x{t}")

        @block.scalar
        def _(act):
            act.wait_ge(*ld_const("cols"))
            act.wait_ge(*ld_x("x"))
            for t in range(NT):
                n_act.mark(act.activation(AT[:, 2 * t:2 * t + 2, :], XR[:, t, :].rearrange("p (a b) -> p a b", a=2), ACT.Square, accum_out=stat[:, t:t + 1]), f"sq{t}")
            act.wait_ge(*z_pool("one"))
            act.wait_ge(*n_act("sq3"))
            n_act.mark(act.activation(stat[:, 4:8], stat[:, 0:4], ACT.Sqrt, bias=eps, scale=1.0 / DM), "rms")
            for b in range(0, KB, 2):
                act.wait_ge(*n_pe(f"T{b}"))
                n_act.mark(act.activation(AT[:, b, :], psum[b][:, :], ACT.Copy, scale=cols[:, V_MIXPRE + b:V_MIXPRE + b + 1]), f"AT{b}")

            for q in range(4):
                act.wait_ge(*n_act(f"AT{2 * q}"))
                act.wait_ge(*n_vec(f"AT{2 * q + 1}"))
                high(act, n_act, at_hi[:, 2 * q:2 * q + 2, :], AT[:, 2 * q:2 * q + 2, :], f"ATh{q}")

            act.wait_ge(*s_pe("proj"))
            act.wait_ge(*z_pool("pads"))
            act.activation(ST[32:40, :], psum[3][32:40, :], ACT.Sigmoid)
            s_act.link(act, act.activation(u8[0:8, 0, :], psum[3][0:8, :], ACT.Identity, bias=cols[0:8, V_DT:V_DT + 1]))
            s_act.link(act, act.activation(u8[0:8, 1, :], u8[0:8, 0, :], ACT.Abs))
            s_act.link(act, act.activation(u8[0:8, 1, :], u8[0:8, 1, :], ACT.Exp, scale=-1.0))
            s_act.mark(act.activation(stat[0:8, 8:9], cols[0:8, V_ALOG:V_ALOG + 1], ACT.Exp), "alog")
            s_act.mark(act.activation(u8[0:8, 1, :], u8[0:8, 1, :], ACT.Ln, bias=one[0:8, :]), "ln")
            act.wait_ge(*s_vec("kdiff"))
            s_act.mark(act.activation(ST[64:72, :], u8[0:8, 2, :], ACT.Exp), "kd")
            s_act.mark(act.activation(ST[96:104, :], ST[0:8, :], ACT.Exp), "eg")

            def split_a(p, n):
                if n % 4 == 0:
                    act.wait_ge(*a_w[n // 4](("k", "v", "z")[n // 4], p))
                if n >= 4:
                    act.wait_ge(*g_pe(f"g{n - 4}", p))
                elif not (only(p) and p == 0):
                    act.wait_ge(*g_pe("g11", p - 1))
                if n < 8:
                    high(act, g_act, h_col[n % 4], ring[n // 4][:, :, n % 4 * P:(n % 4 + 1) * P], f"w{n}")
                else:
                    high(act, g_act, h_row[n % 4], ring[2][:, n % 4 * 2:n % 4 * 2 + 2, :], f"w{n}")

            def evacuate(p, g):
                act.wait_ge(*g_pe(f"g{g}", p))
                if g < 8:
                    if not only(p):
                        act.wait_ge(*c_vec(f"conv{g}", p - 1))
                    elif g == 0:
                        act.wait_ge(*z_pool("pads"))
                    dst = pre[:, g, 3:515]
                else:
                    if not only(p):
                        act.wait_ge(*c_act("zs", p - 1))
                    dst = zraw[:, g - 8, :]
                g_act.mark(act.activation(dst, psum[g % 2][:, :], ACT.Copy), f"e{g}")
                if g < 8:
                    split_a(p, g + 4)

            def chain_a(p, fill):
                c_act.start()
                first = only(p) and p == 0
                if not first:
                    act.wait_ge(*c_vec("qT1", p - 1))
                    act.wait_ge(*c_vec("kT1", p - 1))
                    act.wait_ge(*c_pe("vN1", p - 1))
                else:
                    act.wait_ge(*n_vec("xn"))
                    act.wait_ge(*n_pe("T7"))
                act.wait_ge(*g_act("e11", p))
                for b in range(8):
                    blk = (p * 2 + b) if b < 2 else (p * 2 + 8 + b - 2) if b < 4 else (p * 4 + 16 + b - 4)
                    c_act.mark(act.activation(y[:, b, :], pre[:, b, 3:515], ACT.Copy,
                                              scale=cols[:, bass.ds(blk * 4 + V_CONV + 3, 1)]), f"tap{b}")
                if not first:
                    act.wait_ge(*c_vec("gate1", p - 1))
                c_act.mark(act.activation(zs, zraw, ACT.Silu), "zs")
                for b in range(8):
                    act.wait_ge(*c_vec(f"conv{b}", p))
                    c_act.mark(act.activation(y[:, b, :], y[:, b, :], ACT.Silu), f"silu{b}")
                for j in range(2):
                    fill(4)
                    prev = (lambda s, what: s(what + "0", p)) if j else (lambda s, what: s(what + "1", p - 1))
                    noprev = first and j == 0
                    if j == 0:
                        fill(A_EARLY)
                    act.wait_ge(*c_act(f"silu{2 + j}", p))
                    if not noprev:
                        act.wait_ge(*prev(c_pe, "wT"))
                        act.wait_ge(*prev(c_pe, "S2_"))
                    c_act.mark(act.activation(sq[:, 0, :], y[:, j, :], ACT.Square), f"sqq{j}")
                    c_act.mark(act.activation(sq[:, 1, :], y[:, 2 + j, :], ACT.Square), f"sqk{j}")
                    act.wait_ge(*c_pe(f"ss{j}", p))
                    if not noprev:
                        act.wait_ge(*prev(c_pe, "V3_"))
                    act.activation(rinv[:, 0, :], psum[2][:, :], ACT.Sqrt, bias=eps)
                    c_act.mark(act.activation(rinv[:, 1, :], psum[3][:, :], ACT.Sqrt, bias=eps), f"root{j}")
                    fill(4)
                    act.wait_ge(*c_vec(f"Dpre{j}", p))
                    c_act.mark(act.activation(D, D, ACT.Exp), f"D{j}")
                    fill(6)
                    for s in range(1, LEVELS):
                        act.wait_ge(*c_pe(f"P{s}_{j}", p))
                        if s > 1:
                            act.wait_ge(*c_pe(f"Y{s - 1}_{j}", p))
                        elif not noprev:
                            act.wait_ge(*prev(c_pe, f"Y{LEVELS - 1}_"))
                            act.wait_ge(*(oa_st[0]("o", p) if j else oa_st[1]("o", p - 1)))
                        c_act.mark(act.activation(PP, psum[4][:, :].rearrange("p (t c) -> p t c", t=NT), ACT.Copy), f"P{s}_{j}")
                        fill(4)
                    act.wait_ge(*c_pe(f"wT{j}", p))
                    if not noprev:
                        act.wait_ge(*prev(c_pe, "V3_"))
                    c_act.mark(act.activation(nwT, psum[7][:, :], ACT.Copy, scale=-1.0), f"wT{j}")
                    fill(1)
                    for t in range(NT):
                        act.wait_ge(*c_pe(f"V{t}_{j}", p))
                        if t:
                            act.wait_ge(*c_pe(f"O{t - 1}{j}", p))
                        elif not noprev:
                            act.wait_ge(*prev(c_pe, "O3"))
                        c_act.mark(act.activation(vnew, psum[2][:, 0:A_DV], ACT.Copy), f"vnew{t}_{j}")
                        fill(2)
                    for t in range(NT):
                        if t == 0:
                            act.wait_ge(*c_pe(f"O3{j}", p))
                        c_act.mark(act.activation(oj[:, t, :], psum[4 + t // 2][:, t % 2 * A_DV:(t % 2 + 1) * A_DV],
                                                  ACT.Square, accum_out=stat[:, t:t + 1]), f"osq{t}_{j}")
                    act.wait_ge(*c_act(f"osq3_{j}", p))
                    c_act.mark(act.activation(stat[:, 4:8], stat[:, 0:4], ACT.Sqrt, bias=eps, scale=1.0 / A_DV), f"orms{j}")
                    fill(2)
                fill(99)

            g_act.start()
            for n in range(4):
                split_a(0, n)
            for g in range(12):
                evacuate(0, g)

            def with_evacuations(p):
                g_act.start()
                for n in range(4):
                    split_a(p, n)
                at = [0]

                def fill(n):
                    for m in range(at[0], min(at[0] + n, 96)):
                        if m % KB == KB - 1:
                            evacuate(p, m // KB)
                    at[0] += n
                chain_a(p - 1, fill)

            with_evacuations(1)
            with act.Fori(2, PAIRS) as p:
                with_evacuations(p)
            chain_a(PAIRS - 1, lambda n: None)

            def merge(x, c):
                m_act[x].start()
                first = only(c) and c == 0
                for n in range(12):
                    b = n - 4
                    if n % 4 == 0 and n < 8:
                        act.wait_ge(*m_w[x][n // 4]("w", c))
                    if n == 5:
                        act.wait_ge(*m_w[x][2]("w", c))
                    if n < 4:
                        if first and n == 0:
                            act.wait_ge(*(g_pe("g11", PAIRS - 1) if x == 0 else bg_pe("g11", B_HEADS - 1)))
                        elif not first:
                            act.wait_ge(*m_pe[x](("lo2", "y2", "lo3", "y3")[n], c - 1))
                    elif n < 8:
                        act.wait_ge(*m_pe[x](f"gate{b}", c))
                        if not first:
                            act.wait_ge(*m_vec[x](f"mix{b}", c - 1))
                        elif x == 0:
                            act.wait_ge(*c_vec("oT11", PAIRS - 1))
                        else:
                            act.wait_ge(*b_vec("PT3", B_HEADS - 1))
                        m_act[x].mark(act.activation(sg[:, b, :], psum[b % 2][:, :], ACT.Sigmoid), f"sg{b}")
                    else:
                        act.wait_ge(*m_pe[x](("lo0", "y0", "lo1", "y1")[n - 8], c))
                    slot, q = (0, n) if n < 4 else (1 + n % 2, b // 2)
                    high(act, m_act[x], h_col[n % 4], ring[slot][:, :, q * P:(q + 1) * P], f"w{n}")
                    if n == 7 and first:
                        act.wait_ge(*ot_ld[x]("o"))
                        for k in range(8):
                            high(act, ot_act[x], oT_hi[:, 2 * k:2 * k + 2, :], oT[:, 2 * k:2 * k + 2, :], f"o{k}")
            merge(0, 0)
            with act.Fori(1, 2) as c:
                merge(0, c)

            def split_b(h, n):
                if n % 4 == 0:
                    act.wait_ge(*b_w[n // 4]("k", h))
                if n >= 8:
                    act.wait_ge(*bg_pe("g7", h))
                elif n >= 4:
                    act.wait_ge(*bg_pe(f"g{n - 4}", h))
                elif not (only(h) and h == 0):
                    act.wait_ge(*bg_pe("g11", h - 1))
                elif n == 0:
                    act.wait_ge(*m_pe[0]("y3", 1))
                if n < 4:
                    high(act, bg_act, h_col[n], ring[0][:, :, n * P:(n + 1) * P], f"w{n}")
                else:
                    high(act, bg_act, h_row[n % 4], ring[n // 4][:, n % 4 * 2:n % 4 * 2 + 2, :], f"w{n}")

            def evacuate_b(h, g):
                later = not (only(h) and h == 0)
                act.wait_ge(*bg_pe(f"g{g}", h))
                if g < 4:
                    if later:
                        act.wait_ge(*b_rope("ropeq", h - 1))
                        act.wait_ge(*b_pool("ropek", h - 1))
                    elif g == 0:
                        act.wait_ge(*m_vec[0]("mix3", 1))
                    bg_act.mark(act.activation(qkr[:, g, :], psum[g % 2][:, :], ACT.Copy), f"e{g}")
                elif g < 8:
                    if later:
                        act.wait_ge(*b_pe("O3", h - 1))
                    bg_act.mark(act.activation(bv[:, g - 4, :], psum[g % 2][:, :], ACT.Copy), f"e{g}")
                else:
                    if later:
                        act.wait_ge(*b_vec("gate", h - 1))
                    bg_act.mark(act.activation(bg[:, g - 8, :], psum[g % 2][:, :], ACT.Silu), f"e{g}")

            def attn_b(h):
                b_act.start()
                for t in range(NT):
                    act.wait_ge(*b_pe(f"O{t}", h))
                    if t == 0 and not (only(h) and h == 0):
                        act.wait_ge(*b_pe("oT3", h - 1))
                    b_act.mark(act.activation(bo[:, t, :], psum[(6, 7, 2, 3)[t]][:, :], ACT.Square, accum_out=stat[:, t:t + 1]), f"osq{t}")
                act.wait_ge(*b_act("osq3", h))
                b_act.mark(act.activation(stat[:, 4:8], stat[:, 0:4], ACT.Sqrt, bias=eps, scale=1.0 / B_DV), "orms")

            def step_b(h):
                bg_act.start()
                for n in range(4):
                    split_b(h, n)
                for g in range(4):
                    evacuate_b(h, g)
                    split_b(h, g + 4)
                if not only(h):
                    attn_b(h - 1)
                for g in range(4, 8):
                    evacuate_b(h, g)
                for n in range(8, 12):
                    split_b(h, n)
                for g in range(8, 12):
                    evacuate_b(h, g)
            step_b(0)
            with act.Fori(1, B_HEADS) as h:
                step_b(h)
            attn_b(B_HEADS - 1)
            merge(1, 0)
            with act.Fori(1, 2) as c:
                merge(1, c)

            def post_norm(pe_s, act_s, vec_s, bank, last, prenorm, hN):
                for t in range(NT):
                    for c in range(2):
                        act.wait_ge(*last(t, c))
                        act_s.mark(act.activation(hN[:, t, c * 512:(c + 1) * 512], psum[bank(t, c)][:, :], ACT.Square,
                                                  accum_out=stat[:, 2 * t + c:2 * t + c + 1]), f"sq{t}{c}")
                    act.wait_ge(*vec_s(f"ss{t}"))
                    act_s.mark(act.activation(stat[:, 12:13], stat[:, 2 * t:2 * t + 1], ACT.Sqrt, bias=eps, scale=1.0 / DM), f"rms{t}")
                    if prenorm:
                        act.wait_ge(*vec_s(f"x{t}"))
                        act_s.link(act, act.activation(hN[:, t, :], XR[:, t, :], ACT.Square, accum_out=stat[:, 13:14]))
                        act_s.mark(act.activation(stat[:, 14:15], stat[:, 13:14], ACT.Sqrt, bias=eps, scale=1.0 / DM), f"hrms{t}")
            act.wait_ge(*m_vec[1]("mix3", 1))
            for n in range(8):
                if n % 2 == 0:
                    high(act, o_act, mix_hi[:, n:n + 2, :], mixT[:, n:n + 2, :], f"mix{n // 2}")
                if n < 2:
                    act.wait_ge(*o_w[n]("w"))
                if n >= 4:
                    act.wait_ge(*o_pe(f"p{n - 4}"))
                high(act, o_act, h_row[n % 4], ring[n % 2][:, n // 2 * 2:n // 2 * 2 + 2, :], f"w{n}")
            post_norm(o_pe, o_act, o_vec, lambda t, c: 2 * t + c, lambda t, c: o_pe(f"m{t}{c}"), True, o_hN)

            act.wait_ge(*o_vec("AT31"))
            for q in range(4):
                high(act, o_act, at_hi[:, 2 * q:2 * q + 2, :], AT[:, 2 * q:2 * q + 2, :], f"ATh{q}")

            def mlp_up(i):
                u_act.start()
                for g in range(-3, 16):
                    n = g + 3
                    if n < 16:
                        if n % 4 == 0:
                            act.wait_ge(*u_w[n // 4]("w", i))
                        if n >= 4:
                            act.wait_ge(*u_pe(f"g{n - 4}", i))
                        elif not only(i):
                            act.wait_ge(*u_pe(f"g{n + 12}", i - 1))
                        high(act, u_act, h_col[n % 4], ring[n // 4 % 2][:, :, n % 4 * P:(n % 4 + 1) * P], f"w{n}")
                    if g < 0:
                        continue
                    act.wait_ge(*u_vec(f"relu{g}", i))
                    at = bass.ds(i * 16 + g, 1)
                    u_act.mark(act.activation(ffT[:, at, :], ffT[:, at, :], ACT.Square), f"ff{g}")
            mlp_up(0)
            with act.Fori(1, 2) as i:
                mlp_up(i)

            def mlp_down(c):
                dn_act.start()
                for n in range(16):
                    if n % 4 == 0:
                        act.wait_ge(*d_w[n // 4]("w", c))
                    if n >= 4:
                        act.wait_ge(*d_pe(f"p{n - 4}", c))
                    elif not only(c):
                        act.wait_ge(*d_pe(f"p{n + 12}" if n < 3 else "m3", c - 1))
                    elif n == 0:
                        act.wait_ge(*u_pe("g15", 1))
                        act.wait_ge(*u_act("ff15", 1))
                    high(act, dn_act, h_row[n % 4], ring[n // 4 % 2][:, n % 4 * 2:n % 4 * 2 + 2, :], f"w{n}")
                    high(act, dn_act, ff_hi[:, n % 4, :, :], ffT[:, 2 * n:2 * n + 2, :], f"ff{n}")
            mlp_down(0)
            with act.Fori(1, 2) as c:
                mlp_down(c)
            post_norm(d_pe, d_act, d_vec, lambda t, c: 4 * c + t, lambda t, c: d_pe("m3", 1), False, hN)

            def attend_body(kind, b):
                pe_s, act_s, vec_s = at_pe[kind], at_act[kind], at_vec[kind]
                act_s.start()
                units, nk = (4, 256) if kind == "m" else (8, 256 if kind == "n" else 512)
                for n in range(units + 1):
                    if n < units:
                        act.wait_ge(*vec_s(f"max{n}", b))
                        if n >= 3:
                            act.wait_ge(*pe_s(f"T{n - 3}", b))
                        src = sc[:, n % 2, 0:nk] if kind == "n" else psum[n % 3][:, 0:nk]
                        act_s.mark(act.activation(pr[:, n % 3, 0:nk], src, ACT.Exp, bias=nmax[:, n:n + 1], accum_out=psums[:, n:n + 1]), f"ex{n}")
                    if n:
                        m = n - 1
                        act.wait_ge(*pe_s(f"T{m}", b))
                        if m >= 2:
                            act.wait_ge(*pe_s(f"AV{m - 2}", b))
                        act_s.mark(act.activation(pT[:, m % 2, 0:nk], psum[3 + m % 2][:, 0:nk], ACT.Copy), f"pT{m}")

            def attend(kind):
                attend_body(kind, 0)
                with act.Fori(1, 4) as b:
                    attend_body(kind, b)

            for g in range(30):
                if g == 22:
                    attend("n")
                act.wait_ge(*p_pe(f"g{g}"))
                if g == 0:
                    act.wait_ge(*d_vec("x3"))
                src = psum[6 + g % 2]
                if g < 4:
                    dst, src = mkT[:, g, :], src[:, 0:256]
                elif g < 6:
                    dst = mvN[:, g - 4, :]
                elif g < 10:
                    dst = qmT[:, g - 6, :]
                elif g < 14:
                    dst = qnT[:, g - 10, :]
                elif g < 18:
                    dst = knT[:, g - 14, :]
                elif g < 22:
                    dst = vnN[:, g - 18, :]
                elif g < 26:
                    dst = qkN[:, g - 22, 0:512]
                else:
                    dst, src = qkN[:, g - 26, 512:768], src[:, 0:256]
                scale = 128 ** -0.5 if 6 <= g < 10 else 0.125 if 10 <= g < 14 else 1.0
                p_act.mark(act.activation(dst, src, ACT.Copy, scale=scale), f"e{g}")
            attend("m")
            act.wait_ge(*r_vec("ss"))
            r_act.mark(act.activation(gst, gst, ACT.Sqrt, bias=eps, scale=1.0 / 64), "root")
            for n in range(6):
                act.wait_ge(*r_pe(f"T{n}"))
                src = psum[6 + n % 2][:, :]
                if n < 4:
                    r_act.mark(act.activation(qgT[:, n, :], src, ACT.Copy, scale=0.125), f"qT{n}")
                else:
                    act.activation(kgT[:, 2 * (n - 4), :], src, ACT.Copy)
                    r_act.mark(act.activation(kgT[:, 2 * (n - 4) + 1, :], src, ACT.Copy), f"kT{n - 4}")
            attend("g")

            def merge2(c):
                mg_act.start()
                for g in range(3):
                    for b in range(4):
                        act.wait_ge(*mg_pe(f"gate{g}{b}", c))
                        if g:
                            act.wait_ge(*mg_vec(f"m{g - 1}{b}", c))
                        elif not only(c):
                            act.wait_ge(*mg_vec(f"m2{b}", c - 1))
                        elif b == 0:
                            act.wait_ge(*at_pe["g"]("AV7", 3))
                        mg_act.mark(act.activation(sg2[:, b, :], psum[b][:, :], ACT.Sigmoid, bias=cols[:, bass.ds(c * 4 + V_BG + g * 8 + b, 1)]), f"sg{g}{b}")
            merge2(0)
            with act.Fori(1, 2) as c:
                merge2(c)
            for t in range(NT):
                act.wait_ge(*l_vec(f"var{t}"))
                l_act.mark(act.activation(stat[:, 2:3], stat[:, 1:2], ACT.Sqrt, bias=eps5), f"root{t}")
            act.wait_ge(*q_vec("less"))
            q_act.mark(act.activation(affN, affN, ACT.Exp), "exp")

            def experts(p):
                e_act.start()
                for q in range(2):
                    act.wait_ge(*e_pe(f"x{q}", p))
                    if q == 0 and not only(p):
                        act.wait_ge(*e_pe("group3", p - 1))
                    e_act.mark(act.activation(xst[:, 4 * q:4 * q + 4, :], psum[q][:, :].rearrange("p (b c) -> p b c", b=4), ACT.Copy), f"x{q}")
                for f in range(2):
                    act.wait_ge(*e_pe(f"group{2 * f}", p))
                    if not only(p):
                        act.wait_ge(*e_pe(f"a{f}", p - 1))
                    e_act.mark(act.activation(ga[:, f, :], psum[3 + 2 * f][:, :], ACT.Silu), f"silu{f}")
                for f in range(2):
                    act.wait_ge(*e_pe(f"a{f}", p))
                    if not only(p):
                        act.wait_ge(*e_pe("group5", p - 1))
                    e_act.mark(act.activation(actT[:, 4 * f:4 * f + 4, :], psum[(7, 3)[f]][:, :].rearrange("p (b c) -> p b c", b=4), ACT.Copy), f"a{f}")
                for n in range(2):
                    act.wait_ge(*e_pe(f"group{4 + n}", p))
                    if not only(p):
                        act.wait_ge(*e_pe("y7", p - 1))
                    e_act.mark(act.activation(ye[:, n, :], psum[4 + n][:, :], ACT.Copy), f"y{n}")
            experts(0)
            with act.Fori(1, NE // 2) as p:
                experts(p)
            for t in range(NT):
                act.wait_ge(*f_vec(f"var{t}"))
                f_act.mark(act.activation(stat[:, 2:3], stat[:, 1:2], ACT.Sqrt, bias=eps5), f"root{t}")

        @block.tensor
        def _(pe):
            pe.wait_ge(*ld_const("cols"))
            pe.wait_ge(*n_vec("xn"))
            for b in range(KB):
                for t in range(NT):
                    mm = pe.transpose(psum[b][:, t * P:(t + 1) * P], XR[:, t, b * P:(b + 1) * P], ident)
                n_pe.mark(mm, f"T{b}")
            pe.wait_ge(*ld_small("w"))
            pe.wait_ge(*n_act("AT6"))
            pe.wait_ge(*n_vec("AT7"))
            for k in range(KB):
                mm = pe.matmul(psum[3][0:40, :], wsm[:, k, :], AT[:, k, :], start=(k == 0), stop=(k == KB - 1))
            s_pe.mark(mm, "proj")

            def gemm_a(p):
                g_pe.start()
                for g in range(12):
                    slot = g // 4
                    if g <= 8:
                        pe.wait_ge(*ga_vec(f"w{g}", p))
                    if g >= 2:
                        pe.wait_ge(*g_act(f"e{g - 2}", p))
                    elif not (only(p) and p == 0):
                        pe.wait_ge(*g_act(f"e{g + 10}", p - 1))
                    for k in range(KB):
                        if only(p) and p == 0 and g == 0 and k % 2 == 0:
                            pe.wait_ge(*n_vec(f"ATl{k // 2}"))
                        if g == 8 and k and k % 2 == 0:
                            pe.wait_ge(*ga_vec(f"w{8 + k // 2}", p))
                        if g < 8:
                            lhs, rhs = (h_col[g % 4][:, k, :], ring[slot][:, k, g % 4 * P:(g % 4 + 1) * P]), (at_hi[:, k, :], AT[:, k, :])
                        else:
                            lhs = [x[:, k, (g - 8) * P:(g - 7) * P] for x in (at_hi, AT)]
                            rhs = (h_row[k // 2][:, k % 2, :], ring[slot][:, k, :])
                        mm = product(pe, psum[g % 2][:, :], lhs, rhs, k == 0, k == KB - 1)
                        if k == KB - 1:
                            g_pe.mark(mm, f"g{g}")
                        yield

            def chain_a(p, fill):
                c_pe.start()
                for j in range(2):
                    prev = (lambda s, what: s(what + "0", p)) if j else (lambda s, what: s(what + "1", p - 1))
                    noprev = only(p) and p == 0 and j == 0
                    fill(4)
                    if j == 0:
                        fill(A_EARLY)
                    pe.wait_ge(*c_act(f"sqk{j}", p))
                    if not noprev:
                        pe.wait_ge(*prev(c_act, "vnew3_"))
                        pe.wait_ge(*prev(c_vec, f"S{NT - 2}_"))
                    else:
                        pe.wait_ge(*s_vec("begN"))
                        pe.wait_ge(*n_act("AT6"))
                        pe.wait_ge(*n_vec("AT7"))
                    pe.matmul(psum[2][:, :], ones, sq[:, 0, :], start=True, stop=True)
                    c_pe.mark(pe.matmul(psum[3][:, :], ones, sq[:, 1, :], start=True, stop=True), f"ss{j}")
                    fill(4)
                    pe.wait_ge(*c_vec(f"qT{j}", p))
                    pe.wait_ge(*c_vec(f"kT{j}", p))
                    pe.wait_ge(*c_pool(f"kbT{j}", p))
                    if not noprev:
                        pe.wait_ge(*prev(c_vec, "gate"))
                    for t in range(NT):
                        c = slice(t * P, (t + 1) * P)
                        mm = pe.matmul(psum[4][:, c], kT[:, c], kbT[:, c], start=True, stop=True)
                    c_pe.mark(mm, f"KK{j}")
                    for t in range(NT):
                        c = slice(t * P, (t + 1) * P)
                        mm = pe.matmul(psum[5][:, c], kT[:, c], qT[:, c], start=True, stop=True)
                    c_pe.mark(mm, f"KQ{j}")
                    pe.wait_ge(*c_act(f"root{j}", p))
                    for t in range(NT):
                        c = slice(t * P, (t + 1) * P)
                        mm = pe.transpose(psum[2][:, c], kT[:, c], ident)
                    c_pe.mark(mm, f"kN{j}")
                    pe.wait_ge(*c_act(f"silu{5 + 2 * j}", p))
                    if not noprev:
                        pe.wait_ge(*prev(c_vec, "oT1"))
                    for t in range(NT):
                        for d in range(2):
                            mm = pe.transpose(psum[3 if t < 2 else 7][:, (t % 2 * 2 + d) * P:(t % 2 * 2 + d + 1) * P],
                                              y[:, 4 + 2 * j + d, t * P:(t + 1) * P], ident)
                    c_pe.mark(mm, f"vN{j}")
                    fill(4)
                    pe.wait_ge(*c_pool(f"NM0_{j}", p))
                    if not noprev:
                        pe.wait_ge(*prev(c_vec, "oT0"))
                    for t in range(NT):
                        mm = pe.transpose(psum[6][:, t * P:(t + 1) * P], NM[:, 0, t * P:(t + 1) * P], ident)
                    c_pe.mark(mm, f"P0_{j}")
                    fill(2)
                    for s in range(1, LEVELS):
                        pe.wait_ge(*c_pool(f"NM{s}_{j}", p))
                        pe.wait_ge(*c_vec(f"X{s - 1}_{j}", p))
                        if s == 1:
                            pe.wait_ge(*c_vec(f"LT{j}", p))
                        for t in range(NT):
                            mm = pe.matmul(psum[4][:, t * P:(t + 1) * P], NM[:, s % 2, t * P:(t + 1) * P], X[:, t, :], start=True, stop=True)
                        c_pe.mark(mm, f"P{s}_{j}")
                        fill(2)
                        pe.wait_ge(*c_act(f"P{s}_{j}", p))
                        pe.wait_ge(*c_vec(f"Y{s - 1}_{j}", p))
                        if s < LEVELS - 1:
                            if s == 1:
                                pe.wait_ge(*c_vec(f"ATT{j}", p))
                            for t in range(NT):
                                mm = pe.matmul(psum[5][:, t * P:(t + 1) * P], Y[:, t, :], PP[:, t, :], start=True, stop=True)
                            c_pe.mark(mm, f"X{s}_{j}")
                        for t in range(NT):
                            mm = pe.matmul(psum[6][:, t * P:(t + 1) * P], PP[:, t, :], Y[:, t, :], start=True, stop=True)
                        c_pe.mark(mm, f"Y{s}_{j}")
                        fill(2)
                    pe.wait_ge(*c_vec(f"Y{LEVELS - 1}_{j}", p))
                    pe.wait_ge(*c_vec(f"kbeg{j}", p))
                    pe.wait_ge(*c_vec(f"vb{j}", p))
                    for t in range(NT):
                        mm = pe.matmul(psum[7][:, t * P:(t + 1) * P], kbeg[:, t, :], Y[:, t, :], start=True, stop=True)
                    c_pe.mark(mm, f"wT{j}")
                    fill(1)
                    for t in range(NT):
                        c = slice(t * P, (t + 1) * P)
                        if t == 0:
                            pe.wait_ge(*c_vec(f"kd{j}", p))
                            pe.wait_ge(*c_pool(f"qeT{j}", p))
                        else:
                            pe.wait_ge(*c_act(f"vnew{t - 1}_{j}", p))
                        mm = pe.matmul(psum[2][:, 0:A_DV], Y[:, t, :], vb[:, t, :], start=True, stop=(t == 0))
                        if t:
                            if t == 1:
                                pe.wait_ge(*c_act(f"wT{j}", p))
                            pe.wait_ge(*c_vec(f"S{t - 1}_{j}", p) if t < NT else None)
                            mm = pe.matmul(psum[2][:, 0:A_DV], nwT[:, c], S, start=False, stop=True)
                        c_pe.mark(mm, f"V{t}_{j}")
                        fill(1)
                        O = psum[4 + t // 2][:, t % 2 * A_DV:(t % 2 + 1) * A_DV]
                        if t:
                            pe.matmul(O, qeT[:, c], S, start=True, stop=False)
                        pe.wait_ge(*c_act(f"vnew{t}_{j}", p))
                        if t < NT - 1:
                            c_pe.mark(pe.matmul(psum[3][:, 0:A_DV], kdN[:, t, :], vnew, start=True, stop=True), f"S{t}_{j}")
                        c_pe.mark(pe.matmul(O, ATT[:, t, :], vnew, start=(t == 0), stop=True), f"O{t}{j}")
                        fill(1)
                    fill(2)
                    pe.wait_ge(*c_vec(f"gate{j}", p))
                    pe.wait_ge(*c_act(f"wT{j}", p))
                    for d in range(2):
                        for t in range(NT):
                            mm = pe.transpose(psum[6 + d][:, t * P:(t + 1) * P], oN[:, t, d * P:(d + 1) * P], ident)
                        c_pe.mark(mm, f"oT{d}{j}")
                fill(99)

            steps = gemm_a(0)
            for _ in range(4 * KB):
                next(steps)
            pe.wait_ge(*s_act("eg"))
            pe.wait_ge(*s_vec("gcum"))
            for t in range(NT):
                mm = pe.transpose(psum[2][:, t * P:(t + 1) * P], ST[:, t * P:(t + 1) * P], ident)
            s_pe.mark(mm, "stT")
            for _ in steps:
                pass

            def with_gemm(p):
                steps = gemm_a(p)

                def fill(n):
                    for _ in range(n):
                        next(steps, None)
                chain_a(p - 1, fill)

            with_gemm(1)
            with pe.Fori(2, PAIRS) as p:
                with_gemm(p)
            chain_a(PAIRS - 1, lambda n: None)

            def merge(x, c):
                later = not (only(c) and c == 0)
                m_pe[x].start()
                for b in range(4):
                    pe.wait_ge(*m_vec[x](f"w{b}", c))
                    if b >= 2:
                        pe.wait_ge(*m_act[x](f"sg{b - 2}", c))
                    elif later:
                        pe.wait_ge(*m_act[x](f"sg{b + 2}", c - 1))
                    else:
                        pe.wait_ge(*(g_act(f"e{10 + b}", PAIRS - 1) if x == 0 else bg_act(f"e{10 + b}", B_HEADS - 1)))
                    for k in range(KB):
                        mm = product(pe, psum[b % 2][:, :], (h_col[b][:, k, :], ring[0][:, k, b * P:(b + 1) * P]), (at_hi[:, k, :], AT[:, k, :]),
                                     k == 0, k == KB - 1)
                    m_pe[x].mark(mm, f"gate{b}")
                for b in range(4):
                    if later:
                        pe.wait_ge(*m_vec[x](f"mix{b}", c - 1))
                    elif b == 0:
                        pe.wait_ge(*(c_vec("oT11", PAIRS - 1) if x == 0 else b_vec("oT3", B_HEADS - 1)))
                    for half, name in enumerate(("lo", "y")):
                        pe.wait_ge(*m_vec[x](f"w{4 + 2 * b + half}", c))
                        for k in range(KB):
                            block = half * 8 + k
                            if not later and b == 0 and k % 2 == 0:
                                pe.wait_ge(*ot_vec[x](f"o{block // 2}"))
                            mm = product(pe, psum[2 + b][:, :], (h_col[half + 2 * (b % 2)][:, k, :], ring[1 + half][:, k, b * P:(b + 1) * P]),
                                         (oT_hi[:, block, :], oT[:, block, :]), block == 0, block == 15)
                        m_pe[x].mark(mm, f"{name}{b}")
            merge(0, 0)
            with pe.Fori(1, 2) as c:
                merge(0, c)

            def gemm_b(h, groups):
                for g in groups:
                    slot = g // 4
                    if g < 4 or g % 4 == 0:
                        pe.wait_ge(*bs_vec(f"w{g}", h))
                    if g >= 2:
                        pe.wait_ge(*bg_act(f"e{g - 2}", h))
                    elif not (only(h) and h == 0):
                        pe.wait_ge(*bg_act(f"e{g + 10}", h - 1))
                    else:
                        pe.wait_ge(*m_act[0](f"sg{g + 2}", 1))
                    for k in range(KB):
                        if g % 4 == 0 and g and k and k % 2 == 0:
                            pe.wait_ge(*bs_vec(f"w{g + k // 2}", h))
                        if g < 4:
                            lhs, rhs = (h_col[g][:, k, :], ring[slot][:, k, g * P:(g + 1) * P]), (at_hi[:, k, :], AT[:, k, :])
                        else:
                            lhs = [x[:, k, g % 4 * P:(g % 4 + 1) * P] for x in (at_hi, AT)]
                            rhs = (h_row[k // 2][:, k % 2, :], ring[slot][:, k, :])
                        mm = product(pe, psum[g % 2][:, :], lhs, rhs, k == 0, k == KB - 1)
                    bg_pe.mark(mm, f"g{g}")

            def scores_b(h):
                b_pe.start()
                pe.wait_ge(*b_rope("ropeq", h))
                pe.wait_ge(*b_pool("ropek", h))
                pe.wait_ge(*(b_vec("oT3", h - 1) if not (only(h) and h == 0) else m_vec[0]("mix3", 1)))
                for m in range(NT):
                    for k in range(2):
                        mm = pe.matmul(psum[2 + m][:, m * P:], qkT[:, 2 + k, m * P:(m + 1) * P], qkT[:, k, m * P:],
                                       start=(k == 0), stop=(k == 1))
                    b_pe.mark(mm, f"S{m}")

            def values_b(h):
                for t in range(NT):
                    pe.wait_ge(*b_vec("PT3" if t == 3 else f"PT{max(t, 1)}", h))
                    if t == 0:
                        pe.wait_ge(*bg_act("e7", h))
                    for m in range(t + 1):
                        mm = pe.matmul(psum[(6, 7, 2, 3)[t]][:, :], PT[:, m, t * P:(t + 1) * P], bv[:, m, :], start=(m == 0), stop=(m == t))
                    b_pe.mark(mm, f"O{t}")

            def turn_b(h):
                pe.wait_ge(*b_vec("gate", h))
                for d in range(4):
                    for t in range(NT):
                        mm = pe.transpose(psum[4 + d][:, t * P:(t + 1) * P], bo[:, t, d * P:(d + 1) * P], ident)
                    b_pe.mark(mm, f"oT{d}")

            bg_pe.start()
            gemm_b(0, range(12))

            def step_b(h):
                bg_pe.start()
                scores_b(h - 1)
                gemm_b(h, range(4))
                values_b(h - 1)
                gemm_b(h, range(4, 8))
                turn_b(h - 1)
                gemm_b(h, range(8, 12))
            with pe.Fori(1, B_HEADS) as h:
                step_b(h)
            scores_b(B_HEADS - 1)
            values_b(B_HEADS - 1)
            turn_b(B_HEADS - 1)
            merge(1, 0)
            with pe.Fori(1, 2) as c:
                merge(1, c)

            for n in range(8):
                k, c = n // 2 * 2, n % 2
                pe.wait_ge(*o_vec(f"w{n}"))
                for t in range(NT):
                    for a in range(2):
                        mm = product(pe, psum[2 * t + c][:, :], [x[:, k + a, t * P:(t + 1) * P] for x in (mix_hi, mixT)],
                                     (h_row[n % 4][:, a, :], ring[c][:, k + a, :]), k + a == 0, k + a == KB - 1)
                    if n >= 6:
                        o_pe.mark(mm, f"m{t}{c}")
                if n < 6:
                    o_pe.mark(mm, f"p{n}")

            def turn(pe_s, src, bank, ready):
                for t in range(NT):
                    pe.wait_ge(*ready(t))
                    for q in range(2):
                        for b in range(4):
                            mm = pe.transpose(psum[bank(t, q)][:, b * P:(b + 1) * P], src[:, t, (4 * q + b) * P:(4 * q + b + 1) * P], ident)
                        pe_s.mark(mm, f"T{t}{q}")
            turn(o_pe, o_hN, lambda t, q: 2 * t + q, lambda t: o_vec(f"hn{t}"))

            def mlp_up(i):
                u_pe.start()
                for g in range(16):
                    pe.wait_ge(*u_vec(f"w{g}", i))
                    if g >= 4:
                        pe.wait_ge(*u_vec(f"relu{g - 4}", i))
                    elif not (only(i) and i == 0):
                        pe.wait_ge(*u_vec(f"relu{g + 12}", i - 1))
                    for k in range(KB):
                        if only(i) and g == 0 and k % 2 == 0:
                            pe.wait_ge(*o_vec(f"ATl{k // 2}"))
                        mm = product(pe, psum[g % 4][:, :], (h_col[g % 4][:, k, :], ring[g // 4 % 2][:, k, g % 4 * P:(g % 4 + 1) * P]),
                                     (at_hi[:, k, :], AT[:, k, :]), k == 0, k == KB - 1)
                    u_pe.mark(mm, f"g{g}")
            mlp_up(0)
            with pe.Fori(1, 2) as i:
                mlp_up(i)

            def mlp_down(c):
                d_pe.start()
                if only(c):
                    pe.wait_ge(*u_vec("relu15", 1))
                for n in range(16):
                    pe.wait_ge(*dn_vec(f"ff{n}", c))
                    for t in range(NT):
                        for a in range(2):
                            mm = product(pe, ps_all[:, bass.ds(c * 4 + t, 1), :].rearrange("p a n -> p (a n)"),
                                         [x[:, n % 4, a, t * P:(t + 1) * P] for x in (ff_hi, ff_lo)],
                                         (h_row[n % 4][:, a, :], ring[n // 4 % 2][:, n % 4 * 2 + a, :]), n + a == 0, n == 15 and a == 1)
                        if n == 15:
                            d_pe.mark(mm, f"m{t}")
                    if n < 15:
                        d_pe.mark(mm, f"p{n}")
            mlp_down(0)
            with pe.Fori(1, 2) as c:
                mlp_down(c)

            turn(t2_pe, XR, lambda t, q: 4 * q + t, lambda t: d_vec(f"x{t}"))

            pe.wait_ge(*mem_ld("mem"))
            pe.wait_ge(*t2_vec("AT31"))
            for q in range(4):
                for k in range(2):
                    for m in range(2):
                        mm = pe.transpose(psum[q][:, (2 * k + m) * P:(2 * k + m + 1) * P], memN[:, m, (2 * q + k) * P:(2 * q + k + 1) * P], ident)
                p_pe.mark(mm, f"memT{q}")

            def project(groups):
                for g in groups:
                    n = 0 if g < 4 else 1 if g < 6 else (g - 6) // 4 + 2
                    slot, at = n % 3, g if g < 4 else g - 4 if g < 6 else (g - 6) % 4
                    pe.wait_ge(*w2[slot](f"w{n}"))
                    if g >= 2:
                        pe.wait_ge(*p_act(f"e{g - 2}"))
                    elif g == 0:
                        pe.wait_ge(*p_vec("memT3"))
                    for k in range(KB):
                        wide = ring[slot][:, k, :] if g < 26 else ring[slot][:, k, 0:256]
                        block = ring[slot][:, k, at * P:(at + 1) * P]
                        if g < 4:
                            lhsT, rhs = block, memT[:, k, :]
                        elif g < 6:
                            lhsT, rhs = memT[:, k, at * P:(at + 1) * P], wide
                        elif g < 18:
                            lhsT, rhs = block, AT[:, k, :]
                        else:
                            lhsT, rhs = AT[:, k, at * P:(at + 1) * P], wide
                        N = 256 if g < 4 or g >= 26 else 512
                        mm = pe.matmul(psum[6 + g % 2][:, 0:N], lhsT, rhs, start=(k == 0), stop=(k == KB - 1))
                    p_pe.mark(mm, f"g{g}")

            def attend_body(kind, b):
                pe_s, act_s, vec_s, pool_s = at_pe[kind], at_act[kind], at_vec[kind], at_pool[kind]
                pe_s.start()
                units = 4 if kind == "m" else 8
                nk = 512 if kind == "g" else 256
                flat = lambda x: x.rearrange("p a n -> p (a n)")
                for n in range(units + 2):
                    if n < units:
                        e, u = n // 4, n % 4
                        if u == 0:
                            pe.wait_ge(*pool_s(f"q{e}", b))
                        if n >= 3:
                            pe.wait_ge(*(vec_s(f"s{n - 3}", b) if kind == "n" else act_s(f"ex{n - 3}", b)))
                        elif n == 0 and only(b):
                            if kind == "n":
                                pe.wait_ge(*p_act("e17"))
                            else:
                                pe.wait_ge(*(at_act["n"]("ex7", 3) if kind == "m" else at_act["m"]("ex3", 3)))
                                if kind == "g":
                                    pe.wait_ge(*r_act("kT1"))
                        if kind == "n":
                            start = (0, 8, 24, 32)[u]
                            lhsT = qz[:, e, u * P:(u + 1) * P]
                            rhs = flat(knT[:, bass.ds(b, 1), :]).rearrange("p (r c) -> p r c", r=8)[:, :, start:start + 32]
                            o = psum[n % 3][:, 0:nk].rearrange("p (r c) -> p r c", r=8)
                        elif kind == "m":
                            lhsT, rhs, o = qst[:, u * P:(u + 1) * P], flat(mkT[:, bass.ds(b, 1), :]), psum[n % 3][:, 0:nk]
                        else:
                            lhsT, rhs, o = qz[:, e, u * P:(u + 1) * P], flat(kgT[:, bass.ds(b, 1), :]), psum[n % 3][:, 0:nk]
                        pe_s.mark(pe.matmul(o, lhsT, rhs, start=True, stop=True), f"S{n}")
                    if 1 <= n <= units:
                        m = n - 1
                        pe.wait_ge(*vec_s(f"n{m}", b))
                        if m >= 2:
                            pe.wait_ge(*act_s(f"pT{m - 2}", b))
                        for k in range(nk // P):
                            mm = pe.transpose(psum[3 + m % 2][:, k * P:(k + 1) * P], pr[:, m % 3, k * P:(k + 1) * P], ident)
                        pe_s.mark(mm, f"T{m}")
                    if n >= 2:
                        m = n - 2
                        e, u = m // 4, m % 4
                        pe.wait_ge(*act_s(f"pT{m}", b))
                        if m == 0:
                            pe.wait_ge(*pool_s("v", b))
                            if not only(b):
                                pe.wait_ge(*vec_s("y", b - 1))
                            elif kind != "n":
                                pe.wait_ge(*at_vec["n" if kind == "m" else "m"]("y", 3))
                        for k in range(nk // P):
                            if kind == "m":
                                o, lhsT = psum[5][:, u * P:(u + 1) * P], vst[:, k, :]
                            else:
                                o = psum[5][64 * e:64 * e + 64, u * P:(u + 1) * P]
                                lhsT = vst[:, 2 * u + k, 64 * e:64 * e + 64] if kind == "n" else vst[:, k, 0:64]
                            mm = pe.matmul(o, lhsT, pT[:, m % 2, k * P:(k + 1) * P], start=(k == 0), stop=(k == nk // P - 1))
                        pe_s.mark(mm, f"AV{m}")

            def attend(kind):
                attend_body(kind, 0)
                with pe.Fori(1, 4) as b:
                    attend_body(kind, b)

            project(range(22))
            attend("n")
            project(range(22, 30))
            attend("m")
            for n in range(6):
                if n == 0:
                    pe.wait_ge(*r_vec("rope3"))
                if n == 4:
                    pe.wait_ge(*r_pool("dup"))
                if n >= 2:
                    pe.wait_ge(*r_act(f"qT{n - 2}"))
                else:
                    pe.wait_ge(*p_act(f"e{28 + n}"))
                for t in range(NT):
                    src = ro[:, t, n * P:(n + 1) * P] if n < 4 else kdup[:, t, n - 4, :]
                    mm = pe.transpose(psum[6 + n % 2][:, t * P:(t + 1) * P], src, ident)
                r_pe.mark(mm, f"T{n}")
            attend("g")

            def merge2(c):
                mg_pe.start()
                for g in range(3):
                    pe.wait_ge(*mg_w[g % 2](f"w{g}", c))
                    for b in range(4):
                        if g:
                            pe.wait_ge(*mg_act(f"sg{g - 1}{b}", c))
                        elif not only(c):
                            pe.wait_ge(*mg_act(f"sg2{b}", c - 1))
                        elif b == 0:
                            pe.wait_ge(*at_act["g"]("pT7", 3))
                        for k in range(KB):
                            mm = pe.matmul(psum[b][:, :], ring[g % 2][:, k, b * P:(b + 1) * P], AT[:, k, :], start=(k == 0), stop=(k == KB - 1))
                        mg_pe.mark(mm, f"gate{g}{b}")
                    pe.wait_ge(*mg_w[2 + g % 2](f"w{g}", c))
                    for b in range(4):
                        if g:
                            pe.wait_ge(*mg_vec(f"m{g - 1}{b}", c))
                        elif not only(c):
                            pe.wait_ge(*mg_vec(f"m2{b}", c - 1))
                        elif b == 0:
                            pe.wait_ge(*at_vec["g"]("y", 3))
                        for k in range(4):
                            mm = pe.matmul(psum[4 + b][:, :], ring[2 + g % 2][:, k, b * P:(b + 1) * P], yT[:, 4 * g + k, :], start=(k == 0), stop=(k == 3))
                        mg_pe.mark(mm, f"br{g}{b}")
            merge2(0)
            with pe.Fori(1, 2) as c:
                merge2(c)
            for q in range(2):
                pe.wait_ge(*l_w[q]("w"))
            pe.wait_ge(*mg_vec("m23", 1))
            for t in range(NT):
                for c in range(2):
                    b = 2 * t + c
                    for k in range(KB):
                        mm = pe.matmul(psum[b][:, :], mgT[:, k, t * P:(t + 1) * P], ring[c][:, k, :], start=(k == 0), stop=(k == KB - 1))
                    l_pe.mark(mm, f"m{t}{c}")
            turn(q_pe, XR, lambda t, q: 2 * t + q, lambda t: l_pool(f"x{t}"))
            pe.wait_ge(*q_ld("wr"))
            pe.wait_ge(*q_vec("AT31"))
            for t in range(NT):
                for k in range(KB):
                    mm = pe.matmul(psum[0][:, t * NE:(t + 1) * NE], AT[:, k, t * P:(t + 1) * P], wr[:, k, :], start=(k == 0), stop=(k == KB - 1))
            q_pe.mark(mm, "logits")
            pe.wait_ge(*q_vec("aff"))
            for t in range(NT):
                mm = pe.transpose(psum[1][0:NE, t * P:(t + 1) * P], affN[:, t, :], ident)
            q_pe.mark(mm, "affT")
            pe.wait_ge(*q_vec("pos"))
            for t in range(NT):
                mm = pe.transpose(psum[2][:, t * NE:(t + 1) * NE], cum[0:NE, t * P:(t + 1) * P], ident[0:NE, 0:NE])
            q_pe.mark(mm, "posN")

            def experts(p):
                e_pe.start()
                pe.wait_ge(*e_vec("SP", p))
                for b in range(KB):
                    if b % 4 == 0:
                        if not only(p):
                            pe.wait_ge(*e_vec(f"acc{4 + b // 4}", p - 1))
                    for t in range(NT):
                        mm = pe.matmul(psum[b // 4][:, b % 4 * P:(b % 4 + 1) * P], XR[:, t, b * P:(b + 1) * P], SP[:, t, :], start=(t == 0), stop=(t == NT - 1))
                    if b % 4 == 3:
                        e_pe.mark(mm, f"x{b // 4}")
                pe.wait_ge(*e_vec("SG", p))
                if not only(p):
                    pe.wait_ge(*e_vec("acc6", p - 1))
                for t in range(NT):
                    mm = pe.transpose(psum[2][:, t * P:(t + 1) * P], SG[:, t, :], ident)
                e_pe.mark(mm, "SGT")
                for q in range(4):
                    for e in range(2):
                        pe.wait_ge(*e_w[(2 * q + e) % 6](f"w{(2 * q + e) // 6}", p))
                    if q == 0:
                        pe.wait_ge(*e_act("x1", p))
                    if not only(p):
                        pe.wait_ge(*((e_act("a1", p - 1), e_act("y0", p - 1), e_act("y1", p - 1), e_vec("acc7", p - 1))[q]))
                    for k in range(KB):
                        for e in range(2):
                            mm = pe.matmul(psum[3 + q][64 * e:64 * e + 64, :], xst[:, k, 64 * e:64 * e + 64], eslot[(2 * q + e) % 6][:, k, :],
                                           start=(k == 0), stop=(k == KB - 1))
                    e_pe.mark(mm, f"group{q}")
                for f in range(2):
                    pe.wait_ge(*e_vec(f"ga{f}", p))
                    for b in range(4):
                        mm = pe.transpose(psum[(7, 3)[f]][:, b * P:(b + 1) * P], ga[:, f, b * P:(b + 1) * P], ident)
                    e_pe.mark(mm, f"a{f}")
                for n in range(2):
                    q = 4 + n
                    for e in range(2):
                        pe.wait_ge(*e_w[(2 * q + e) % 6](f"w{(2 * q + e) // 6}", p))
                    if n == 0:
                        pe.wait_ge(*e_act("a1", p))
                    for k in range(KB):
                        for e in range(2):
                            mm = pe.matmul(psum[4 + n][64 * e:64 * e + 64, :], actT[:, k, 64 * e:64 * e + 64], eslot[(2 * q + e) % 6][:, k, :],
                                           start=(k == 0), stop=(k == KB - 1))
                    e_pe.mark(mm, f"group{q}")
                for m in range(8):
                    t, n = m // 2, m % 2
                    if m < 2:
                        pe.wait_ge(*e_act(f"y{n}", p))
                    if m == 0:
                        pe.wait_ge(*e_vec("SGT", p))
                    if m >= 4:
                        pe.wait_ge(*e_vec(f"acc{m - 4}", p))
                    e_pe.mark(pe.matmul(psum[(0, 1, 2, 6)[m % 4]][:, :], SGT[:, t * P:(t + 1) * P], ye[:, n, :], start=True, stop=True), f"y{m}")
            experts(0)
            with pe.Fori(1, NE // 2) as p:
                experts(p)

        @block.vector
        def _(dve):
            dve.wait_ge(*n_act("rms"))
            n_vec.link(dve, dve.reciprocal(stat[:, 4:8], stat[:, 4:8]))
            for t in range(NT):
                i = dve.tensor_scalar(XR[:, t, :], XR[:, t, :], stat[:, 4 + t:5 + t], None, ALU.mult)
            n_vec.mark(i, "xn")
            for b in range(1, KB, 2):
                dve.wait_ge(*n_pe(f"T{b}"))
                n_vec.mark(dve.tensor_scalar(AT[:, b, :], psum[b][:, :], cols[:, V_MIXPRE + b:V_MIXPRE + b + 1], None, ALU.mult), f"AT{b}")
            dve.wait_ge(*s_pe("proj"))
            for q in range(4):
                dve.wait_ge(*n_act(f"ATh{q}"))
                a = AT[:, 2 * q:2 * q + 2, :]
                low(dve, n_vec, a, a, at_hi[:, 2 * q:2 * q + 2, :], f"ATl{q}")
            dve.wait_ge(*s_act("ln"))
            s_vec.link(dve, dve.scalar_tensor_tensor(u8[0:8, 0, :], u8[0:8, 0, :], 0.0, u8[0:8, 1, :], ALU.max, ALU.add))
            s_vec.link(dve, dve.tensor_scalar(u8[0:8, 0, :], u8[0:8, 0, :], stat[0:8, 8:9], -1.0, ALU.mult, ALU.mult))
            dve.wait_ge(*z_pool("ST"))
            for t in range(NT):
                c = slice(t * P, (t + 1) * P)
                i = dve.tensor_tensor_scan(ST[0:8, c], ones[0:8, :], u8[0:8, 0, c], 0.0, ALU.mult, ALU.add)
            s_vec.mark(i, "gcum")
            dve.wait_ge(*s_vec("gcum"))
            for t in range(NT):
                c = slice(t * P, (t + 1) * P)
                i = dve.tensor_scalar(u8[0:8, 2, c], ST[0:8, c], ST[0:8, (t + 1) * P - 1:(t + 1) * P], -1.0, ALU.subtract, ALU.mult)
            s_vec.mark(i, "kdiff")

            def split_a(p, n):
                dve.wait_ge(*g_act(f"w{n}", p))
                w, hi = (ring[n // 4][:, :, n % 4 * P:(n % 4 + 1) * P], h_col[n % 4]) if n < 8 else (ring[2][:, n % 4 * 2:n % 4 * 2 + 2, :], h_row[n % 4])
                low(dve, ga_vec, w, w, hi, f"w{n}")
            ga_vec.start()
            for n in range(8):
                split_a(0, n)
            dve.wait_ge(*s_pe("stT"))
            s_vec.link(dve, dve.tensor_copy(stN, psum[2][:, :].rearrange("p (t c) -> p t c", t=NT)))
            s_vec.mark(dve.tensor_tensor(begN, stN[:, :, 32:40], stN[:, :, 96:104], ALU.mult), "begN")
            for n in range(8, 12):
                split_a(0, n)

            def chain_a(p, fill):
                c_vec.start()
                first = only(p) and p == 0
                for b in range(8):
                    blk = (p * 2 + b) if b < 2 else (p * 2 + 8 + b - 2) if b < 4 else (p * 4 + 16 + b - 4)
                    dve.wait_ge(*c_act(f"tap{b}", p))
                    for k in range(2, -1, -1):
                        i = dve.scalar_tensor_tensor(y[:, b, :], pre[:, b, k:k + 512], cols[:, bass.ds(blk * 4 + V_CONV + k, 1)],
                                                     y[:, b, :], ALU.mult, ALU.add)
                        if k:
                            c_vec.link(dve, i, p)
                    c_vec.mark(i, f"conv{b}")
                for j in range(2):
                    h = p * 2 + j
                    prev = (lambda s, what: s(what + "0", p)) if j else (lambda s, what: s(what + "1", p - 1))
                    noprev = first and j == 0

                    def per_token(col):
                        return stN[:, :, bass.ds(h + col, 1)]
                    fill(4)
                    if j == 0:
                        fill(A_EARLY)
                    dve.wait_ge(*c_act(f"root{j}", p))
                    dve.reciprocal(rinv[:, 0, :], rinv[:, 0, :])
                    c_vec.link(dve, dve.reciprocal(rinv[:, 1, :], rinv[:, 1, :]), p)
                    if not noprev:
                        dve.wait_ge(*prev(c_pe, "kN"))
                        dve.wait_ge(*prev(c_pool, "qeT"))
                    c_vec.mark(dve.tensor_tensor(kT, y[:, 2 + j, :], rinv[:, 1, :], ALU.mult), f"kT{j}")
                    c_vec.mark(dve.scalar_tensor_tensor(qT, y[:, j, :], float(A_DK ** -0.5), rinv[:, 0, :], ALU.mult, ALU.mult), f"qT{j}")
                    dve.wait_ge(*a_bc[j]("r2", p))
                    if not noprev:
                        dve.wait_ge(*prev(c_pe, "oT1"))
                    for t in range(NT):
                        i = dve.tensor_scalar(D[:, t, :], bc[:, j, 0, t * P:(t + 1) * P], stN[:, t, bass.ds(h, 1)], 0.0,
                                              ALU.subtract, ALU.min)
                    c_vec.mark(i, f"Dpre{j}")
                    dve.wait_ge(*c_pe(f"KK{j}", p))
                    dve.wait_ge(*c_pool(f"D{j}", p))
                    v4 = lambda b: psum[b][:, :].rearrange("p (t c) -> p t c", t=NT)
                    c_vec.mark(dve.tensor_tensor(LT, v4(4), D, ALU.mult), f"LT{j}")
                    dve.wait_ge(*c_pe(f"KQ{j}", p))
                    if not noprev:
                        dve.wait_ge(*prev(c_pe, "O3"))
                    c_vec.mark(dve.tensor_tensor(ATT, v4(5), D, ALU.mult), f"ATT{j}")
                    fill(4)
                    dve.wait_ge(*c_pe(f"kN{j}", p))
                    dve.wait_ge(*c_pe(f"ss{j}", p))
                    c_vec.mark(dve.tensor_tensor(kbeg, v4(2), begN[:, :, bass.ds(h, 1)].broadcast_to([P, NT, P]), ALU.mult), f"kbeg{j}")
                    c_vec.mark(dve.tensor_tensor(kdN, v4(2), per_token(64).broadcast_to([P, NT, P]), ALU.mult), f"kd{j}")
                    dve.wait_ge(*c_pe(f"vN{j}", p))
                    for q in range(2):
                        i = dve.tensor_tensor(vb[:, 2 * q:2 * q + 2, :], psum[3 + 4 * q][:, :].rearrange("p (t c) -> p t c", t=2),
                                              stN[:, 2 * q:2 * q + 2, bass.ds(h + 32, 1)].broadcast_to([P, 2, A_DV]), ALU.mult)
                    c_vec.mark(i, f"vb{j}")
                    eye = ident.unsqueeze(1).broadcast_to([P, NT, P])
                    dve.wait_ge(*c_pool(f"NM0_{j}", p))
                    if not noprev:
                        dve.wait_ge(*prev(c_pe, "V3_"))
                    c_vec.mark(dve.tensor_tensor(Y, NM[:, 0, :].rearrange("p (t c) -> p t c", t=NT), eye, ALU.add), f"Y0_{j}")
                    dve.wait_ge(*c_pe(f"P0_{j}", p))
                    if not noprev:
                        dve.wait_ge(*(oa_st[0]("o", p) if j else oa_st[1]("o", p - 1)))
                    c_vec.mark(dve.tensor_tensor(X, v4(6), eye, ALU.add), f"X0_{j}")
                    fill(6)
                    for s in range(1, LEVELS):
                        if s < LEVELS - 1:
                            dve.wait_ge(*c_pe(f"X{s}_{j}", p))
                            dve.wait_ge(*c_vec(f"X{s - 1}_{j}", p))
                            c_vec.mark(dve.tensor_tensor(X, v4(5), X, ALU.add), f"X{s}_{j}")
                        dve.wait_ge(*c_pe(f"Y{s}_{j}", p))
                        dve.wait_ge(*c_vec(f"Y{s - 1}_{j}", p))
                        c_vec.mark(dve.tensor_tensor(Y, v4(6), Y, ALU.add), f"Y{s}_{j}")
                        fill(4)
                    fill(1)
                    for t in range(NT - 1):
                        dve.wait_ge(*c_pe(f"S{t}_{j}", p))
                        if t == 0:
                            if not noprev:
                                dve.wait_ge(*prev(c_pe, "O3"))
                            i = dve.tensor_copy(S, psum[3][:, 0:A_DV])
                        else:
                            dve.wait_ge(*c_pe(f"O{t}{j}", p))
                            dve.wait_ge(*c_vec(f"S{t - 1}_{j}", p))
                            i = dve.scalar_tensor_tensor(S, S, bc[:, j, 2, (t + 1) * P - 1:(t + 1) * P], psum[3][:, 0:A_DV],
                                                         ALU.mult, ALU.add)
                        c_vec.mark(i, f"S{t}_{j}" if t < NT - 2 else f"S{t}_{j}")
                        fill(2)
                    fill(2)
                    dve.wait_ge(*c_act(f"orms{j}", p))
                    c_vec.link(dve, dve.reciprocal(stat[:, 4:8], stat[:, 4:8]), p)
                    for t in range(NT):
                        i = dve.scalar_tensor_tensor(oN[:, t, :], psum[4 + t // 2][:, t % 2 * A_DV:(t % 2 + 1) * A_DV],
                                                     stat[:, 4 + t:5 + t], zs[:, t, j * A_DV:(j + 1) * A_DV], ALU.mult, ALU.mult)
                    c_vec.mark(i, f"gate{j}")
                    for d in range(2):
                        dve.wait_ge(*c_pe(f"oT{d}{j}", p))
                        c_vec.mark(dve.tensor_scalar(o_st[:, d:d + 1, :], psum[6 + d][:, :].unsqueeze(1),
                                                     cols[:, V_NA + d:V_NA + d + 1], None, ALU.mult), f"oT{d}{j}")

                    fill(2)
                fill(99)

            def with_splits(p):
                ga_vec.start()
                for n in range(4):
                    split_a(p, n)
                at = [0]

                def fill(n):
                    for m in range(at[0], min(at[0] + n, 96)):
                        if m % KB == KB - 1 and m // KB < 8:
                            split_a(p, m // KB + 4)
                    at[0] += n
                chain_a(p - 1, fill)

            with_splits(1)
            with dve.Fori(2, PAIRS) as p:
                with_splits(p)
            chain_a(PAIRS - 1, lambda n: None)

            def merge(x, c):
                m_vec[x].start()

                def split(n):
                    dve.wait_ge(*m_act[x](f"w{n}", c))
                    slot, q = (0, n) if n < 4 else (1 + n % 2, (n - 4) // 2)
                    w = ring[slot][:, :, q * P:(q + 1) * P]
                    low(dve, m_vec[x], w, w, h_col[n % 4], f"w{n}")
                for n in range(8):
                    split(n)
                if only(c) and c == 0:
                    for k in range(8):
                        dve.wait_ge(*ot_act[x](f"o{k}"))
                        o = oT[:, 2 * k:2 * k + 2, :]
                        low(dve, ot_vec[x], o, o, oT_hi[:, 2 * k:2 * k + 2, :], f"o{k}")
                for b in range(4):
                    if b < 2:
                        split(8 + 2 * b)
                        split(9 + 2 * b)
                    dve.wait_ge(*m_pe[x](f"y{b}", c))
                    dve.wait_ge(*m_act[x](f"sg{b}", c))
                    to = mixT[:, bass.ds(c * 4 + b, 1), :].rearrange("p a n -> p (a n)")
                    if x == 0:
                        m_vec[x].mark(dve.tensor_tensor(to, psum[2 + b][:, :], sg[:, b, :], ALU.mult), f"mix{b}")
                    else:
                        m_vec[x].link(dve, dve.tensor_tensor(ytmp[:, b % 2, :], psum[2 + b][:, :], sg[:, b, :], ALU.mult), c)
                        m_vec[x].mark(dve.tensor_tensor(to, to, ytmp[:, b % 2, :], ALU.add), f"mix{b}")
            merge(0, 0)
            with dve.Fori(1, 2) as c:
                merge(0, c)

            def rope_q(h):
                dve.wait_ge(*bg_act("e1", h))
                if only(h) and h == 0:
                    dve.wait_ge(*b_tab("decay"))
                else:
                    dve.wait_ge(*b_pe("S3", h - 1))
                for o, (c0, c1, op) in enumerate(((cosT, sinT, ALU.subtract), (sinT, cosT, ALU.add))):
                    dve.tensor_tensor(rt[:, 0, :], qkr[:, 0, :], c0, ALU.mult)
                    b_rope.link(dve, dve.tensor_tensor(rt[:, 1, :], qkr[:, 1, :], c1, ALU.mult), h)
                    i = dve.tensor_tensor(qkT[:, o, :], rt[:, 0, :], rt[:, 1, :], op)
                    if o == 0:
                        b_rope.link(dve, i, h)
                b_rope.mark(i, "ropeq")

            def split_b(h, n):
                dve.wait_ge(*bg_act(f"w{n}", h))
                w, hi = (ring[0][:, :, n * P:(n + 1) * P], h_col[n]) if n < 4 else (ring[n // 4][:, n % 4 * 2:n % 4 * 2 + 2, :], h_row[n % 4])
                low(dve, bs_vec, w, w, hi, f"w{n}")

            def decay_b(h):
                b_vec.start()
                for m in range(NT):
                    dve.wait_ge(*b_pe(f"S{m}", h))
                    b_vec.mark(dve.tensor_tensor(PT[:, m, m * P:], psum[2 + m][:, m * P:],
                                                 dmask[:, bass.ds(h, 1), 0:512 - m * P].rearrange("p a n -> p (a n)"), ALU.mult), f"PT{m}")

            def gate_b(h):
                dve.wait_ge(*b_act("orms", h))
                b_vec.link(dve, dve.reciprocal(stat[:, 4:8], stat[:, 4:8]), h)
                dve.wait_ge(*bg_act("e11", h))
                for t in range(NT):
                    i = dve.scalar_tensor_tensor(bo[:, t, :], psum[(6, 7, 2, 3)[t]][:, :], stat[:, 4 + t:5 + t], bg[:, t, :], ALU.mult, ALU.mult)
                b_vec.mark(i, "gate")

            def out_b(h):
                if not only(h):
                    dve.wait_ge(*ob_st_s("o", h - 1))
                for d in range(4):
                    dve.wait_ge(*b_pe(f"oT{d}", h))
                    b_vec.mark(dve.tensor_scalar(ob_st[:, d, :], psum[4 + d][:, :],
                                                 cols[:, bass.ds(h * 4 + V_NB + d, 1)], None, ALU.mult), f"oT{d}")

            def step_b(h):
                bs_vec.start()
                b_rope.start()
                for n in range(4):
                    split_b(h, n)
                if not only(h):
                    decay_b(h - 1)
                for n in range(4, 8):
                    split_b(h, n)
                rope_q(h)
                if not only(h):
                    gate_b(h - 1)
                for n in range(8, 12):
                    split_b(h, n)
                if not only(h):
                    out_b(h - 1)
            step_b(0)
            with dve.Fori(1, B_HEADS) as h:
                step_b(h)
            decay_b(B_HEADS - 1)
            gate_b(B_HEADS - 1)
            out_b(B_HEADS - 1)
            merge(1, 0)
            with dve.Fori(1, 2) as c:
                merge(1, c)

            def post_norm(act_s, vec_s, bank, rowsig, prenorm, pt_tmp, hN):
                for t in range(NT):
                    dve.wait_ge(*act_s(f"sq{t}1"))
                    vec_s.mark(dve.tensor_tensor(stat[:, 2 * t:2 * t + 1], stat[:, 2 * t:2 * t + 1], stat[:, 2 * t + 1:2 * t + 2], ALU.add), f"ss{t}")
                    dve.wait_ge(*act_s(f"rms{t}"))
                    vec_s.link(dve, dve.reciprocal(stat[:, 12:13], stat[:, 12:13]))
                    if t == 0:
                        dve.wait_ge(*rowsig)
                    for c in range(2):
                        i = dve.scalar_tensor_tensor(pt_tmp[:, t, c * 512:(c + 1) * 512], psum[bank(t, c)][:, :], stat[:, 12:13],
                                                     row[:, c * 512:(c + 1) * 512], ALU.mult, ALU.mult)
                    vec_s.link(dve, i)
                    vec_s.mark(dve.tensor_tensor(XR[:, t, :], XR[:, t, :], pt_tmp[:, t, :], ALU.add), f"x{t}")
                    if prenorm:
                        dve.wait_ge(*act_s(f"hrms{t}"))
                        vec_s.link(dve, dve.reciprocal(stat[:, 14:15], stat[:, 14:15]))
                        vec_s.mark(dve.tensor_scalar(hN[:, t, :], XR[:, t, :], stat[:, 14:15], None, ALU.mult), f"hn{t}")
            for n in range(8):
                if n % 2 == 0:
                    dve.wait_ge(*o_act(f"mix{n // 2}"))
                    low(dve, o_vec, mixT[:, n:n + 2, :], mixT[:, n:n + 2, :], mix_hi[:, n:n + 2, :], f"mix{n // 2}")
                dve.wait_ge(*o_act(f"w{n}"))
                w = ring[n % 2][:, n // 2 * 2:n // 2 * 2 + 2, :]
                low(dve, o_vec, w, w, h_row[n % 4], f"w{n}")
            dve.wait_ge(*x_back("x"))
            post_norm(o_act, o_vec, lambda t, c: 2 * t + c, o_row("row"), True, o_tmp, o_hN)

            def turned(pe_s, vec_s, bank, scale):
                for t in range(NT):
                    for q in range(2):
                        dve.wait_ge(*pe_s(f"T{t}{q}"))
                        to = AT[:, 4 * q:4 * q + 4, t * P:(t + 1) * P]
                        fr = psum[bank(t, q)][:, :].rearrange("p (b c) -> p b c", b=4)
                        if scale is None:
                            i = dve.tensor_copy(to, fr)
                        else:
                            i = dve.tensor_tensor(to, fr, cols[:, scale + 4 * q:scale + 4 * q + 4].unsqueeze(2).broadcast_to([P, 4, P]), ALU.mult)
                        vec_s.mark(i, f"AT{t}{q}")
            turned(o_pe, o_vec, lambda t, q: 2 * t + q, V_MLPPRE)

            for q in range(4):
                dve.wait_ge(*o_act(f"ATh{q}"))
                a = AT[:, 2 * q:2 * q + 2, :]
                low(dve, o_vec, a, a, at_hi[:, 2 * q:2 * q + 2, :], f"ATl{q}")

            def mlp_up(i):
                u_vec.start()
                for g in range(-3, 16):
                    n = g + 3
                    if n < 16:
                        dve.wait_ge(*u_act(f"w{n}", i))
                        w = ring[n // 4 % 2][:, :, n % 4 * P:(n % 4 + 1) * P]
                        low(dve, u_vec, w, w, h_col[n % 4], f"w{n}")
                    if g < 0:
                        continue
                    dve.wait_ge(*u_pe(f"g{g}", i))
                    u_vec.mark(dve.tensor_scalar(ffT[:, bass.ds(i * 16 + g, 1), :].rearrange("p a n -> p (a n)"), psum[g % 4][:, :], 0.0, None, ALU.max), f"relu{g}")
            mlp_up(0)
            with dve.Fori(1, 2) as i:
                mlp_up(i)

            def mlp_down(c):
                dn_vec.start()
                for n in range(16):
                    dve.wait_ge(*dn_act(f"w{n}", c))
                    w = ring[n // 4 % 2][:, n % 4 * 2:n % 4 * 2 + 2, :]
                    low(dve, dn_vec, w, w, h_row[n % 4], f"w{n}")
                    dve.wait_ge(*dn_act(f"ff{n}", c))
                    low(dve, dn_vec, ff_lo[:, n % 4, :, :], ffT[:, 2 * n:2 * n + 2, :], ff_hi[:, n % 4, :, :], f"ff{n}")
            mlp_down(0)
            with dve.Fori(1, 2) as c:
                mlp_down(c)
            post_norm(d_act, d_vec, lambda t, c: 4 * c + t, f_row("row"), False, pt_tmp, hN)
            turned(t2_pe, t2_vec, lambda t, q: 4 * q + t, None)
            for q in range(4):
                dve.wait_ge(*p_pe(f"memT{q}"))
                p_vec.mark(dve.tensor_copy(memT[:, 2 * q:2 * q + 2, :], psum[q][:, :].rearrange("p (k n) -> p k n", k=2)), f"memT{q}")

            def attend_body(kind, b):
                pe_s, act_s, vec_s = at_pe[kind], at_act[kind], at_vec[kind]
                vec_s.start()
                units, nk = (4, 256) if kind == "m" else (8, 256 if kind == "n" else 512)
                for n in range(units + 1):
                    if n < units:
                        e, u = n // 4, n % 4
                        dve.wait_ge(*pe_s(f"S{n}", b))
                        src = psum[n % 3][:, 0:nk]
                        if kind == "n":
                            if n >= 2:
                                dve.wait_ge(*act_s(f"ex{n - 2}", b))
                            if n == 0:
                                dve.wait_ge(*at_pool["n"]("bias", b))
                            vec_s.mark(dve.tensor_tensor(sc[:, n % 2, 0:nk], src, bias[:, e, (0, 1, 1, 2)[u], :], ALU.add), f"s{n}")
                            dve.wait_ge(*vec_s(f"s{n}", b))
                            src = sc[:, n % 2, 0:nk]
                        vec_s.mark(dve.tensor_reduce(nmax[:, n:n + 1], src, AX, ALU.max, negate=True), f"max{n}")
                    if n:
                        m = n - 1
                        dve.wait_ge(*act_s(f"ex{m}", b))
                        vec_s.link(dve, dve.reciprocal(pinv[:, m:m + 1], psums[:, m:m + 1]), b)
                        vec_s.mark(dve.tensor_scalar(pr[:, m % 3, 0:nk], pr[:, m % 3, 0:nk], pinv[:, m:m + 1], None, ALU.mult), f"n{m}")
                dve.wait_ge(*pe_s(f"AV{units - 1}", b))
                off = {"n": 0, "g": 4, "m": 8}[kind]
                to = yT[:, bass.ds(b + off, 1), :].rearrange("p a n -> p (a n)")
                if kind == "n":
                    for cb in range(4):
                        i = dve.tensor_copy(to.rearrange("p (r c) -> p r c", r=8)[:, :, cb * 16:cb * 16 + 16],
                                            psum[5][:, cb * P:(cb + 1) * P].rearrange("p (r q) -> p r q", r=8))
                else:
                    i = dve.tensor_copy(to, psum[5][:, :])
                vec_s.mark(i, "y")

            def attend(kind):
                attend_body(kind, 0)
                with dve.Fori(1, 4) as b:
                    attend_body(kind, b)

            attend("n")
            for t in range(NT):
                dve.wait_ge(*r_pool(f"sq{t}"))
                i = dve.tensor_reduce(gst[:, t, :], ro[:, t, :].rearrange("p (h d) -> p h d", h=10), AX, ALU.add)
            r_vec.mark(i, "ss")
            attend("m")
            dve.wait_ge(*r_act("root"))
            r_vec.link(dve, dve.reciprocal(gst, gst))
            for t in range(NT):
                x = qkN[:, t, 0:640].rearrange("p (h d) -> p h d", h=10)
                r_vec.mark(dve.tensor_tensor(x, x, gst[:, t, :].unsqueeze(2).broadcast_to([P, 10, 64]), ALU.mult), f"scaled{t}")
            for t in range(NT):
                dve.wait_ge(*r_pool(f"gain{t}"))
                x = qkN[:, t, 0:640].rearrange("p (h d two) -> p h d two", h=10, two=2)
                o = ro[:, t, :].rearrange("p (h d two) -> p h d two", h=10, two=2)
                cb, sb_ = [v[:, t:t + 1, :].broadcast_to([P, 10, 32]) for v in (cosN, sinN)]
                a3, b3 = [v.rearrange("p (h d) -> p h d", h=10) for v in (ra, rb)]
                for out_at, (c0, c1, op) in enumerate(((cb, sb_, ALU.subtract), (sb_, cb, ALU.add))):
                    dve.tensor_tensor(a3, x[:, :, :, 0], c0, ALU.mult)
                    r_vec.link(dve, dve.tensor_tensor(b3, x[:, :, :, 1], c1, ALU.mult))
                    i = dve.tensor_tensor(o[:, :, :, out_at], a3, b3, op)
                    if out_at == 0 or t < 3:
                        r_vec.link(dve, i)
            r_vec.mark(i, "rope3")
            attend("g")

            def merge2(c):
                mg_vec.start()
                for g in range(3):
                    for b in range(4):
                        dve.wait_ge(*mg_pe(f"br{g}{b}", c))
                        dve.wait_ge(*mg_act(f"sg{g}{b}", c))
                        to = mgT[:, bass.ds(c * 4 + b, 1), :].rearrange("p a n -> p (a n)")
                        if g == 0:
                            i = dve.tensor_tensor(to, psum[4 + b][:, :], sg2[:, b, :], ALU.mult)
                        else:
                            mg_vec.link(dve, dve.tensor_tensor(mtmp[:, b % 2, :], psum[4 + b][:, :], sg2[:, b, :], ALU.mult), c)
                            i = dve.tensor_tensor(to, to, mtmp[:, b % 2, :], ALU.add)
                        mg_vec.mark(i, f"m{g}{b}")
            merge2(0)
            with dve.Fori(1, 2) as c:
                merge2(c)

            def normed(t, act_s, vec_s, src):
                st6 = gst.rearrange("p t h -> p (t h)")
                for c in range(2):
                    i = dve.bn_stats(st6[:, 6 * c:6 * c + 6], src[:, c * 512:(c + 1) * 512])
                vec_s.link(dve, i)
                vec_s.mark(dve.bn_aggr(stat[:, 0:2], st6[:, 0:12]), f"var{t}")
                dve.wait_ge(*act_s(f"root{t}"))
                vec_s.link(dve, dve.reciprocal(stat[:, 3:4], stat[:, 2:3]))
                vec_s.mark(dve.tensor_scalar(src, src, stat[:, 0:1], stat[:, 3:4], ALU.subtract, ALU.mult), f"n{t}")
            for t in range(NT):
                for c in range(2):
                    dve.wait_ge(*l_pe(f"m{t}{c}"))
                    i = dve.scalar_tensor_tensor(v2[:, t, c * 512:(c + 1) * 512], XR[:, t, c * 512:(c + 1) * 512], ALPHA, psum[2 * t + c][:, :],
                                                 ALU.mult, ALU.add)
                l_vec.link(dve, i)
                normed(t, l_act, l_vec, v2[:, t, :])
            turned(q_pe, q_vec, lambda t, q: 2 * t + q, None)
            for t in range(NT):
                i = dve.tensor_scalar(acc[:, t, :], XR[:, t, :], ALPHA, None, ALU.mult)
            q_vec.link(dve, dve.memset(affT[0:NE, :], 1.0))
            dve.wait_ge(*q_pe("logits"))
            lg = psum[0][:, 0:NT * NE].rearrange("p (t e) -> p t e", t=NT)
            q_vec.link(dve, dve.tensor_reduce(lmax, lg, AX, ALU.max))
            q_vec.mark(dve.tensor_tensor(affN, lg, lmax.unsqueeze(2).broadcast_to([P, NT, NE]), ALU.subtract), "less")
            dve.wait_ge(*q_act("exp"))
            q_vec.link(dve, dve.tensor_reduce(lsum, affN, AX, ALU.add))
            q_vec.link(dve, dve.reciprocal(lsum, lsum))
            q_vec.mark(dve.tensor_tensor(affN, affN, lsum.unsqueeze(2).broadcast_to([P, NT, NE]), ALU.mult), "aff")
            dve.wait_ge(*q_pe("affT"))
            q_vec.link(dve, dve.tensor_copy(wrk[0:NE, :], psum[1][0:NE, :]))
            for r in range(EC // 8):
                q_vec.link(dve, dve.max(m8[0:NE, :], wrk[0:NE, :]))
                q_vec.link(dve, dve.match_replace(wrk[0:NE, :], m8[0:NE, :], wrk[0:NE, :], -1.0))
            q_vec.link(dve, dve.tensor_scalar(wrk[0:NE, :], wrk[0:NE, :], 0.0, None, ALU.is_lt))
            q_vec.link(dve, dve.tensor_tensor_scan(cum[0:NE, :], affT[0:NE, :], wrk[0:NE, :], 0.0, ALU.mult, ALU.add))
            q_vec.mark(dve.tensor_tensor(cum[0:NE, :], cum[0:NE, :], wrk[0:NE, :], ALU.mult), "pos")
            dve.wait_ge(*q_pe("posN"))
            dve.wait_ge(*q_ld("wr"))
            q_vec.link(dve, dve.tensor_copy(posN, psum[2][:, 0:NT * NE].rearrange("p (t e) -> p t e", t=NT)))

            def experts(p):
                e_vec.start()
                four = [P, NT, 2, EC]
                v4 = lambda x: x.rearrange("p t (e j) -> p t e j", e=2)
                of = lambda x: x[:, :, bass.ds(p * 2, 2)].unsqueeze(3).broadcast_to(four)
                if not only(p):
                    dve.wait_ge(*e_pe("SGT", p - 1))
                e_vec.mark(dve.tensor_tensor(v4(SP), iota.unsqueeze(1).unsqueeze(1).broadcast_to(four), of(posN), ALU.is_equal), "SP")
                dve.wait_ge(*e_vec("SP", p))
                e_vec.mark(dve.tensor_tensor(v4(SG), v4(SP), of(affN), ALU.mult), "SG")
                dve.wait_ge(*e_pe("SGT", p))
                if not only(p):
                    dve.wait_ge(*e_pe("y7", p - 1))
                e_vec.mark(dve.tensor_copy(SGT, psum[2][:, :]), "SGT")
                for f in range(2):
                    dve.wait_ge(*e_pe(f"group{2 * f + 1}", p))
                    dve.wait_ge(*e_act(f"silu{f}", p))
                    e_vec.mark(dve.tensor_tensor(ga[:, f, :], psum[4 + 2 * f][:, :], ga[:, f, :], ALU.mult), f"ga{f}")
                for m in range(8):
                    t, n = m // 2, m % 2
                    dve.wait_ge(*e_pe(f"y{m}", p))
                    a = acc[:, t, n * 512:(n + 1) * 512]
                    e_vec.mark(dve.tensor_tensor(a, psum[(0, 1, 2, 6)[m % 4]][:, :], a, ALU.add), f"acc{m}")
            experts(0)
            with dve.Fori(1, NE // 2) as p:
                experts(p)
            dve.wait_ge(*e_vec("acc7", NE // 2 - 1))
            for t in range(NT):
                normed(t, f_act, f_vec, acc[:, t, :])


def constants():
    i = np.arange(P)
    ident = np.eye(P)
    ones = np.ones((P, P))
    incl = (i[:, None] <= i[None, :]).astype(float)
    lv = []
    for s in range(LEVELS):
        w = 1 << s
        same = i[:, None] // (2 * w) == i[None, :] // (2 * w)
        lv.append(-(same & (i[:, None] // w % 2 == 0) & (i[None, :] // w % 2 == 1)).astype(float))
    return np.concatenate([ident, ones, incl] + lv, axis=1).astype(np.float32)


def retention_tables():
    inv = 10000.0 ** (-np.arange(0, B_DK, 2, dtype=np.float32) / B_DK)
    ang = np.arange(SEQ, dtype=np.float32)[None, :] * inv.astype(np.float32)[:, None]
    lg = np.log1p(-np.exp2(-5.0 - np.arange(B_HEADS)))
    m, c = np.arange(P)[:, None], np.arange(SEQ)[None, :]
    keep = c // 64 >= m // 64
    decay = [np.where(keep, np.exp(g * np.abs(c - m)), 0.0) * B_DK ** -0.5 for g in lg]
    return (np.concatenate([np.cos(ang), np.sin(ang)], axis=1).astype(np.float32),
            np.concatenate(decay, axis=1).astype(np.float32))


def rope_rows():
    t = np.arange(SEQ)
    inv = (10000.0 ** (-np.arange(0, 32, 2, dtype=np.float32) / 32)).astype(np.float32)
    ang = np.concatenate([(t // 64).astype(np.float32)[:, None] * inv, (t % 64).astype(np.float32)[:, None] * inv], axis=-1)
    by = lambda v: v.reshape(NT, P, 32).transpose(1, 0, 2).reshape(P, NT * 32)
    return np.concatenate([by(np.cos(ang)), by(np.sin(ang))], axis=1).astype(np.float32)


def neighbourhood(rpb):
    q, k = np.arange(P), np.arange(256)
    r, qq, kr, kk = q[:, None] // 16, q[:, None] % 16, k[None, :] // 32, k[None, :] % 32
    padded = np.pad(rpb, ((0, 0), (0, 0), (16, 17)))
    bias, mask = [], []
    for o, start in ((0, np.maximum(qq - 8, 0)), (-8, qq), (-16, np.minimum(qq + 8, 16))):
        bias.append(padded[:, kr - r + 7, kk - qq + 15 + o + 16])
        mask.append(np.where((kk >= start) & (kk < start + 16), 0.0, -1e30))
    bias = np.stack(bias, axis=1)
    bias = bias.reshape(4, 2, 3, P, 256).transpose(0, 3, 1, 2, 4).reshape(4, P, 1536)
    return np.ascontiguousarray(bias), np.concatenate(mask, axis=1).astype(np.float32)


def layout(inputs):
    g = {k: np.asarray(v) for k, v in inputs.items()}
    one = {k: np.ascontiguousarray(v[0]) for k, v in g.items()}

    def by_partition(v):
        return v.reshape(-1, P).T

    pad = lambda v: np.pad(v.reshape(-1, 1), ((0, P - v.size), (0, 0)))
    conv = one["conv_a"].reshape(4, 32, P).transpose(2, 1, 0).reshape(P, 128)
    cols = np.concatenate([
        by_partition(one["norm_mix_pre"]), by_partition(one["norm_mlp_pre"]), conv, by_partition(one["norm_a"]),
        by_partition(one["norm_b"]), by_partition(one["b_gate_2"]), pad(one["a_log"]), pad(one["dt_bias"]), np.repeat(np.eye(2, dtype=np.float32), 64, axis=0)], axis=1)
    t = {"cols": np.ascontiguousarray(cols), "consts": constants()}
    t["rope_b"], t["decay_b"] = retention_tables()
    for k in ("x", "w_in", "w_br_a", "w_br_b", "w_out", "w_up", "w_down"):
        t[k] = one[k]
    t["rope_g"] = rope_rows()
    t["na_bias"], t["na_mask"] = neighbourhood(one["na_rpb_2"])
    t["iota"] = np.broadcast_to(np.arange(1, EC + 1, dtype=np.float32), (P, EC)).copy()
    t["gains"] = np.concatenate([one["gqa_q_gain_2"], one["gqa_k_gain_2"]]).reshape(1, 128)
    t["mem_2"] = g["mem_2"][0]
    t["w_branch_2"] = one["w_branch_2"].reshape(3 * 512, DM)
    for k in ("w_in_2", "w_mem_kv_2", "w_out_2", "w_router_2", "w_gate_up_2", "w_down_2"):
        t[k] = one[k]
    for k in ("norm_mix_post", "norm_mlp_post", "ln1_g_2", "ln1_b_2", "ln2_g_2", "ln2_b_2"):
        t[k] = one[k].reshape(1, DM)
    return t


def kernel(**inputs):
    import concourse.bacc as bacc
    from concourse.bass_utils import run_bass_kernel_spmd

    t = layout(inputs)
    for _ in range(2):
        nc = bacc.Bacc("TRN2", target_bir_lowering=False, num_devices=1)
        aps = {k: nc.dram_tensor(k + "_in", v.shape, F32, kind="ExternalInput").ap() for k, v in t.items()}
        out = nc.dram_tensor("out", (SEQ, DM), F32, kind="ExternalOutput").ap()
        build(nc, aps, out)
    r = run_bass_kernel_spmd(nc, [{k + "_in": v for k, v in t.items()}], core_ids=[0])
    return r.results[0]["out"].reshape(1, SEQ, DM)
```

```python
import concourse.bass as bass
from concourse import mybir
from contextlib import ExitStack
import numpy as np

F32, F32R = mybir.dt.float32, mybir.dt.float32r
ALU = mybir.AluOpType
ACT = mybir.ActivationFunctionType
AX = mybir.AxisListType.X

SEQ, DM, P = 512, 1024, 128
NT = SEQ // P
KB = DM // P
EPS = 1e-6
A_HEADS, A_DK, A_DV = 8, 128, 256
B_HEADS, B_DK, B_DV = 4, 256, 512
A_QK, A_V, B_QK, B_V = 1024, 2048, 1024, 2048
C_QA, C_KA, C_VA, C_ZA = 0, 1024, 2048, 4096
C_BETA = 6144
C_QB = 6160
C_KB, C_VB, C_GB = C_QB + 1024, C_QB + 2048, C_QB + 4096
C_GA = C_GB + 2048
C_GBT = C_GA + 1024
ALPHA = 2 ** 0.25
NE, EC = 16, 64
LEVELS = 7
PAIRS = A_HEADS // 2
TURNS = (("ring", 4 * 4096), ("activations_T", 4096), ("work", 26500))
PAUSE = 8
FILL = dict(conv=3, norm=8, scores=7, tokens=2, inverse=1, level=(1, 1), w=1, state=(1, 1), out=5)

V_MIXPRE, V_MLPPRE, V_CONV, V_NA, V_NB, V_BG, V_ALOG, V_DT = 0, 8, 16, 144, 146, 162, 186, 187
V_HALF, V_N = 188, 190


class Sig:

    known = {}

    def __init__(self, nc, ctx, name, step=1):
        self.sem, self.name, self.step = ctx.enter_context(nc.semaphore(name)), name, step
        self.seen, self.was, self.k = {}, Sig.known.get(name, {}), 0

    def start(self):
        self.k = 0

    def mark(self, ins, what):
        self.k += 1
        assert self.seen.setdefault(what, self.k) == self.k, (self.name, what)
        Sig.known[self.name] = self.seen
        ins.then_inc(self.sem, self.step)

    def __call__(self, what, i=0):
        per = len(self.was) or 1
        if self.was and what not in self.was:
            raise KeyError((self.name, what))
        return self.sem, (i * per + self.was.get(what, 1)) * self.step

    def link(self, eng, ins, i=0):
        what = f"link{self.k}"
        self.mark(ins, what)
        eng.wait_ge(*self(what, i))


TWINS = {}


def R(x):
    return bass.AP(tensor=TWINS[x.tensor.name], offset=x.offset, ap=[list(a) for a in x.ap])


def high(act, s, dst, src, what):
    s.mark(act.activation(R(dst), src, ACT.Copy), what)


def low(dve, s, dst, src, hi, what):
    s.mark(dve.tensor_tensor(R(dst), src, R(hi).bitcast(F32), ALU.subtract), what)


def product(pe, out, lhs, rhs, start, stop):
    (lh, ll), (rh, rl) = lhs, rhs
    pe.matmul(out, R(ll), R(rh), start=start, stop=False)
    pe.matmul(out, R(lh), R(rh), start=False, stop=False)
    return pe.matmul(out, R(lh), R(rl), start=False, stop=stop)


def build(nc, T, out):
    with ExitStack() as ctx:
        def sb(name, words):
            return ctx.enter_context(nc.sbuf_tensor(name, [P, words], F32))

        def sig(name, step=1):
            return Sig(nc, ctx, name, step)

        xr_t = sb("residual", 4096)
        const = sb("const", 2048)
        with ExitStack() as over:
            plain = [over.enter_context(nc.sbuf_tensor(n, [P, w], F32)) for n, w in TURNS]
        for n, w in TURNS:
            TWINS[n] = ctx.enter_context(nc.sbuf_tensor(n + "_split", [P, w], F32R))
        ring_t, at_t, work = plain
        ps_all = ctx.enter_context(nc.psum_tensor("banks", [P, 8, 512], F32))
        psum = [ps_all[:, b, :] for b in range(8)]

        ring = [ring_t[:, s * 4096:(s + 1) * 4096].rearrange("p (k n) -> p k n", k=8) for s in range(4)]
        hq = [ring_t[:, 3 * 4096 + n * 1024:3 * 4096 + (n + 1) * 1024] for n in range(4)]
        h_col = [h.rearrange("p (k n) -> p k n", k=8) for h in hq]
        h_row = [h.rearrange("p (k n) -> p k n", k=2) for h in hq]
        XR = xr_t[:, :].rearrange("p (t d) -> p t d", t=NT)
        AT = at_t[:, :].rearrange("p (k n) -> p k n", k=KB)

        def carve(t, start, shapes):
            got, at = [], start
            for s in shapes:
                n = int(np.prod(s))
                v = t[:, at:at + n]
                if len(s) == 2:
                    v = v.rearrange("p (a b) -> p a b", a=s[0])
                if len(s) == 3:
                    v = v.rearrange("p (a b c) -> p a b c", a=s[0], b=s[1])
                got.append(v)
                at += n
            return got, at

        (ident, ones, m_incl, m_lvl, cols, stat, eps, one), at_c = carve(
            const, 0, [(P,), (P,), (P,), (LEVELS, P), (192,), (16,), (1,), (1,)])

        (at_hi,), _ = carve(work, 0, [(KB, 512)])
        a, at_w = carve(work, 8192, [(512,), (NT, P), (NT, 8), (8, 516), (NT, 512), (2, 3, 512), (512,), (512,),
                                     (512,), (512,), (1024,), (NT, P)])
        ST, stN, begN, pre, zs, bc, kT, qT, kbT, qeT, dl, ATT = a
        o_st = work[:, at_w:at_w + 1024].rearrange("p (d n) -> p d n", d=2)
        a, at_w = carve(work, at_w, [(NT, P), (NT, P), (NT, P), (1024,), (NT, A_DV), (A_DV,), (A_DV,)])
        X, PP, Y, kk, vb, S, vnew = a
        assert at_w <= 26500, at_w
        (zraw, NM, nwT, wsm), at_z = carve(work, 4096, [(NT, 512), (2, 512), (512,), (KB, 40)])
        assert at_z <= 8192
        D = dl[:, 0:512].rearrange("p (t c) -> p t c", t=NT)
        LT = dl[:, 512:1024].rearrange("p (t c) -> p t c", t=NT)
        oN = dl.rearrange("p (t c) -> p t c", t=NT)
        kbeg = kk[:, 0:512].rearrange("p (t c) -> p t c", t=NT)
        kdN = kk[:, 512:1024].rearrange("p (t c) -> p t c", t=NT)
        sq = kk.rearrange("p (a c) -> p a c", a=2)
        oj = kk.rearrange("p (t c) -> p t c", t=NT)
        rinv = vb.rearrange("p t d -> p (t d)").rearrange("p (a c) -> p a c", a=2)
        u8 = work[:, 4096 + 2048:4096 + 2048 + 1536].rearrange("p (a n) -> p a n", a=3)
        y = xr_t[:, :].rearrange("p (b n) -> p b n", b=8)

        qkr, bv, bg = pre[:, 0:4, 0:512], pre[:, 4:8, 0:512], zraw
        at_pre = 8192 + 2 * 512 + 32 + 8 * 516
        (qkT, PT, _, rope_tab, bo, _), at_b = carve(work, at_pre, [(4, 512), (NT, 512), (1024,), (2, 512), (NT, 512), (2560,)])
        (rk, rt), at_b = carve(work, at_b, [(2, 512), (2, 512)])
        dmask = xr_t[:, 2048:4096].rearrange("p (h c) -> p h c", h=B_HEADS)
        cosT, sinT = rope_tab[:, 0, :], rope_tab[:, 1, :]
        (mixT,), _ = carve(work, 4096, [(KB, 512)])
        (oT, oT_hi, ytmp), at_o = carve(work, 8192, [(16, 512), (16, 512), (2, 512)])
        assert max(at_b, at_o) <= 26500
        ob_st = xr_t[:, 0:2048].rearrange("p (d n) -> p d n", d=4)
        sg = xr_t[:, 2048:4096].rearrange("p (b n) -> p b n", b=4)
        oT_rows = [nc.dram_tensor(f"o_{x}", (16, P, SEQ), F32).ap() for x in "ab"]
        (pt_tmp, hN), _ = carve(work, 0, [(NT, DM), (NT, DM)])
        (o_tmp, o_hN), _ = carve(work, 12288, [(NT, DM), (NT, DM)])
        (ffT, row), at_m = carve(work, 8192, [(32, 512), (DM,)])
        (mix_hi,), _ = carve(work, 8192, [(KB, 512)])
        (ff_hi, ff_lo), _ = carve(work, 0, [(4, 2, 512), (4, 2, 512)])
        (mem_hi,), _ = carve(work, 4096, [(KB, 256)])
        (_, y_st, _, area, qmT, mkT, mvN, bias, bmask, qz, vst), at_2 = carve(work, 0, [
            (8 * 512,), (512,), (1536,), (11392,), (4, 512), (4, 256), (2, 512), (2, 3, 256), (3, 256), (2, 512), (8, P)])
        assert at_2 <= 26500, at_2
        A0 = 12 * 512
        (memN, memT), _ = carve(work, A0, [(2, DM), (KB, 256)])
        (qnT, knT, vnN, vband), _ = carve(work, A0, [(4, 512), (4, 512), (NT, 512), (8, 512)])
        (qkN, ro, kdup, ra, rb, qgT, kgT), at_g = carve(work, A0, [
            (NT, 768), (NT, 640), (NT, 2, P), (320,), (320,), (4, 512), (4, 512)])
        (mgT, sg2, mtmp, v2), _ = carve(work, A0, [(KB, 512), (4, 512), (2, 512), (NT, DM)])
        (yT, yT_hi), at_y = carve(work, A0 + 7168, [(12, 512), (12, 512)])
        assert at_g <= A0 + 11392 and at_y <= 26500
        mg_hi = at_hi
        vdup = bias.rearrange("p e v n -> p (e v n)")[:, 0:1024].rearrange("p (t n) -> p t n", t=NT)
        qst = qz[:, 0, :]
        (lnrow,), _ = carve(work, 4096, [(2, DM)])
        (lnrow2,), _ = carve(work, A0 + 11392, [(2, DM)])
        (sc, pr, pT, gain), _ = carve(ring_t, 2 * 4096, [(2, 512), (3, 512), (2, 512), (2, 64)])
        (cosN, sinN, nmax, psums, pinv, gst, eps5), at_c = carve(const, at_c, [
            (NT, 32), (NT, 32), (8,), (8,), (8,), (NT, 10), (1,)])
        assert at_c <= 2048
        (slot4, SP, SG, SGT, xst, ga, actT, ye, acc, affT, wrk, cum, posN, affN, m8, lmax, lsum), at_e = carve(work, 0, [
            (KB, 512), (NT, P), (NT, P), (512,), (KB, P), (2, 512), (KB, P), (2, 512), (NT, DM),
            (512,), (512,), (512,), (NT, NE), (NT, NE), (8,), (NT,), (NT,)])
        assert at_e <= A0 + 11392
        (slot5, iota, wr), _ = carve(work, A0 + 11392 + 2 * DM, [(KB, 512), (EC,), (KB, NE)])
        y_rows = nc.dram_tensor("y_rows", (12, P, SEQ), F32).ap()
        eslot = ring + [slot4, slot5]
        v_rows = nc.dram_tensor("v_rows", (SEQ, 512), F32).ap()

        scratch = nc.dram_tensor("stat_rows", (P, SEQ), F32).ap()
        W = T["w_in"].rearrange("(k p) n -> p k n", p=P)

        ld_const, ld_small = sig("loaded_const", 16), sig("loaded_small", 16)
        ld_x = sig("loaded_x", 16)
        z_pool = sig("pool_setup")
        n_act, n_vec, n_pe = sig("norm_act"), sig("norm_vec"), sig("norm_pe")
        s_pe, s_act, s_vec, s_dma = sig("stats_pe"), sig("stats_act"), sig("stats_vec"), sig("stats_stored", 16)
        a_w = [sig(f"a_weights{s}", 16) for s in range(3)]
        a_bc = [sig(f"a_rows{j}", 16) for j in range(2)]
        g_pe, g_act = sig("a_gemm_pe"), sig("a_gemm_act")
        c_pe, c_act, c_vec, c_pool = sig("a_chain_pe"), sig("a_chain_act"), sig("a_chain_vec"), sig("a_chain_pool")
        ga_vec, bs_vec = sig("a_split_vec"), sig("b_split_vec")
        oa_st, ob_st_s = [sig(f"a_stored{j}", 16) for j in range(2)], sig("b_stored", 16)
        ot_ld, ot_act, ot_vec = [[sig(f"merge{x}_o_{e}", n) for x in "ab"] for e, n in (("loaded", 16), ("act", 1), ("vec", 1))]
        b_rope = sig("b_rope_vec")
        done = sig("done", 16)
        m_w = [[sig(f"merge{x}_weights{q}", 16) for q in range(3)] for x in "ab"]
        m_pe, m_act, m_vec = [[sig(f"merge{x}_{e}") for x in "ab"] for e in ("pe", "act", "vec")]
        t2_pe, t2_vec = sig("x2_turn_pe"), sig("x2_turn_vec")
        mem_ld, n2_tab, bias_ld = sig("memory_loaded", 16), sig("attn_tables", 16), sig("bias_loaded", 16)
        w2 = [sig(f"proj_weights{q}", 16) for q in range(3)]
        p_pe, p_act, p_vec = sig("proj_pe"), sig("proj_act"), sig("proj_vec")
        y_sd, y_ld = [{k: sig(f"y{k}_{e}", 16) for k in "nmg"} for e in ("stored", "loaded")]
        v_st, v_ld = sig("v_stored", 16), sig("v_bands", 16)
        at_pe, at_act, at_vec, at_pool = [{k: sig(f"attn{k}_{e}") for k in "nmg"} for e in ("pe", "act", "vec", "pool")]
        r_pe, r_act, r_vec, r_pool = sig("rope_pe"), sig("rope_act"), sig("rope_vec"), sig("rope_pool")
        mg_w = [sig(f"merge2_weights{q}", 16) for q in range(4)]
        mg_pe, mg_act, mg_vec = sig("merge2_pe"), sig("merge2_act"), sig("merge2_vec")
        y_act, y_vec = sig("y_split_act"), sig("y_split_vec")
        l_w, l_row = [sig(f"out2_weights{q}", 16) for q in range(2)], sig("ln1_rows", 16)
        l_pe, l_act, l_vec = sig("ln1_pe"), sig("ln1_act"), sig("ln1_vec")
        q_ld, q_pe, q_act, q_vec = sig("route_loaded", 16), sig("route_pe"), sig("route_act"), sig("route_vec")
        e_w = [sig(f"expert_weights{q}", 16) for q in range(6)]
        e_pe, e_act, e_vec = sig("expert_pe"), sig("expert_act"), sig("expert_vec")
        f_rowl, f_act, f_vec = sig("ln2_rows", 16), sig("ln2_act"), sig("ln2_vec")
        b_w = [sig(f"b_weights{q}", 16) for q in range(3)]
        b_tab = sig("b_tables", 16)
        bg_pe, bg_act = sig("b_gemm_pe"), sig("b_gemm_act")
        b_pe, b_act, b_vec, b_pool = sig("b_attn_pe"), sig("b_attn_act"), sig("b_attn_vec"), sig("b_attn_pool")
        x_back, o_row, f_row = sig("x_again", 16), sig("mix_row", 16), sig("ff_row", 16)
        o_w = [sig(f"out_weights{q}", 16) for q in range(2)]
        o_pe, o_act, o_vec = sig("out_pe"), sig("out_act"), sig("out_vec")
        u_w = [sig(f"up_weights{q}", 16) for q in range(4)]
        u_pe, u_act, u_vec = sig("up_pe"), sig("up_act"), sig("up_vec")
        d_w = [sig(f"down_weights{q}", 16) for q in range(4)]
        dn_act, dn_vec = sig("down_split_act"), sig("down_split_vec")
        d_pe, d_act, d_vec = sig("down_pe"), sig("down_act"), sig("down_vec")

        def over_chain(ended):
            at = [0]

            def fill(n):
                for m in range(at[0], min(at[0] + n, 12 * KB + PAUSE)):
                    g = m // KB if m < 8 * KB else (m - PAUSE) // KB
                    if m % KB == KB - 1 and not 8 * KB <= m < 8 * KB + PAUSE:
                        ended(g)
                at[0] += n
            return fill

        def pieces_b(g):
            return [g + 4] if g < 4 else range(8, 12) if g == 7 else []

        slots2 = [(range(0, 4), False), (range(4, 6), True), (range(6, 10), True), (range(10, 14), False),
                  (range(14, 18), False), (range(18, 22), False), (range(22, 26), True), (range(26, 30), True)]

        def pieces_after(g):
            n = next(n for n, (groups, _) in enumerate(slots2) if g in groups)
            groups, wide = slots2[n]
            if n == 7:
                return []
            return [4 * n + 4 + g - groups[0]] if not wide else [4 * n + 4 + q for q in range(4)] if g == groups[-1] else []

        def piece2(p):
            n, q = p // 4, p % 4
            if slots2[n][1]:
                width = 256 if n == 7 else 512
                return ring[n % 2][:, 2 * q:2 * q + 2, 0:width], h_row[q][:, :, 0:width]
            return ring[n % 2][:, :, q * P:(q + 1) * P], h_col[q]

        events2 = [(g, b, part) for g in range(3) for part in ("gate", "br") for b in range(4)]

        def piece_done(g, b, part):
            return 6 * g + b if part == "gate" else 6 * g + 4 + b // 2 if b % 2 else None

        def piece3(i):
            g, j = i // 6, i % 6
            if j < 4:
                return ring[g % 2][:, :, j * P:(j + 1) * P], h_col[i % 4]
            return ring[2][:, 4 * (g % 2):4 * (g % 2) + 4, (j - 4) * 256:(j - 3) * 256], hq[i % 4].rearrange("p (k n) -> p k n", k=4)

        def only(i):
            return isinstance(i, int) and i == 0

        block = ctx.enter_context(nc.Block())

        @block.sync
        def _(sp):
            ld_x.mark(sp.dma_start(XR, T["x"].rearrange("(t p) d -> p t d", p=P)), "x")
            ld_const.mark(sp.dma_start(const[:, 0:T["consts"].shape[1]], T["consts"]), "consts")
            ld_const.mark(sp.dma_start(cols[:, 0:V_N], T["cols"]), "cols")
            sp.wait_ge(*z_pool("wsm"))
            ld_small.mark(sp.dma_start(wsm[:, :, 0:8], W[:, :, C_BETA + 8:C_BETA + 16]), "steps")
            ld_small.mark(sp.dma_start(wsm[:, :, 32:40], W[:, :, C_BETA:C_BETA + 8]), "w")

            def load_a(p):
                last = not (only(p) and p == 0)
                if last:
                    sp.wait_ge(*g_pe("g3", p - 1))
                a_w[0].start()
                a_w[0].mark(sp.dma_start(ring[0][:, :, 0:256], W[:, :, bass.ds(p * 256 + C_QA, 256)]), "q")
                a_w[0].mark(sp.dma_start(ring[0][:, :, 256:512], W[:, :, bass.ds(p * 256 + C_KA, 256)]), "k")
                if last:
                    sp.wait_ge(*g_pe("g7", p - 1))
                a_w[1].start()
                a_w[1].mark(sp.dma_start(ring[1], W[:, :, bass.ds(p * 512 + C_VA, 512)]), "v")
                if last:
                    sp.wait_ge(*g_pe("g11", p - 1))
                a_w[2].start()
                a_w[2].mark(sp.dma_start(ring[2], W[:, :, bass.ds(p * 512 + C_ZA, 512)]), "z")

            load_a(0)
            sp.wait_ge(*s_act("eg"))
            sp.wait_ge(*s_vec("gcum"))
            s_dma.mark(sp.dma_start(scratch, ST), "rows")
            with sp.Fori(1, PAIRS) as p:
                load_a(p)

            def load_merge(x, c, before=None):
                col, wb = (C_GA, T["w_br_a"]) if x == 0 else (C_GBT, T["w_br_b"])
                wb = wb.rearrange("(a k p) n -> a p k n", p=P, a=2)
                srcs = (W[:, :, bass.ds(c * 512 + col, 512)], wb[0][:, :, bass.ds(c * 512, 512)], wb[1][:, :, bass.ds(c * 512, 512)])
                for q in range(3):
                    sp.wait_ge(*(before[q] if before else m_pe[x](("gate3", "lo3", "y3")[q], c - 1)))
                    m_w[x][q].start()
                    m_w[x][q].mark(sp.dma_start(ring[q], srcs[q]), "w")

            def load_b(h, before=None):
                for q in range(3):
                    sp.wait_ge(*(before[q] if before else bg_pe(f"g{4 * q + 3}", h - 1)))
                    b_w[q].start()
                    if q == 0:
                        b_w[0].mark(sp.dma_start(ring[0][:, :, 0:256], W[:, :, bass.ds(h * 256 + C_QB, 256)]), "q")
                        b_w[0].mark(sp.dma_start(ring[0][:, :, 256:512], W[:, :, bass.ds(h * 256 + C_KB, 256)]), "k")
                    else:
                        b_w[q].mark(sp.dma_start(ring[q], W[:, :, bass.ds(h * 512 + (C_VB if q == 1 else C_GB), 512)]), "k")

            load_b(0, [g_pe(f"g{g}", PAIRS - 1) for g in (3, 7, 11)])
            for s_, what in ((c_pe, "vN1"), (c_vec, "qT1"), (c_pool, "qeT1")):
                sp.wait_ge(*s_(what, PAIRS - 1))
            b_tab.mark(sp.dma_start(rope_tab, T["rope_b"].rearrange("p (a n) -> p a n", a=2)), "rope")
            b_tab.mark(sp.dma_start(dmask, T["decay_b"].rearrange("p (h c) -> p h c", h=B_HEADS)), "decay")
            with sp.Fori(1, B_HEADS) as h:
                load_b(h)

            def load_o(x):
                ot_ld[x].mark(sp.dma_start(oT, oT_rows[x].rearrange("k p n -> p k n")), "o")
            load_merge(0, 0, [bg_pe(f"g{g}", B_HEADS - 1) for g in (3, 7, 11)])
            sp.wait_ge(*b_vec("oT3", B_HEADS - 1))
            sp.wait_ge(*ob_st_s("o", B_HEADS - 1))
            load_o(0)
            with sp.Fori(1, 2) as c:
                load_merge(0, c)
            load_merge(1, 0, [m_pe[0](n, 1) for n in ("gate3", "lo3", "y3")])
            load_o(1)
            with sp.Fori(1, 2) as c:
                load_merge(1, c)

            WO = T["w_out"].rearrange("(k p) n -> p k n", p=P)
            for q in range(2):
                sp.wait_ge(*m_pe[1](("gate3", "lo3")[q], 1))
                o_w[q].mark(sp.dma_start(ring[q], WO[:, :, q * 512:(q + 1) * 512]), "w")
            sp.wait_ge(*m_vec[1]("mix3", 1))
            x_back.mark(sp.dma_start(XR, T["x"].rearrange("(t p) d -> p t d", p=P)), "x")
            o_row.mark(sp.dma_start(row, T["norm_mix_post"].broadcast_to([P, DM])), "row")
            WU = T["w_up"].rearrange("(k p) n -> p k n", p=P)
            WD = T["w_down"].rearrange("(a k p) n -> a p k n", p=P, a=4)

            def load_up(i, before=None):
                for q in range(4):
                    sp.wait_ge(*(u_pe(f"g{4 * q - 5}", i) if q >= 2 else before[q] if before else u_pe(f"g{4 * q + 11}", i - 1)))
                    u_w[q].start()
                    u_w[q].mark(sp.dma_start(ring[q % 2], WU[:, :, bass.ds(i * 2048 + q * 512, 512)]), "w")
            load_up(0, [o_pe("m31"), o_pe("m31")])
            with sp.Fori(1, 2) as i:
                load_up(i)

            def load_down(c, before=None):
                for q in range(4):
                    sp.wait_ge(*(d_pe(f"p{4 * q - 5}", c) if q >= 2 else before[q] if before else d_pe(("p11", "m3")[q], c - 1)))
                    d_w[q].start()
                    d_w[q].mark(sp.dma_start(ring[q % 2], WD[q][:, :, bass.ds(c * 512, 512)]), "w")
            load_down(0, [u_pe(f"g{4 * q + 11}", 1) for q in range(2)])
            with sp.Fori(1, 2) as c:
                load_down(c)
            sp.wait_ge(*o_vec("x3"))
            f_row.mark(sp.dma_start(row, T["norm_mlp_post"].broadcast_to([P, DM])), "row")
            sp.wait_ge(*d_vec("x3"))
            mem_ld.mark(sp.dma_start(memN, T["mem_2"].rearrange("(t p) d -> p t d", p=P)), "mem")
            n2_tab.mark(sp.dma_start(const[:, 1490:1490 + 256], T["rope_g"]), "rope")
            n2_tab.mark(sp.dma_start(bmask, T["na_mask"].rearrange("p (v n) -> p v n", v=3)), "mask")
            n2_tab.mark(sp.dma_start(gain, T["gains"].rearrange("o (a n) -> o a n", a=2).broadcast_to([P, 2, 64])), "gain")
            W2 = T["w_in_2"].rearrange("(k p) n -> p k n", p=P)
            WM = T["w_mem_kv_2"].rearrange("(k p) n -> p k n", p=P)
            order = [(WM, 0, 512), (WM, 512, 512), (W2, 1024, 512), (W2, 1536 + 768, 512), (W2, 0, 512), (W2, 512, 512),
                     (W2, 1536, 512), (W2, 2048, 256)]
            last_group = [3, 5, 9, 13, 17, 21, 25, 29]
            for n, (src, col, width) in enumerate(order):
                q = n % 2
                sp.wait_ge(*(d_pe(("p11", "m3")[q], 1) if n < 2 else p_pe(f"g{last_group[n - 2]}")))
                w2[q].mark(sp.dma_start(ring[q][:, :, 0:width], src[:, :, col:col + width]), f"w{n}")
                if n == 4:
                    sp.wait_ge(*p_act("e9"))
                    v_st.mark(sp.dma_start(v_rows.rearrange("(t p) d -> p t d", p=P), vnN), "v")
                    sp.wait_ge(*v_st("v"))
                    for cb, start in enumerate((0, 8, 24, 32)):
                        for half in range(2):
                            rows = v_rows.rearrange("(r c) d -> r c d", c=64)[4 * half:4 * half + 4, start:start + 32, :]
                            v_ld.mark(sp.dma_start(vband[:, cb * 2 + half, :], rows), f"v{cb}{half}")
                if n == 6:
                    def load_bias(b):
                        if not only(b):
                            sp.wait_ge(*at_vec["n"]("s7", b - 1))
                        bias_ld.start()
                        bias_ld.mark(sp.dma_start(bias, T["na_bias"][bass.ds(b, 1), :, :].rearrange("a p (e v n) -> (a p) e v n", e=2, v=3)), "bias")
                    load_bias(0)
                    with sp.Fori(1, 4) as b:
                        load_bias(b)

            WB2 = T["w_branch_2"].rearrange("(g k p) n -> g p k n", p=P, k=4)

            def load_merge2(c, first=False):
                for q in range(4):
                    mg_w[q].start()
                for g in range(3):
                    q = g % 2
                    sp.wait_ge(*((p_pe("g25"), p_pe("g29"), mg_pe("gate03", 0))[g] if first
                                 else mg_pe(("gate23", "gate13")[g], c - 1) if g < 2 else mg_pe("gate03", c)))
                    mg_w[q].mark(sp.dma_start(ring[q], W2[:, :, bass.ds(c * 512 + 2816 + g * DM, 512)]), f"w{g}")
                    if first and g == 0:
                        sp.wait_ge(*at_pe["g"]("AV7", 3))
                        sp.wait_ge(*at_vec["g"]("n7", 3))
                        sp.wait_ge(*r_pool("dup"))
                    elif g == 2:
                        sp.wait_ge(*mg_pe("br03", c))
                    elif not first:
                        sp.wait_ge(*mg_pe(("br23", "br13")[g], c - 1))
                    mg_w[2 + q].mark(sp.dma_start(ring[2][:, 4 * q:4 * q + 4, :], WB2[g][:, :, bass.ds(c * 512, 512)]), f"w{g}")
                    if first:
                        kind, at = (("n", 0), ("g", 4), ("m", 8))[g]
                        sp.wait_ge(*y_sd[kind]("y", 3))
                        y_ld[kind].mark(sp.dma_start(yT[:, at:at + 4, :], y_rows[at:at + 4].rearrange("k p n -> p k n")), "y")
            load_merge2(0, True)
            with sp.Fori(1, 2) as c:
                load_merge2(c)
            WO2 = T["w_out_2"].rearrange("(k p) n -> p k n", p=P)
            for q in range(2):
                sp.wait_ge(*mg_pe(("gate23", "gate13")[q], 1))
                l_w[q].mark(sp.dma_start(ring[q], WO2[:, :, q * 512:(q + 1) * 512]), "w")
            sp.wait_ge(*y_sd["g"]("y", 3))
            for n, name in enumerate(("ln1_g_2", "ln1_b_2")):
                l_row.mark(sp.dma_start(lnrow[:, n, :], T[name].broadcast_to([P, DM])), name)
            sp.wait_ge(*mg_pe("br23", 1))
            q_ld.mark(sp.dma_start(iota, T["iota"]), "iota")
            q_ld.mark(sp.dma_start(wr, T["w_router_2"].rearrange("(k p) e -> p k e", p=P)), "wr")
            WGU = T["w_gate_up_2"].rearrange("e (k p) n -> e p k n", p=P)
            WDN = T["w_down_2"].rearrange("e (k p) n -> e p k n", p=P)

            def load_experts(p):
                for q in range(6):
                    e_w[q].start()
                for n in range(12):
                    q, e = n // 2, n % 2
                    if q >= 3:
                        sp.wait_ge(*e_pe(f"group{q - 3}", p))
                    elif not only(p):
                        sp.wait_ge(*e_pe(f"group{q + 3}", p - 1))
                    else:
                        sp.wait_ge(*l_pe("m31"))
                    src, col = (WGU, q // 2 * 512 + q % 2 * DM) if q < 4 else (WDN, (q - 4) * 512)
                    e_w[n % 6].mark(sp.dma_start(eslot[n % 6], src[bass.ds(p * 2 + e, 1), :, :, col:col + 512].rearrange("a p k n -> (a p) k n")), f"w{n // 6}")
            load_experts(0)
            sp.wait_ge(*l_vec("x3"))
            for n, name in enumerate(("ln2_g_2", "ln2_b_2")):
                f_rowl.mark(sp.dma_start(lnrow2[:, n, :], T[name].broadcast_to([P, DM])), name)
            with sp.Fori(1, NE // 2) as p:
                load_experts(p)
            for t in range(NT):
                sp.wait_ge(*f_vec(f"x{t}"))
                done.mark(sp.dma_start(out[t * P:(t + 1) * P, :], XR[:, t, :]), f"out{t}")
            sp.wait_ge(*done("out3"))

        @block.gpsimd
        def _(pool):
            z_pool.mark(pool.memset(eps, EPS), "eps")
            z_pool.mark(pool.memset(one, 1.0), "one")
            z_pool.mark(pool.memset(eps5, 1e-5), "eps5")
            z_pool.mark(pool.memset(wsm, 0.0), "wsm")
            z_pool.mark(pool.memset(ST, 0.0), "ST")
            z_pool.mark(pool.memset(pre[:, :, 0:4], 0.0), "pads")
            pool.wait_ge(*s_dma("rows"))

            def rows(p, j):
                h = p * 2 + j
                if not only(p):
                    pool.wait_ge(*c_vec(f"S{NT - 2}_{j}", p - 1))
                    pool.wait_ge(*c_vec(f"Dpre{j}", p - 1))
                    pool.wait_ge(*c_pool(f"qeT{j}", p - 1))
                a_bc[j].start()
                for n, r in enumerate((0, 32, 96)):
                    a_bc[j].mark(pool.dma_start(bc[:, j, n, :], scratch[bass.ds(h + r, 1), :].broadcast_to([P, SEQ])), f"r{n}")

            def store_a(p, j):
                pool.wait_ge(*c_vec(f"oT1{j}", p))
                oa_st[j].start()
                oa_st[j].mark(pool.dma_start(oT_rows[0][bass.ds((p * 2 + j) * 2, 2), :, :].rearrange("d p n -> p d n"), o_st), "o")

            def chain_a(p):
                c_pool.start()
                for j in range(2):
                    rows(p, j)
                if not only(p):
                    store_a(p - 1, 1)
                for b in range(6, 8):
                    pool.wait_ge(*c_act(f"tap{b}", p))
                    if b == 6 and not only(p):
                        pool.wait_ge(*c_pe("oT11", p - 1))
                    for k in range(2, -1, -1):
                        term = dl[:, k % 2 * 512:(k % 2 + 1) * 512]
                        w = cols[:, bass.ds((p * 4 + 16 + b - 4) * 4 + V_CONV + k, 1)].broadcast_to([P, 512])
                        c_pool.link(pool, pool.tensor_tensor(term, pre[:, b, k:k + 512], w, ALU.mult), p)
                        i = pool.tensor_tensor(y[:, b, :], y[:, b, :], term, ALU.add)
                        if k:
                            c_pool.link(pool, i, p)
                    c_pool.mark(i, f"conv{b}")
                    if b == 6:
                        pool.wait_ge(*c_pool("conv6", p))
                for j in range(2):
                    before = (lambda what: c_vec(what + "0", p)) if j else (lambda what: c_vec(what + "1", p - 1))
                    pbefore = (lambda what: c_pe(what + "0", p)) if j else (lambda what: c_pe(what + "1", p - 1))
                    first = only(p) and j == 0
                    if j:
                        store_a(p, 0)
                    pool.wait_ge(*a_bc[j]("r2", p))
                    pool.wait_ge(*c_vec(f"kT{j}", p))
                    if not first:
                        pool.wait_ge(*pbefore("KK"))
                    c_pool.mark(pool.tensor_tensor(kbT, kT, bc[:, j, 1, :], ALU.mult), f"kbT{j}")
                    pool.wait_ge(*c_vec(f"qT{j}", p))
                    if not first:
                        pool.wait_ge(*pbefore("O3"))
                    c_pool.mark(pool.tensor_tensor(qeT, qT, bc[:, j, 2, :], ALU.mult), f"qeT{j}")
                    pool.wait_ge(*c_act(f"D{j}", p))
                    c_pool.mark(pool.tensor_tensor(D, D, m_incl.unsqueeze(1).broadcast_to([P, NT, P]), ALU.mult), f"D{j}")
                    pool.wait_ge(*c_vec(f"LT{j}", p))
                    for s in range(LEVELS):
                        if s >= 2:
                            pool.wait_ge(*c_pe(f"P{s - 2}_{j}", p))
                        elif not first:
                            pool.wait_ge(*pbefore(f"P{LEVELS - 2 + s}_" if LEVELS % 2 == 0 else f"P{LEVELS - 1 if s == 0 else LEVELS - 2}_"))
                        if s == 2:
                            pool.wait_ge(*c_vec(f"Y0_{j}", p))
                        c_pool.mark(pool.tensor_tensor(
                            NM[:, s % 2, :].rearrange("p (t c) -> p t c", t=NT), LT,
                            m_lvl[:, s, :].unsqueeze(1).broadcast_to([P, NT, P]), ALU.mult), f"NM{s}_{j}")

            chain_a(0)
            with pool.Fori(1, PAIRS) as p:
                chain_a(p)
            store_a(PAIRS - 1, 1)

            def rope_k(h):
                b_pool.start()
                if only(h) and h == 0:
                    pool.wait_ge(*b_tab("decay"))
                    pool.wait_ge(*c_vec("oT11", PAIRS - 1))
                else:
                    pool.wait_ge(*b_pe("S3", h - 1))
                pool.wait_ge(*bg_act("e3", h))
                for o, (c0, c1, op) in enumerate(((cosT, sinT, ALU.subtract), (sinT, cosT, ALU.add))):
                    pool.tensor_tensor(rk[:, 0, :], qkr[:, 2, :], c0, ALU.mult)
                    b_pool.link(pool, pool.tensor_tensor(rk[:, 1, :], qkr[:, 3, :], c1, ALU.mult), h)
                    i = pool.tensor_tensor(qkT[:, 2 + o, :], rk[:, 0, :], rk[:, 1, :], op)
                    if o == 0:
                        b_pool.link(pool, i, h)
                b_pool.mark(i, "ropek")
            def store_b(h):
                pool.wait_ge(*b_vec("oT3", h))
                ob_st_s.start()
                ob_st_s.mark(pool.dma_start(oT_rows[1][bass.ds(h * 4, 4), :, :].rearrange("d p n -> p d n"), ob_st), "o")
            rope_k(0)
            with pool.Fori(1, B_HEADS) as h:
                rope_k(h)
                store_b(h - 1)
            store_b(B_HEADS - 1)

            pool.wait_ge(*d_vec("x3"))

            def stage(kind, b):
                S = at_pool[kind]
                S.start()
                flat = lambda x: x.rearrange("p a n -> p (a n)")
                if not only(b):
                    pool.wait_ge(*at_pe[kind]("S7" if kind != "m" else "S3", b - 1))
                elif kind == "m":
                    pool.wait_ge(*at_pe["n"]("AV7", 3))
                elif kind == "g":
                    pool.wait_ge(*at_pe["m"]("AV3", 3))
                if kind == "n":
                    if only(b):
                        pool.wait_ge(*p_act("e17"))
                    for e in range(2):
                        for cb in range(4):
                            i = pool.tensor_tensor(qz[:, e, cb * P:(cb + 1) * P].rearrange("p (r q) -> p r q", r=8),
                                                   flat(qnT[:, bass.ds(b, 1), :]).rearrange("p (r c) -> p r c", r=8)[:, :, cb * 16:cb * 16 + 16],
                                                   cols[:, V_HALF + e:V_HALF + e + 1].unsqueeze(2).broadcast_to([P, 8, 16]), ALU.mult)
                        S.mark(i, f"q{e}")
                    if only(b):
                        pool.wait_ge(*n2_tab("gain"))
                    pool.wait_ge(*bias_ld("bias", b))
                    S.mark(pool.tensor_tensor(bias, bias, bmask.unsqueeze(1).broadcast_to([P, 2, 3, 256]), ALU.add), "bias")
                    if only(b):
                        pool.wait_ge(*v_ld("v31"))
                    else:
                        pool.wait_ge(*at_pe["n"]("AV7", b - 1))
                    S.mark(pool.tensor_copy(vst, vband[:, :, bass.ds(b * P, P)]), "v")
                elif kind == "m":
                    S.mark(pool.tensor_copy(qst, flat(qmT[:, bass.ds(b, 1), :])), "q0")
                    if not only(b):
                        pool.wait_ge(*at_pe["m"]("AV3", b - 1))
                    S.mark(pool.tensor_copy(vst[:, 0:2, :], mvN[:, :, bass.ds(b * P, P)]), "v")
                else:
                    if only(b):
                        pool.wait_ge(*r_act("kT1"))
                    for e in range(2):
                        S.mark(pool.tensor_tensor(qz[:, e, :], flat(qgT[:, bass.ds(b, 1), :]),
                                                  cols[:, V_HALF + e:V_HALF + e + 1].broadcast_to([P, 512]), ALU.mult), f"q{e}")
                    if not only(b):
                        pool.wait_ge(*at_pe["g"]("AV7", b - 1))
                    S.mark(pool.tensor_copy(vst[:, 0:4, 0:64], vdup[:, :, bass.ds(b * 64, 64)]), "v")
                if not only(b):
                    store_y(kind, b - 1)

            def store_y(kind, b):
                pool.wait_ge(*at_vec[kind]("y", b))
                y_sd[kind].start()
                off = {"n": 0, "g": 4, "m": 8}[kind]
                y_sd[kind].mark(pool.dma_start(y_rows[bass.ds(b + off, 1), :, :].rearrange("a p n -> p (a n)"), y_st), "y")

            def staged(kind):
                stage(kind, 0)
                with pool.Fori(1, 4) as b:
                    stage(kind, b)
                store_y(kind, 3)
            staged("n")

            for t in range(NT):
                pool.wait_ge(*p_act(f"e{26 + t}"))
                r_pool.mark(pool.tensor_tensor(ro[:, t, :], qkN[:, t, 0:640], qkN[:, t, 0:640], ALU.mult), f"sq{t}")
            staged("m")
            for t in range(NT):
                pool.wait_ge(*r_vec(f"scaled{t}"))
                x = qkN[:, t, 0:640].rearrange("p (h d) -> p h d", h=10)
                pool.tensor_tensor(x[:, 0:8, :], x[:, 0:8, :], gain[:, 0:1, :].broadcast_to([P, 8, 64]), ALU.mult)
                r_pool.mark(pool.tensor_tensor(x[:, 8:10, :], x[:, 8:10, :], gain[:, 1:2, :].broadcast_to([P, 2, 64]), ALU.mult), f"gain{t}")
            pool.wait_ge(*r_vec("rope3"))
            k3 = ro[:, :, 512:640].rearrange("p t (a d) -> p t a d", a=2)
            for e in range(2):
                i = pool.tensor_copy(kdup[:, :, :, 64 * e:64 * e + 64], k3)
            r_pool.mark(i, "dup")
            for n in range(4):
                i = pool.tensor_copy(vdup[:, :, n * 64:(n + 1) * 64], qkN[:, :, 640 + n // 2 * 64:704 + n // 2 * 64])
            r_pool.mark(i, "vdup")
            pool.wait_ge(*r_pool("vdup"))
            staged("g")

        @block.scalar
        def _(act):
            act.wait_ge(*ld_const("cols"))
            act.wait_ge(*ld_x("x"))
            for t in range(NT):
                n_act.mark(act.activation(AT[:, 2 * t:2 * t + 2, :], XR[:, t, :].rearrange("p (a b) -> p a b", a=2), ACT.Square, accum_out=stat[:, t:t + 1]), f"sq{t}")
            act.wait_ge(*z_pool("one"))
            act.wait_ge(*n_act("sq3"))
            n_act.mark(act.activation(stat[:, 4:8], stat[:, 0:4], ACT.Sqrt, bias=eps, scale=1.0 / DM), "rms")
            for b in range(0, KB, 2):
                act.wait_ge(*n_pe(f"T{b}"))
                n_act.mark(act.activation(AT[:, b, :], psum[b][:, :], ACT.Copy, scale=cols[:, V_MIXPRE + b:V_MIXPRE + b + 1]), f"AT{b}")

            for q in range(4):
                act.wait_ge(*n_act(f"AT{2 * q}"))
                act.wait_ge(*n_vec(f"AT{2 * q + 1}"))
                high(act, n_act, at_hi[:, 2 * q:2 * q + 2, :], AT[:, 2 * q:2 * q + 2, :], f"ATh{q}")

            def split_a(p, n):
                if n % 4 == 0:
                    act.wait_ge(*a_w[n // 4](("k", "v", "z")[n // 4], p))
                if n >= 4:
                    act.wait_ge(*g_pe(f"g{n - 4}", p))
                elif not (only(p) and p == 0):
                    act.wait_ge(*g_pe("g11", p - 1))
                if n < 8:
                    high(act, g_act, h_col[n % 4], ring[n // 4][:, :, n % 4 * P:(n % 4 + 1) * P], f"w{n}")
                else:
                    high(act, g_act, h_row[n % 4], ring[2][:, n % 4 * 2:n % 4 * 2 + 2, :], f"w{n}")

            g_act.start()
            for n in range(4):
                split_a(0, n)

            act.wait_ge(*s_pe("proj"))
            act.wait_ge(*z_pool("pads"))
            act.activation(ST[32:40, :], psum[3][32:40, :], ACT.Sigmoid)
            s_act.link(act, act.activation(u8[0:8, 0, :], psum[3][0:8, :], ACT.Identity, bias=cols[0:8, V_DT:V_DT + 1]))
            s_act.link(act, act.activation(u8[0:8, 1, :], u8[0:8, 0, :], ACT.Abs))
            s_act.link(act, act.activation(u8[0:8, 1, :], u8[0:8, 1, :], ACT.Exp, scale=-1.0))
            s_act.mark(act.activation(stat[0:8, 8:9], cols[0:8, V_ALOG:V_ALOG + 1], ACT.Exp), "alog")
            s_act.mark(act.activation(u8[0:8, 1, :], u8[0:8, 1, :], ACT.Ln, bias=one[0:8, :]), "ln")
            act.wait_ge(*s_vec("kdiff"))
            s_act.mark(act.activation(ST[64:72, :], u8[0:8, 2, :], ACT.Exp), "kd")
            s_act.mark(act.activation(ST[96:104, :], ST[0:8, :], ACT.Exp), "eg")

            def evacuate(p, g):
                act.wait_ge(*g_pe(f"g{g}", p))
                if g < 8:
                    if not only(p):
                        act.wait_ge(*(c_vec if g < 6 else c_pool)(f"conv{g}", p - 1))
                    elif g == 0:
                        act.wait_ge(*z_pool("pads"))
                    dst = pre[:, g, 3:515]
                else:
                    if not only(p):
                        act.wait_ge(*c_act("zs", p - 1))
                    dst = zraw[:, g - 8, :]
                g_act.mark(act.activation(dst, psum[g % 2][:, :], ACT.Copy), f"e{g}")
                if g < 8:
                    split_a(p, g + 4)

            def chain_a(p, fill):
                c_act.start()
                first = only(p) and p == 0
                if not first:
                    act.wait_ge(*c_vec("qT1", p - 1))
                    act.wait_ge(*c_vec("kT1", p - 1))
                    act.wait_ge(*c_pe("vN1", p - 1))
                else:
                    act.wait_ge(*n_vec("xn"))
                    act.wait_ge(*n_pe("T7"))
                act.wait_ge(*g_act("e11", p))
                for b in range(8):
                    blk = (p * 2 + b) if b < 2 else (p * 2 + 8 + b - 2) if b < 4 else (p * 4 + 16 + b - 4)
                    c_act.mark(act.activation(y[:, b, :], pre[:, b, 3:515], ACT.Copy,
                                              scale=cols[:, bass.ds(blk * 4 + V_CONV + 3, 1)]), f"tap{b}")
                if not first:
                    act.wait_ge(*c_vec("gate1", p - 1))
                c_act.mark(act.activation(zs, zraw, ACT.Silu), "zs")

                def squares(j):
                    act.wait_ge(*c_act(f"silu{2 + j}", p))
                    if j or not first:
                        act.wait_ge(*(c_pe("wT0", p) if j else c_pe("wT1", p - 1)))
                        act.wait_ge(*(c_pe("S2_0", p) if j else c_pe("S2_1", p - 1)))
                    c_act.mark(act.activation(sq[:, 0, :], y[:, j, :], ACT.Square), f"sqq{j}")
                    c_act.mark(act.activation(sq[:, 1, :], y[:, 2 + j, :], ACT.Square), f"sqk{j}")
                for b in range(8):
                    act.wait_ge(*(c_vec if b < 6 else c_pool)(f"conv{b}", p))
                    c_act.mark(act.activation(y[:, b, :], y[:, b, :], ACT.Silu), f"silu{b}")
                    fill(FILL["conv"])
                    if b == 3:
                        squares(0)
                for j in range(2):
                    prev = (lambda s, what: s(what + "0", p)) if j else (lambda s, what: s(what + "1", p - 1))
                    noprev = first and j == 0
                    if j:
                        fill(FILL["norm"])
                        squares(1)
                    act.wait_ge(*c_pe(f"ss{j}", p))
                    if not noprev:
                        act.wait_ge(*prev(c_pe, "V3_"))
                    for n, what in ((1, "k"), (0, "q")):
                        c_act.link(act, act.activation(rinv[:, n, :], psum[2 + n][:, :], ACT.Ln, bias=eps), p)
                        c_act.mark(act.activation(rinv[:, n, :], rinv[:, n, :], ACT.Exp, scale=-0.5), f"root{what}{j}")
                    fill(FILL["scores"])
                    act.wait_ge(*c_vec(f"Dpre{j}", p))
                    c_act.mark(act.activation(D, D, ACT.Exp), f"D{j}")
                    fill(FILL["tokens"] + FILL["inverse"])
                    for s in range(1, LEVELS):
                        act.wait_ge(*c_pe(f"P{s}_{j}", p))
                        if s > 1:
                            act.wait_ge(*c_pe(f"Y{s - 1}_{j}", p))
                        elif not noprev:
                            act.wait_ge(*prev(c_pe, f"Y{LEVELS - 1}_"))
                            act.wait_ge(*(oa_st[0]("o", p) if j else oa_st[1]("o", p - 1)))
                        c_act.mark(act.activation(PP, psum[4][:, :].rearrange("p (t c) -> p t c", t=NT), ACT.Copy), f"P{s}_{j}")
                        fill(sum(FILL["level"]))
                    act.wait_ge(*c_pe(f"wT{j}", p))
                    if not noprev:
                        act.wait_ge(*prev(c_pe, "V3_"))
                    c_act.mark(act.activation(nwT, psum[7][:, :], ACT.Copy, scale=-1.0), f"wT{j}")
                    fill(FILL["w"])
                    for t in range(NT):
                        act.wait_ge(*c_pe(f"V{t}_{j}", p))
                        if t:
                            act.wait_ge(*c_pe(f"O{t - 1}{j}", p))
                        elif not noprev:
                            act.wait_ge(*prev(c_pe, "O3"))
                        c_act.mark(act.activation(vnew, psum[2][:, 0:A_DV], ACT.Copy), f"vnew{t}_{j}")
                        fill(sum(FILL["state"]))
                    for t in range(NT):
                        if t == 0:
                            act.wait_ge(*c_pe(f"O3{j}", p))
                        c_act.mark(act.activation(oj[:, t, :], psum[4 + t // 2][:, t % 2 * A_DV:(t % 2 + 1) * A_DV],
                                                  ACT.Square, accum_out=stat[:, t:t + 1]), f"osq{t}_{j}")
                    act.wait_ge(*c_act(f"osq3_{j}", p))
                    c_act.mark(act.activation(stat[:, 4:8], stat[:, 0:4], ACT.Sqrt, bias=eps, scale=1.0 / A_DV), f"orms{j}")
                    fill(FILL["out"])
                fill(99)

            for g in range(12):
                evacuate(0, g)

            def with_evacuations(p):
                g_act.start()
                for n in range(4):
                    split_a(p, n)
                at = [0]

                def fill(n):
                    for m in range(at[0], min(at[0] + n, 96)):
                        if m % KB == KB - 1:
                            evacuate(p, m // KB)
                    at[0] += n
                chain_a(p - 1, fill)

            with_evacuations(1)
            with act.Fori(2, PAIRS) as p:
                with_evacuations(p)
            def split_b(h, n):
                if n % 4 == 0:
                    act.wait_ge(*b_w[n // 4]("k", h))
                if n >= 8:
                    act.wait_ge(*bg_pe("g7", h))
                elif n >= 4:
                    act.wait_ge(*bg_pe(f"g{n - 4}", h))
                elif not (only(h) and h == 0):
                    act.wait_ge(*bg_pe("g11", h - 1))
                elif n == 0:
                    act.wait_ge(*g_pe("g11", PAIRS - 1))
                if n < 4:
                    high(act, bg_act, h_col[n], ring[0][:, :, n * P:(n + 1) * P], f"w{n}")
                else:
                    high(act, bg_act, h_row[n % 4], ring[n // 4][:, n % 4 * 2:n % 4 * 2 + 2, :], f"w{n}")

            def evacuate_b(h, g):
                later = not (only(h) and h == 0)
                act.wait_ge(*bg_pe(f"g{g}", h))
                if g < 4:
                    if later:
                        act.wait_ge(*b_rope("ropeq", h - 1))
                        act.wait_ge(*b_pool("ropek", h - 1))
                    else:
                        act.wait_ge(*(c_vec if g < 6 else c_pool)(f"conv{g}", PAIRS - 1))
                    bg_act.mark(act.activation(qkr[:, g, :], psum[g % 2][:, :], ACT.Copy), f"e{g}")
                elif g < 8:
                    if later:
                        act.wait_ge(*b_pe("O3", h - 1))
                    else:
                        act.wait_ge(*(c_vec if g < 6 else c_pool)(f"conv{g}", PAIRS - 1))
                    bg_act.mark(act.activation(bv[:, g - 4, :], psum[g % 2][:, :], ACT.Copy), f"e{g}")
                else:
                    if later:
                        act.wait_ge(*b_vec("gate", h - 1))
                    elif g == 8:
                        act.wait_ge(*c_act("zs", PAIRS - 1))
                    bg_act.mark(act.activation(bg[:, g - 8, :], psum[g % 2][:, :], ACT.Silu), f"e{g}")

            def attn_b(h):
                b_act.start()
                for t in range(NT):
                    act.wait_ge(*b_pe(f"O{t}", h))
                    if t == 0 and not (only(h) and h == 0):
                        act.wait_ge(*b_pe("oT3", h - 1))
                    b_act.mark(act.activation(bo[:, t, :], psum[(6, 7, 2, 3)[t]][:, :], ACT.Square, accum_out=stat[:, t:t + 1]), f"osq{t}")
                act.wait_ge(*b_act("osq3", h))
                b_act.mark(act.activation(stat[:, 4:8], stat[:, 0:4], ACT.Sqrt, bias=eps, scale=1.0 / B_DV), "orms")

            def step_b(h):
                bg_act.start()
                for n in range(4):
                    split_b(h, n)
                for g in range(4):
                    evacuate_b(h, g)
                    split_b(h, g + 4)
                attn_b(h - 1)
                for g in range(4, 8):
                    evacuate_b(h, g)
                for n in range(8, 12):
                    split_b(h, n)
                for g in range(8, 12):
                    evacuate_b(h, g)
            bg_act.start()
            for n in range(4):
                split_b(0, n)

            def ended_b(g):
                evacuate_b(0, g)
                for n in pieces_b(g):
                    split_b(0, n)
            chain_a(PAIRS - 1, over_chain(ended_b))
            with act.Fori(1, B_HEADS) as h:
                step_b(h)
            attn_b(B_HEADS - 1)

            def merge(x, c):
                m_act[x].start()
                first = only(c) and c == 0
                for n in range(12):
                    b = n - 4
                    if n % 4 == 0 and n < 8:
                        act.wait_ge(*m_w[x][n // 4]("w", c))
                    if n == 5:
                        act.wait_ge(*m_w[x][2]("w", c))
                    if n < 4:
                        if first and n == 0:
                            act.wait_ge(*(bg_pe("g11", B_HEADS - 1) if x == 0 else m_pe[0]("y3", 1)))
                        elif not first:
                            act.wait_ge(*m_pe[x](("lo2", "y2", "lo3", "y3")[n], c - 1))
                    elif n < 8:
                        act.wait_ge(*m_pe[x](f"gate{b}", c))
                        if not first:
                            act.wait_ge(*m_vec[x](f"mix{b}", c - 1))
                        elif x == 1:
                            act.wait_ge(*m_vec[0](f"mix{b}", 1))
                        elif b == 0:
                            act.wait_ge(*b_vec("PT3", B_HEADS - 1))
                        m_act[x].mark(act.activation(sg[:, b, :], psum[b % 2][:, :], ACT.Sigmoid), f"sg{b}")
                    else:
                        act.wait_ge(*m_pe[x](("lo0", "y0", "lo1", "y1")[n - 8], c))
                    slot, q = (0, n) if n < 4 else (1 + n % 2, b // 2)
                    high(act, m_act[x], h_col[n % 4], ring[slot][:, :, q * P:(q + 1) * P], f"w{n}")
                    if n == 7 and first:
                        act.wait_ge(*ot_ld[x]("o"))
                        for k in range(8):
                            high(act, ot_act[x], oT_hi[:, 2 * k:2 * k + 2, :], oT[:, 2 * k:2 * k + 2, :], f"o{k}")
            merge(0, 0)
            with act.Fori(1, 2) as c:
                merge(0, c)
            merge(1, 0)
            with act.Fori(1, 2) as c:
                merge(1, c)

            def post_norm(pe_s, act_s, vec_s, bank, last, prenorm, hN):
                for t in range(NT):
                    for c in range(2):
                        act.wait_ge(*last(t, c))
                        act_s.mark(act.activation(hN[:, t, c * 512:(c + 1) * 512], psum[bank(t, c)][:, :], ACT.Square,
                                                  accum_out=stat[:, 2 * t + c:2 * t + c + 1]), f"sq{t}{c}")
                    act.wait_ge(*vec_s(f"ss{t}"))
                    act_s.mark(act.activation(stat[:, 12:13], stat[:, 2 * t:2 * t + 1], ACT.Sqrt, bias=eps, scale=1.0 / DM), f"rms{t}")
                    if prenorm:
                        act.wait_ge(*vec_s(f"x{t}"))
                        act_s.link(act, act.activation(hN[:, t, :], XR[:, t, :], ACT.Square, accum_out=stat[:, 13:14]))
                        act_s.mark(act.activation(stat[:, 14:15], stat[:, 13:14], ACT.Sqrt, bias=eps, scale=1.0 / DM), f"hrms{t}")
            act.wait_ge(*m_vec[1]("mix3", 1))
            for n in range(8):
                if n % 2 == 0:
                    high(act, o_act, mix_hi[:, n:n + 2, :], mixT[:, n:n + 2, :], f"mix{n // 2}")
                if n < 2:
                    act.wait_ge(*o_w[n]("w"))
                if n >= 4:
                    act.wait_ge(*o_pe(f"p{n - 4}"))
                high(act, o_act, h_row[n % 4], ring[n % 2][:, n // 2 * 2:n // 2 * 2 + 2, :], f"w{n}")
            post_norm(o_pe, o_act, o_vec, lambda t, c: 2 * t + c, lambda t, c: o_pe(f"m{t}{c}"), True, o_hN)

            def up_piece(n):
                return ring[n // 4 % 2][:, :, n % 4 * P:(n % 4 + 1) * P], h_col[n % 4]
            u_act.start()
            act.wait_ge(*u_w[0]("w"))
            for n in range(3):
                w, hi = up_piece(n)
                high(act, u_act, hi, w, f"w{n}")
            act.wait_ge(*o_vec("AT31"))
            for q in range(4):
                high(act, o_act, at_hi[:, 2 * q:2 * q + 2, :], AT[:, 2 * q:2 * q + 2, :], f"ATh{q}")

            def mlp_up(i):
                if not only(i):
                    u_act.start()
                for g in range(0 if only(i) else -3, 16):
                    n = g + 3
                    if n < 16:
                        if n % 4 == 0:
                            act.wait_ge(*u_w[n // 4]("w", i))
                        if n >= 4:
                            act.wait_ge(*u_pe(f"g{n - 4}", i))
                        elif not only(i):
                            act.wait_ge(*u_pe(f"g{n + 12}", i - 1))
                        high(act, u_act, h_col[n % 4], ring[n // 4 % 2][:, :, n % 4 * P:(n % 4 + 1) * P], f"w{n}")
                    if g < 0:
                        continue
                    act.wait_ge(*u_vec(f"relu{g}", i))
                    at = bass.ds(i * 16 + g, 1)
                    u_act.mark(act.activation(ffT[:, at, :], ffT[:, at, :], ACT.Square), f"ff{g}")
            mlp_up(0)
            with act.Fori(1, 2) as i:
                mlp_up(i)

            def mlp_down(c):
                dn_act.start()
                for n in range(16):
                    if n % 4 == 0:
                        act.wait_ge(*d_w[n // 4]("w", c))
                    if n >= 4:
                        act.wait_ge(*d_pe(f"p{n - 4}", c))
                    elif not only(c):
                        act.wait_ge(*d_pe(f"p{n + 12}" if n < 3 else "m3", c - 1))
                    elif n == 0:
                        act.wait_ge(*u_pe("g15", 1))
                        act.wait_ge(*u_act("ff15", 1))
                    high(act, dn_act, h_row[n % 4], ring[n // 4 % 2][:, n % 4 * 2:n % 4 * 2 + 2, :], f"w{n}")
                    high(act, dn_act, ff_hi[:, n % 4, :, :], ffT[:, 2 * n:2 * n + 2, :], f"ff{n}")
            mlp_down(0)
            with act.Fori(1, 2) as c:
                mlp_down(c)
            post_norm(d_pe, d_act, d_vec, lambda t, c: 4 * c + t, lambda t, c: d_pe("m3", 1), False, hN)

            def attend_body(kind, b):
                pe_s, act_s, vec_s = at_pe[kind], at_act[kind], at_vec[kind]
                act_s.start()
                units, nk = (4, 256) if kind == "m" else (8, 256 if kind == "n" else 512)
                for n in range(units + 1):
                    if n < units:
                        act.wait_ge(*vec_s(f"max{n}", b))
                        if n >= 3:
                            act.wait_ge(*pe_s(f"T{n - 3}", b))
                        src = sc[:, n % 2, 0:nk] if kind == "n" else psum[n % 3][:, 0:nk]
                        act_s.mark(act.activation(pr[:, n % 3, 0:nk], src, ACT.Exp, bias=nmax[:, n:n + 1], accum_out=psums[:, n:n + 1]), f"ex{n}")
                    if n:
                        m = n - 1
                        act.wait_ge(*pe_s(f"T{m}", b))
                        if m >= 2:
                            act.wait_ge(*pe_s(f"AV{m - 2}", b))
                        act_s.mark(act.activation(pT[:, m % 2, 0:nk], psum[3 + m % 2][:, 0:nk], ACT.Copy), f"pT{m}")

            def attend(kind):
                attend_body(kind, 0)
                with act.Fori(1, 4) as b:
                    attend_body(kind, b)

            def split2(p):
                if p % 4 == 0:
                    act.wait_ge(*w2[p // 4 % 2](f"w{p // 4}"))
                w, hi = piece2(p)
                high(act, p_act, hi, w, f"w{p}")
            split2(0)
            for q in range(4):
                act.wait_ge(*p_vec(f"memT{q}"))
                high(act, p_act, mem_hi[:, 2 * q:2 * q + 2, :], memT[:, 2 * q:2 * q + 2, :], f"mh{q}")
            for p in range(1, 4):
                split2(p)
            for q in range(4):
                high(act, p_act, at_hi[:, 2 * q:2 * q + 2, :], AT[:, 2 * q:2 * q + 2, :], f"ATh{q}")

            for g in range(30):
                if g == 22:
                    attend("n")
                act.wait_ge(*p_pe(f"g{g}"))
                if g == 0:
                    act.wait_ge(*d_vec("x3"))
                src = psum[6 + g % 2]
                if g < 4:
                    dst, src = mkT[:, g, :], src[:, 0:256]
                elif g < 6:
                    dst = mvN[:, g - 4, :]
                elif g < 10:
                    dst = vnN[:, g - 6, :]
                elif g < 14:
                    dst = qmT[:, g - 10, :]
                elif g < 18:
                    dst = qnT[:, g - 14, :]
                elif g < 22:
                    dst = knT[:, g - 18, :]
                elif g < 26:
                    dst = qkN[:, g - 22, 0:512]
                else:
                    dst, src = qkN[:, g - 26, 512:768], src[:, 0:256]
                scale = 128 ** -0.5 if 10 <= g < 14 else 0.125 if 14 <= g < 18 else 1.0
                p_act.mark(act.activation(dst, src, ACT.Copy, scale=scale), f"e{g}")
                for p in pieces_after(g):
                    split2(p)
            attend("m")
            act.wait_ge(*r_vec("ss"))
            r_act.mark(act.activation(gst, gst, ACT.Sqrt, bias=eps, scale=1.0 / 64), "root")
            for n in range(6):
                act.wait_ge(*r_pe(f"T{n}"))
                src = psum[6 + n % 2][:, :]
                if n < 4:
                    r_act.mark(act.activation(qgT[:, n, :], src, ACT.Copy, scale=0.125), f"qT{n}")
                else:
                    act.activation(kgT[:, 2 * (n - 4), :], src, ACT.Copy)
                    r_act.mark(act.activation(kgT[:, 2 * (n - 4) + 1, :], src, ACT.Copy), f"kT{n - 4}")
            attend("g")

            def merge2(c):
                mg_act.start()

                def split(i):
                    g, j = i // 6, i % 6
                    if j == 0:
                        act.wait_ge(*mg_w[g % 2](f"w{g}", c))
                    if j == 4:
                        act.wait_ge(*mg_w[2 + g % 2](f"w{g}", c))
                    w, hi = piece3(i)
                    high(act, mg_act, hi, w, f"w{i}")
                for i in range(4):
                    if not only(c):
                        act.wait_ge(*mg_pe(("br21", "br23", "gate22", "gate23")[i], c - 1))
                    split(i)
                for g, b, part in events2:
                    act.wait_ge(*mg_pe(f"{part}{g}{b}", c))
                    if part == "gate":
                        if g:
                            act.wait_ge(*mg_vec(f"m{g - 1}{b}", c))
                        elif not only(c):
                            act.wait_ge(*mg_vec(f"m2{b}", c - 1))
                        elif b == 0:
                            act.wait_ge(*at_pe["g"]("AV7", 3))
                        mg_act.mark(act.activation(sg2[:, b, :], psum[b][:, :], ACT.Sigmoid, bias=cols[:, bass.ds(c * 4 + V_BG + g * 8 + b, 1)]), f"sg{g}{b}")
                    i = piece_done(g, b, part)
                    if i is not None and i + 4 < 18:
                        split(i + 4)
                    if only(c) and (b, part) == (1, "gate"):
                        for k in range(2 * g, 2 * g + 2):
                            if k % 2 == 0:
                                act.wait_ge(*y_ld["ngm"[k // 2]]("y"))
                            high(act, y_act, yT_hi[:, 2 * k:2 * k + 2, :], yT[:, 2 * k:2 * k + 2, :], f"y{k}")
            merge2(0)
            with act.Fori(1, 2) as c:
                merge2(c)
            act.wait_ge(*mg_vec("m23", 1))
            for n in range(8):
                if n % 2 == 0:
                    high(act, l_act, mg_hi[:, n:n + 2, :], mgT[:, n:n + 2, :], f"mg{n // 2}")
                if n < 2:
                    act.wait_ge(*l_w[n]("w"))
                if n >= 4:
                    act.wait_ge(*l_pe(f"p{n - 4}"))
                high(act, l_act, h_row[n % 4], ring[n % 2][:, n // 2 * 2:n // 2 * 2 + 2, :], f"w{n}")
            act.wait_ge(*l_vec("var"))
            l_act.mark(act.activation(stat[:, 8:12].unsqueeze(2), stat[:, 0:8].rearrange("p (t two) -> p t two", two=2)[:, :, 1:2],
                                      ACT.Sqrt, bias=eps5), "root")
            act.wait_ge(*q_vec("less"))
            q_act.mark(act.activation(affN, affN, ACT.Exp), "exp")

            def experts(p):
                e_act.start()
                for q in range(2):
                    act.wait_ge(*e_pe(f"x{q}", p))
                    if q == 0 and not only(p):
                        act.wait_ge(*e_pe("group3", p - 1))
                    e_act.mark(act.activation(xst[:, 4 * q:4 * q + 4, :], psum[q][:, :].rearrange("p (b c) -> p b c", b=4), ACT.Copy), f"x{q}")
                for f in range(2):
                    act.wait_ge(*e_pe(f"group{2 * f}", p))
                    if not only(p):
                        act.wait_ge(*e_pe(f"a{f}", p - 1))
                    e_act.mark(act.activation(ga[:, f, :], psum[3 + 2 * f][:, :], ACT.Silu), f"silu{f}")
                for f in range(2):
                    act.wait_ge(*e_pe(f"a{f}", p))
                    if not only(p):
                        act.wait_ge(*e_pe("group5", p - 1))
                    e_act.mark(act.activation(actT[:, 4 * f:4 * f + 4, :], psum[(7, 3)[f]][:, :].rearrange("p (b c) -> p b c", b=4), ACT.Copy), f"a{f}")
                for n in range(2):
                    act.wait_ge(*e_pe(f"group{4 + n}", p))
                    if not only(p):
                        act.wait_ge(*e_pe("y7", p - 1))
                    e_act.mark(act.activation(ye[:, n, :], psum[4 + n][:, :], ACT.Copy), f"y{n}")
            experts(0)
            with act.Fori(1, NE // 2) as p:
                experts(p)
            act.wait_ge(*f_vec("var"))
            f_act.mark(act.activation(stat[:, 8:12].unsqueeze(2), stat[:, 0:8].rearrange("p (t two) -> p t two", two=2)[:, :, 1:2],
                                      ACT.Sqrt, bias=eps5), "root")

        @block.tensor
        def _(pe):
            pe.wait_ge(*ld_const("cols"))
            pe.wait_ge(*n_vec("xn"))
            for b in range(KB):
                for t in range(NT):
                    mm = pe.transpose(psum[b][:, t * P:(t + 1) * P], XR[:, t, b * P:(b + 1) * P], ident)
                n_pe.mark(mm, f"T{b}")
            pe.wait_ge(*ld_small("w"))
            pe.wait_ge(*n_act("AT6"))
            pe.wait_ge(*n_vec("AT7"))
            for k in range(KB):
                mm = pe.matmul(psum[3][0:40, :], wsm[:, k, :], AT[:, k, :], start=(k == 0), stop=(k == KB - 1))
            s_pe.mark(mm, "proj")

            def gemm_a(p):
                g_pe.start()
                for g in range(12):
                    slot = g // 4
                    if g <= 8:
                        pe.wait_ge(*ga_vec(f"w{g}", p))
                    if g >= 2:
                        pe.wait_ge(*g_act(f"e{g - 2}", p))
                    elif not (only(p) and p == 0):
                        pe.wait_ge(*g_act(f"e{g + 10}", p - 1))
                    for k in range(KB):
                        if only(p) and p == 0 and g == 0 and k % 2 == 0:
                            pe.wait_ge(*n_vec(f"ATl{k // 2}"))
                        if g == 8 and k and k % 2 == 0:
                            pe.wait_ge(*ga_vec(f"w{8 + k // 2}", p))
                        if g < 8:
                            lhs, rhs = (h_col[g % 4][:, k, :], ring[slot][:, k, g % 4 * P:(g % 4 + 1) * P]), (at_hi[:, k, :], AT[:, k, :])
                        else:
                            lhs = [x[:, k, (g - 8) * P:(g - 7) * P] for x in (at_hi, AT)]
                            rhs = (h_row[k // 2][:, k % 2, :], ring[slot][:, k, :])
                        mm = product(pe, psum[g % 2][:, :], lhs, rhs, k == 0, k == KB - 1)
                        if k == KB - 1:
                            g_pe.mark(mm, f"g{g}")
                        yield

            def chain_a(p, fill):
                c_pe.start()
                for j in range(2):
                    prev = (lambda s, what: s(what + "0", p)) if j else (lambda s, what: s(what + "1", p - 1))
                    noprev = only(p) and p == 0 and j == 0
                    fill(FILL["norm"] if j else 4 * FILL["conv"])
                    pe.wait_ge(*c_act(f"sqk{j}", p))
                    if not noprev:
                        pe.wait_ge(*prev(c_act, "vnew3_"))
                        pe.wait_ge(*prev(c_vec, f"S{NT - 2}_"))
                    else:
                        pe.wait_ge(*s_vec("begN"))
                        pe.wait_ge(*n_act("AT6"))
                        pe.wait_ge(*n_vec("AT7"))
                    pe.matmul(psum[2][:, :], ones, sq[:, 0, :], start=True, stop=True)
                    c_pe.mark(pe.matmul(psum[3][:, :], ones, sq[:, 1, :], start=True, stop=True), f"ss{j}")
                    if j == 0:
                        fill(4 * FILL["conv"])
                    fill(FILL["scores"])
                    pe.wait_ge(*c_vec(f"qT{j}", p))
                    pe.wait_ge(*c_vec(f"kT{j}", p))
                    pe.wait_ge(*c_pool(f"kbT{j}", p))
                    if not noprev:
                        pe.wait_ge(*prev(c_vec, "gate"))
                    for t in range(NT):
                        c = slice(t * P, (t + 1) * P)
                        mm = pe.matmul(psum[4][:, c], kT[:, c], kbT[:, c], start=True, stop=True)
                    c_pe.mark(mm, f"KK{j}")
                    for t in range(NT):
                        c = slice(t * P, (t + 1) * P)
                        mm = pe.matmul(psum[5][:, c], kT[:, c], qT[:, c], start=True, stop=True)
                    c_pe.mark(mm, f"KQ{j}")
                    pe.wait_ge(*c_act(f"rootq{j}", p))
                    for t in range(NT):
                        c = slice(t * P, (t + 1) * P)
                        mm = pe.transpose(psum[2][:, c], kT[:, c], ident)
                    c_pe.mark(mm, f"kN{j}")
                    pe.wait_ge(*c_act(f"silu{5 + 2 * j}", p))
                    if not noprev:
                        pe.wait_ge(*prev(c_vec, "oT1"))
                    for t in range(NT):
                        for d in range(2):
                            mm = pe.transpose(psum[3 if t < 2 else 7][:, (t % 2 * 2 + d) * P:(t % 2 * 2 + d + 1) * P],
                                              y[:, 4 + 2 * j + d, t * P:(t + 1) * P], ident)
                    c_pe.mark(mm, f"vN{j}")
                    fill(FILL["tokens"])
                    pe.wait_ge(*c_pool(f"NM0_{j}", p))
                    if not noprev:
                        pe.wait_ge(*prev(c_vec, "oT0"))
                    for t in range(NT):
                        mm = pe.transpose(psum[6][:, t * P:(t + 1) * P], NM[:, 0, t * P:(t + 1) * P], ident)
                    c_pe.mark(mm, f"P0_{j}")
                    fill(FILL["inverse"])
                    for s in range(1, LEVELS):
                        pe.wait_ge(*c_pool(f"NM{s}_{j}", p))
                        pe.wait_ge(*c_vec(f"X{s - 1}_{j}", p))
                        if s == 1:
                            pe.wait_ge(*c_vec(f"LT{j}", p))
                        for t in range(NT):
                            mm = pe.matmul(psum[4][:, t * P:(t + 1) * P], NM[:, s % 2, t * P:(t + 1) * P], X[:, t, :], start=True, stop=True)
                        c_pe.mark(mm, f"P{s}_{j}")
                        fill(FILL["level"][0])
                        pe.wait_ge(*c_act(f"P{s}_{j}", p))
                        pe.wait_ge(*c_vec(f"Y{s - 1}_{j}", p))
                        if s < LEVELS - 1:
                            if s == 1:
                                pe.wait_ge(*c_vec(f"ATT{j}", p))
                            for t in range(NT):
                                mm = pe.matmul(psum[5][:, t * P:(t + 1) * P], Y[:, t, :], PP[:, t, :], start=True, stop=True)
                            c_pe.mark(mm, f"X{s}_{j}")
                        for t in range(NT):
                            mm = pe.matmul(psum[6][:, t * P:(t + 1) * P], PP[:, t, :], Y[:, t, :], start=True, stop=True)
                        c_pe.mark(mm, f"Y{s}_{j}")
                        fill(FILL["level"][1])
                    pe.wait_ge(*c_vec(f"Y{LEVELS - 1}_{j}", p))
                    pe.wait_ge(*c_vec(f"kbeg{j}", p))
                    pe.wait_ge(*c_vec(f"vb{j}", p))
                    for t in range(NT):
                        mm = pe.matmul(psum[7][:, t * P:(t + 1) * P], kbeg[:, t, :], Y[:, t, :], start=True, stop=True)
                    c_pe.mark(mm, f"wT{j}")
                    fill(FILL["w"])
                    for t in range(NT):
                        c = slice(t * P, (t + 1) * P)
                        if t == 0:
                            pe.wait_ge(*c_vec(f"kd{j}", p))
                            pe.wait_ge(*c_pool(f"qeT{j}", p))
                        else:
                            pe.wait_ge(*c_act(f"vnew{t - 1}_{j}", p))
                        mm = pe.matmul(psum[2][:, 0:A_DV], Y[:, t, :], vb[:, t, :], start=True, stop=(t == 0))
                        if t:
                            if t == 1:
                                pe.wait_ge(*c_act(f"wT{j}", p))
                            pe.wait_ge(*c_vec(f"S{t - 1}_{j}", p) if t < NT else None)
                            mm = pe.matmul(psum[2][:, 0:A_DV], nwT[:, c], S, start=False, stop=True)
                        c_pe.mark(mm, f"V{t}_{j}")
                        fill(FILL["state"][0])
                        O = psum[4 + t // 2][:, t % 2 * A_DV:(t % 2 + 1) * A_DV]
                        if t:
                            pe.matmul(O, qeT[:, c], S, start=True, stop=False)
                        pe.wait_ge(*c_act(f"vnew{t}_{j}", p))
                        if t < NT - 1:
                            c_pe.mark(pe.matmul(psum[3][:, 0:A_DV], kdN[:, t, :], vnew, start=True, stop=True), f"S{t}_{j}")
                        c_pe.mark(pe.matmul(O, ATT[:, t, :], vnew, start=(t == 0), stop=True), f"O{t}{j}")
                        fill(FILL["state"][1])
                    fill(FILL["out"])
                    pe.wait_ge(*c_vec(f"gate{j}", p))
                    pe.wait_ge(*c_act(f"wT{j}", p))
                    for d in range(2):
                        for t in range(NT):
                            mm = pe.transpose(psum[6 + d][:, t * P:(t + 1) * P], oN[:, t, d * P:(d + 1) * P], ident)
                        c_pe.mark(mm, f"oT{d}{j}")
                fill(99)

            steps = gemm_a(0)
            for _ in range(4 * KB):
                next(steps)
            pe.wait_ge(*s_act("eg"))
            pe.wait_ge(*s_vec("gcum"))
            for t in range(NT):
                mm = pe.transpose(psum[2][:, t * P:(t + 1) * P], ST[:, t * P:(t + 1) * P], ident)
            s_pe.mark(mm, "stT")
            for _ in steps:
                pass

            def with_gemm(p):
                steps = gemm_a(p)

                def fill(n):
                    for _ in range(n):
                        next(steps, None)
                chain_a(p - 1, fill)

            with_gemm(1)
            with pe.Fori(2, PAIRS) as p:
                with_gemm(p)
            def gemm_b(h, groups):
                for _ in products_b(h, groups):
                    pass

            def products_b(h, groups):
                for g in groups:
                    slot = g // 4
                    if g < 4 or g % 4 == 0:
                        pe.wait_ge(*bs_vec(f"w{g}", h))
                    if g >= 2:
                        pe.wait_ge(*bg_act(f"e{g - 2}", h))
                    elif not (only(h) and h == 0):
                        pe.wait_ge(*bg_act(f"e{g + 10}", h - 1))
                    else:
                        pe.wait_ge(*g_act(f"e{g + 10}", PAIRS - 1))
                    for k in range(KB):
                        if g % 4 == 0 and g and k and k % 2 == 0:
                            pe.wait_ge(*bs_vec(f"w{g + k // 2}", h))
                        if g < 4:
                            lhs, rhs = (h_col[g][:, k, :], ring[slot][:, k, g * P:(g + 1) * P]), (at_hi[:, k, :], AT[:, k, :])
                        else:
                            lhs = [x[:, k, g % 4 * P:(g % 4 + 1) * P] for x in (at_hi, AT)]
                            rhs = (h_row[k // 2][:, k % 2, :], ring[slot][:, k, :])
                        mm = product(pe, psum[g % 2][:, :], lhs, rhs, k == 0, k == KB - 1)
                        if k == KB - 1:
                            bg_pe.mark(mm, f"g{g}")
                        yield

            def scores_b(h):
                b_pe.start()
                pe.wait_ge(*b_rope("ropeq", h))
                pe.wait_ge(*b_pool("ropek", h))
                pe.wait_ge(*(b_vec("oT3", h - 1) if not (only(h) and h == 0) else c_vec("oT11", PAIRS - 1)))
                for m in range(NT):
                    for k in range(2):
                        mm = pe.matmul(psum[2 + m][:, m * P:], qkT[:, 2 + k, m * P:(m + 1) * P], qkT[:, k, m * P:],
                                       start=(k == 0), stop=(k == 1))
                    b_pe.mark(mm, f"S{m}")

            def values_b(h):
                for t in range(NT):
                    pe.wait_ge(*b_vec("PT3" if t == 3 else f"PT{max(t, 1)}", h))
                    if t == 0:
                        pe.wait_ge(*bg_act("e7", h))
                    for m in range(t + 1):
                        mm = pe.matmul(psum[(6, 7, 2, 3)[t]][:, :], PT[:, m, t * P:(t + 1) * P], bv[:, m, :], start=(m == 0), stop=(m == t))
                    b_pe.mark(mm, f"O{t}")

            def turn_b(h):
                pe.wait_ge(*b_vec("gate", h))
                for d in range(4):
                    for t in range(NT):
                        mm = pe.transpose(psum[4 + d][:, t * P:(t + 1) * P], bo[:, t, d * P:(d + 1) * P], ident)
                    b_pe.mark(mm, f"oT{d}")

            bg_pe.start()

            def first_b():
                yield from products_b(0, range(8))
                for _ in range(PAUSE):
                    yield
                yield from products_b(0, range(8, 12))
            steps_b = first_b()

            def fill_b(n):
                for _ in range(n):
                    next(steps_b, None)
            chain_a(PAIRS - 1, fill_b)

            def step_b(h):
                bg_pe.start()
                scores_b(h - 1)
                gemm_b(h, range(4))
                values_b(h - 1)
                gemm_b(h, range(4, 8))
                turn_b(h - 1)
                gemm_b(h, range(8, 12))
            with pe.Fori(1, B_HEADS) as h:
                step_b(h)
            scores_b(B_HEADS - 1)
            values_b(B_HEADS - 1)
            turn_b(B_HEADS - 1)

            def merge(x, c):
                later = not (only(c) and c == 0)
                m_pe[x].start()
                for b in range(4):
                    pe.wait_ge(*m_vec[x](f"w{b}", c))
                    if b >= 2:
                        pe.wait_ge(*m_act[x](f"sg{b - 2}", c))
                    elif later:
                        pe.wait_ge(*m_act[x](f"sg{b + 2}", c - 1))
                    else:
                        pe.wait_ge(*(bg_act(f"e{10 + b}", B_HEADS - 1) if x == 0 else m_act[0](f"sg{b + 2}", 1)))
                    for k in range(KB):
                        mm = product(pe, psum[b % 2][:, :], (h_col[b][:, k, :], ring[0][:, k, b * P:(b + 1) * P]), (at_hi[:, k, :], AT[:, k, :]),
                                     k == 0, k == KB - 1)
                    m_pe[x].mark(mm, f"gate{b}")
                for b in range(4):
                    if later:
                        pe.wait_ge(*m_vec[x](f"mix{b}", c - 1))
                    else:
                        pe.wait_ge(*(b_vec("oT3", B_HEADS - 1) if x == 0 else m_vec[0](f"mix{b}", 1)))
                    for half, name in enumerate(("lo", "y")):
                        pe.wait_ge(*m_vec[x](f"w{4 + 2 * b + half}", c))
                        for k in range(KB):
                            block = half * 8 + k
                            if not later and b == 0 and k % 2 == 0:
                                pe.wait_ge(*ot_vec[x](f"o{block // 2}"))
                            mm = product(pe, psum[2 + b][:, :], (h_col[half + 2 * (b % 2)][:, k, :], ring[1 + half][:, k, b * P:(b + 1) * P]),
                                         (oT_hi[:, block, :], oT[:, block, :]), block == 0, block == 15)
                        m_pe[x].mark(mm, f"{name}{b}")
            merge(0, 0)
            with pe.Fori(1, 2) as c:
                merge(0, c)
            merge(1, 0)
            with pe.Fori(1, 2) as c:
                merge(1, c)

            for n in range(8):
                k, c = n // 2 * 2, n % 2
                pe.wait_ge(*o_vec(f"w{n}"))
                for t in range(NT):
                    for a in range(2):
                        mm = product(pe, psum[2 * t + c][:, :], [x[:, k + a, t * P:(t + 1) * P] for x in (mix_hi, mixT)],
                                     (h_row[n % 4][:, a, :], ring[c][:, k + a, :]), k + a == 0, k + a == KB - 1)
                    if n >= 6:
                        o_pe.mark(mm, f"m{t}{c}")
                if n < 6:
                    o_pe.mark(mm, f"p{n}")

            def turn(pe_s, src, bank, ready):
                for t in range(NT):
                    pe.wait_ge(*ready(t))
                    for q in range(2):
                        for b in range(4):
                            mm = pe.transpose(psum[bank(t, q)][:, b * P:(b + 1) * P], src[:, t, (4 * q + b) * P:(4 * q + b + 1) * P], ident)
                        pe_s.mark(mm, f"T{t}{q}")
            turn(o_pe, o_hN, lambda t, q: 2 * t + q, lambda t: o_vec(f"hn{t}"))

            def mlp_up(i):
                u_pe.start()
                for g in range(16):
                    pe.wait_ge(*u_vec(f"w{g}", i))
                    if g >= 4:
                        pe.wait_ge(*u_vec(f"relu{g - 4}", i))
                    elif not (only(i) and i == 0):
                        pe.wait_ge(*u_vec(f"relu{g + 12}", i - 1))
                    for k in range(KB):
                        if only(i) and g == 0 and k % 2 == 0:
                            pe.wait_ge(*o_vec(f"ATl{k // 2}"))
                        mm = product(pe, psum[g % 4][:, :], (h_col[g % 4][:, k, :], ring[g // 4 % 2][:, k, g % 4 * P:(g % 4 + 1) * P]),
                                     (at_hi[:, k, :], AT[:, k, :]), k == 0, k == KB - 1)
                    u_pe.mark(mm, f"g{g}")
            mlp_up(0)
            with pe.Fori(1, 2) as i:
                mlp_up(i)

            def mlp_down(c):
                d_pe.start()
                if only(c):
                    pe.wait_ge(*u_vec("relu15", 1))
                for n in range(16):
                    pe.wait_ge(*dn_vec(f"ff{n}", c))
                    for t in range(NT):
                        for a in range(2):
                            mm = product(pe, ps_all[:, bass.ds(c * 4 + t, 1), :].rearrange("p a n -> p (a n)"),
                                         [x[:, n % 4, a, t * P:(t + 1) * P] for x in (ff_hi, ff_lo)],
                                         (h_row[n % 4][:, a, :], ring[n // 4 % 2][:, n % 4 * 2 + a, :]), n + a == 0, n == 15 and a == 1)
                        if n == 15:
                            d_pe.mark(mm, f"m{t}")
                    if n < 15:
                        d_pe.mark(mm, f"p{n}")
            mlp_down(0)
            with pe.Fori(1, 2) as c:
                mlp_down(c)

            turn(t2_pe, XR, lambda t, q: 4 * q + t, lambda t: d_vec(f"x{t}"))

            pe.wait_ge(*mem_ld("mem"))
            pe.wait_ge(*t2_vec("AT31"))
            for q in range(4):
                for k in range(2):
                    for m in range(2):
                        mm = pe.transpose(psum[q][:, (2 * k + m) * P:(2 * k + m + 1) * P], memN[:, m, (2 * q + k) * P:(2 * q + k + 1) * P], ident)
                p_pe.mark(mm, f"memT{q}")

            def project(groups):
                for g in groups:
                    n = next(n for n, (of, _) in enumerate(slots2) if g in of)
                    slot, at, wide = n % 2, g - slots2[n][0][0], slots2[n][1]
                    x_hi, x = (mem_hi, memT) if g < 6 else (at_hi, AT)
                    if not wide or at == 0:
                        pe.wait_ge(*p_vec(f"w{4 * n + at}"))
                    if g >= 2:
                        pe.wait_ge(*p_act(f"e{g - 2}"))
                    N = 256 if g < 4 or g >= 26 else 512
                    for k in range(KB):
                        if g in (0, 6) and k % 2 == 0:
                            pe.wait_ge(*p_vec(("ml" if g == 0 else "ATl") + str(k // 2)))
                        if wide and at == 0 and k and k % 2 == 0:
                            pe.wait_ge(*p_vec(f"w{4 * n + k // 2}"))
                        if wide:
                            lhs = [v[:, k, at * P:(at + 1) * P] for v in (x_hi, x)]
                            rhs = (h_row[k // 2][:, k % 2, 0:N], ring[slot][:, k, 0:N])
                        else:
                            lhs = (h_col[at][:, k, :], ring[slot][:, k, at * P:(at + 1) * P])
                            rhs = (x_hi[:, k, :], x[:, k, :])
                        mm = product(pe, psum[6 + g % 2][:, 0:N], lhs, rhs, k == 0, k == KB - 1)
                    p_pe.mark(mm, f"g{g}")

            def attend_body(kind, b):
                pe_s, act_s, vec_s, pool_s = at_pe[kind], at_act[kind], at_vec[kind], at_pool[kind]
                pe_s.start()
                units = 4 if kind == "m" else 8
                nk = 512 if kind == "g" else 256
                flat = lambda x: x.rearrange("p a n -> p (a n)")
                for n in range(units + 3):
                    if n < units:
                        e, u = n // 4, n % 4
                        if u == 0:
                            pe.wait_ge(*pool_s(f"q{e}", b))
                        if n >= 3:
                            pe.wait_ge(*(vec_s(f"s{n - 3}", b) if kind == "n" else act_s(f"ex{n - 3}", b)))
                        elif n == 0 and only(b):
                            if kind == "n":
                                pe.wait_ge(*p_act("e21"))
                            else:
                                pe.wait_ge(*(at_act["n"]("ex7", 3) if kind == "m" else at_act["m"]("ex3", 3)))
                                if kind == "g":
                                    pe.wait_ge(*r_act("kT1"))
                        if kind == "n":
                            start = (0, 8, 24, 32)[u]
                            lhsT = qz[:, e, u * P:(u + 1) * P]
                            rhs = flat(knT[:, bass.ds(b, 1), :]).rearrange("p (r c) -> p r c", r=8)[:, :, start:start + 32]
                            o = psum[n % 3][:, 0:nk].rearrange("p (r c) -> p r c", r=8)
                        elif kind == "m":
                            lhsT, rhs, o = qst[:, u * P:(u + 1) * P], flat(mkT[:, bass.ds(b, 1), :]), psum[n % 3][:, 0:nk]
                        else:
                            lhsT, rhs, o = qz[:, e, u * P:(u + 1) * P], flat(kgT[:, bass.ds(b, 1), :]), psum[n % 3][:, 0:nk]
                        pe_s.mark(pe.matmul(o, lhsT, rhs, start=True, stop=True), f"S{n}")
                    if 2 <= n < units + 2:
                        m = n - 2
                        pe.wait_ge(*vec_s(f"n{m}", b))
                        if m >= 2:
                            pe.wait_ge(*act_s(f"pT{m - 2}", b))
                        for k in range(nk // P):
                            mm = pe.transpose(psum[3 + m % 2][:, k * P:(k + 1) * P], pr[:, m % 3, k * P:(k + 1) * P], ident)
                        pe_s.mark(mm, f"T{m}")
                    if n >= 3:
                        m = n - 3
                        e, u = m // 4, m % 4
                        pe.wait_ge(*act_s(f"pT{m}", b))
                        if m == 0:
                            pe.wait_ge(*pool_s("v", b))
                            if not only(b):
                                pe.wait_ge(*vec_s("y", b - 1))
                            elif kind != "n":
                                pe.wait_ge(*at_vec["n" if kind == "m" else "m"]("y", 3))
                        for k in range(nk // P):
                            if kind == "m":
                                o, lhsT = psum[5][:, u * P:(u + 1) * P], vst[:, k, :]
                            else:
                                o = psum[5][64 * e:64 * e + 64, u * P:(u + 1) * P]
                                lhsT = vst[:, 2 * u + k, 64 * e:64 * e + 64] if kind == "n" else vst[:, k, 0:64]
                            mm = pe.matmul(o, lhsT, pT[:, m % 2, k * P:(k + 1) * P], start=(k == 0), stop=(k == nk // P - 1))
                        pe_s.mark(mm, f"AV{m}")

            def attend(kind):
                attend_body(kind, 0)
                with pe.Fori(1, 4) as b:
                    attend_body(kind, b)

            project(range(22))
            attend("n")
            project(range(22, 30))
            attend("m")
            for n in range(6):
                if n == 0:
                    pe.wait_ge(*r_vec("rope3"))
                if n == 4:
                    pe.wait_ge(*r_pool("dup"))
                if n >= 2:
                    pe.wait_ge(*r_act(f"qT{n - 2}"))
                else:
                    pe.wait_ge(*p_act(f"e{28 + n}"))
                for t in range(NT):
                    src = ro[:, t, n * P:(n + 1) * P] if n < 4 else kdup[:, t, n - 4, :]
                    mm = pe.transpose(psum[6 + n % 2][:, t * P:(t + 1) * P], src, ident)
                r_pe.mark(mm, f"T{n}")
            attend("g")

            def merge2(c):
                mg_pe.start()
                for g, b, part in events2:
                    if part == "gate":
                        pe.wait_ge(*mg_vec(f"w{6 * g + b}", c))
                        if g:
                            pe.wait_ge(*mg_act(f"sg{g - 1}{b}", c))
                        elif not only(c):
                            pe.wait_ge(*mg_act(f"sg2{b}", c - 1))
                        elif b == 0:
                            pe.wait_ge(*at_act["g"]("pT7", 3))
                        for k in range(KB):
                            mm = product(pe, psum[b][:, :], [x[:, k, :] for x in piece3(6 * g + b)[::-1]],
                                         (at_hi[:, k, :], AT[:, k, :]), k == 0, k == KB - 1)
                    else:
                        pe.wait_ge(*mg_vec(f"w{6 * g + 4 + b // 2}", c))
                        if g:
                            pe.wait_ge(*mg_vec(f"m{g - 1}{b}", c))
                        elif not only(c):
                            pe.wait_ge(*mg_vec(f"m2{b}", c - 1))
                        elif b == 0:
                            pe.wait_ge(*at_vec["g"]("y", 3))
                        w_lo, w_hi = piece3(6 * g + 4 + b // 2)
                        for k in range(4):
                            if only(c) and b == 0 and k % 2 == 0:
                                pe.wait_ge(*y_vec(f"y{2 * g + k // 2}"))
                            mm = product(pe, psum[4 + b][:, :], [x[:, k, b % 2 * P:(b % 2 + 1) * P] for x in (w_hi, w_lo)],
                                         (yT_hi[:, 4 * g + k, :], yT[:, 4 * g + k, :]), k == 0, k == 3)
                    mg_pe.mark(mm, f"{part}{g}{b}")
            merge2(0)
            with pe.Fori(1, 2) as c:
                merge2(c)
            for n in range(8):
                k, c = n // 2 * 2, n % 2
                pe.wait_ge(*l_vec(f"w{n}"))
                for t in range(NT):
                    for a in range(2):
                        mm = product(pe, psum[2 * t + c][:, :], [x[:, k + a, t * P:(t + 1) * P] for x in (mg_hi, mgT)],
                                     (h_row[n % 4][:, a, :], ring[c][:, k + a, :]), k + a == 0, k + a == KB - 1)
                    if n >= 6:
                        l_pe.mark(mm, f"m{t}{c}")
                if n < 6:
                    l_pe.mark(mm, f"p{n}")
            turn(q_pe, XR, lambda t, q: 2 * t + q, lambda t: l_vec(f"x{t}"))
            pe.wait_ge(*q_ld("wr"))
            pe.wait_ge(*q_vec("AT31"))
            for t in range(NT):
                for k in range(KB):
                    mm = pe.matmul(psum[0][:, t * NE:(t + 1) * NE], AT[:, k, t * P:(t + 1) * P], wr[:, k, :], start=(k == 0), stop=(k == KB - 1))
            q_pe.mark(mm, "logits")
            pe.wait_ge(*q_vec("aff"))
            for t in range(NT):
                mm = pe.transpose(psum[1][0:NE, t * P:(t + 1) * P], affN[:, t, :], ident)
            q_pe.mark(mm, "affT")
            pe.wait_ge(*q_vec("pos"))
            for t in range(NT):
                mm = pe.transpose(psum[2][:, t * NE:(t + 1) * NE], cum[0:NE, t * P:(t + 1) * P], ident[0:NE, 0:NE])
            q_pe.mark(mm, "posN")

            def experts(p):
                e_pe.start()
                pe.wait_ge(*e_vec("SP", p))
                for b in range(KB):
                    if b % 4 == 0:
                        if not only(p):
                            pe.wait_ge(*e_vec(f"acc{4 + b // 4}", p - 1))
                    for t in range(NT):
                        mm = pe.matmul(psum[b // 4][:, b % 4 * P:(b % 4 + 1) * P], XR[:, t, b * P:(b + 1) * P], SP[:, t, :], start=(t == 0), stop=(t == NT - 1))
                    if b % 4 == 3:
                        e_pe.mark(mm, f"x{b // 4}")
                pe.wait_ge(*e_vec("SG", p))
                if not only(p):
                    pe.wait_ge(*e_vec("acc6", p - 1))
                for t in range(NT):
                    mm = pe.transpose(psum[2][:, t * P:(t + 1) * P], SG[:, t, :], ident)
                e_pe.mark(mm, "SGT")
                for q in range(4):
                    for e in range(2):
                        pe.wait_ge(*e_w[(2 * q + e) % 6](f"w{(2 * q + e) // 6}", p))
                    if q == 0:
                        pe.wait_ge(*e_act("x1", p))
                    if not only(p):
                        pe.wait_ge(*((e_act("a1", p - 1), e_act("y0", p - 1), e_act("y1", p - 1), e_vec("acc7", p - 1))[q]))
                    for k in range(KB):
                        for e in range(2):
                            mm = pe.matmul(psum[3 + q][64 * e:64 * e + 64, :], xst[:, k, 64 * e:64 * e + 64], eslot[(2 * q + e) % 6][:, k, :],
                                           start=(k == 0), stop=(k == KB - 1))
                    e_pe.mark(mm, f"group{q}")
                for f in range(2):
                    pe.wait_ge(*e_vec(f"ga{f}", p))
                    for b in range(4):
                        mm = pe.transpose(psum[(7, 3)[f]][:, b * P:(b + 1) * P], ga[:, f, b * P:(b + 1) * P], ident)
                    e_pe.mark(mm, f"a{f}")
                for n in range(2):
                    q = 4 + n
                    for e in range(2):
                        pe.wait_ge(*e_w[(2 * q + e) % 6](f"w{(2 * q + e) // 6}", p))
                    if n == 0:
                        pe.wait_ge(*e_act("a1", p))
                    for k in range(KB):
                        for e in range(2):
                            mm = pe.matmul(psum[4 + n][64 * e:64 * e + 64, :], actT[:, k, 64 * e:64 * e + 64], eslot[(2 * q + e) % 6][:, k, :],
                                           start=(k == 0), stop=(k == KB - 1))
                    e_pe.mark(mm, f"group{q}")
                for m in range(8):
                    t, n = m // 2, m % 2
                    if m < 2:
                        pe.wait_ge(*e_act(f"y{n}", p))
                    if m == 0:
                        pe.wait_ge(*e_vec("SGT", p))
                    if m >= 4:
                        pe.wait_ge(*e_vec(f"acc{m - 4}", p))
                    e_pe.mark(pe.matmul(psum[(0, 1, 2, 6)[m % 4]][:, :], SGT[:, t * P:(t + 1) * P], ye[:, n, :], start=True, stop=True), f"y{m}")
            experts(0)
            with pe.Fori(1, NE // 2) as p:
                experts(p)

        @block.vector
        def _(dve):
            dve.wait_ge(*n_act("rms"))
            n_vec.link(dve, dve.reciprocal(stat[:, 4:8], stat[:, 4:8]))
            for t in range(NT):
                i = dve.tensor_scalar(XR[:, t, :], XR[:, t, :], stat[:, 4 + t:5 + t], None, ALU.mult)
            n_vec.mark(i, "xn")
            for b in range(1, KB, 2):
                dve.wait_ge(*n_pe(f"T{b}"))
                n_vec.mark(dve.tensor_scalar(AT[:, b, :], psum[b][:, :], cols[:, V_MIXPRE + b:V_MIXPRE + b + 1], None, ALU.mult), f"AT{b}")
            dve.wait_ge(*s_pe("proj"))
            for q in range(4):
                dve.wait_ge(*n_act(f"ATh{q}"))
                a = AT[:, 2 * q:2 * q + 2, :]
                low(dve, n_vec, a, a, at_hi[:, 2 * q:2 * q + 2, :], f"ATl{q}")
            def split_a(p, n):
                dve.wait_ge(*g_act(f"w{n}", p))
                w, hi = (ring[n // 4][:, :, n % 4 * P:(n % 4 + 1) * P], h_col[n % 4]) if n < 8 else (ring[2][:, n % 4 * 2:n % 4 * 2 + 2, :], h_row[n % 4])
                low(dve, ga_vec, w, w, hi, f"w{n}")
            ga_vec.start()
            for n in range(4):
                split_a(0, n)
            dve.wait_ge(*s_act("ln"))
            s_vec.link(dve, dve.scalar_tensor_tensor(u8[0:8, 0, :], u8[0:8, 0, :], 0.0, u8[0:8, 1, :], ALU.max, ALU.add))
            s_vec.link(dve, dve.tensor_scalar(u8[0:8, 0, :], u8[0:8, 0, :], stat[0:8, 8:9], -1.0, ALU.mult, ALU.mult))
            dve.wait_ge(*z_pool("ST"))
            for t in range(NT):
                c = slice(t * P, (t + 1) * P)
                i = dve.tensor_tensor_scan(ST[0:8, c], ones[0:8, :], u8[0:8, 0, c], 0.0, ALU.mult, ALU.add)
            s_vec.mark(i, "gcum")
            dve.wait_ge(*s_vec("gcum"))
            for t in range(NT):
                c = slice(t * P, (t + 1) * P)
                i = dve.tensor_scalar(u8[0:8, 2, c], ST[0:8, c], ST[0:8, (t + 1) * P - 1:(t + 1) * P], -1.0, ALU.subtract, ALU.mult)
            s_vec.mark(i, "kdiff")

            for n in range(4, 8):
                split_a(0, n)
            dve.wait_ge(*s_pe("stT"))
            s_vec.link(dve, dve.tensor_copy(stN, psum[2][:, :].rearrange("p (t c) -> p t c", t=NT)))
            s_vec.mark(dve.tensor_tensor(begN, stN[:, :, 32:40], stN[:, :, 96:104], ALU.mult), "begN")
            for n in range(8, 12):
                split_a(0, n)

            def chain_a(p, fill):
                c_vec.start()
                first = only(p) and p == 0
                for b in range(6):
                    blk = (p * 2 + b) if b < 2 else (p * 2 + 8 + b - 2) if b < 4 else (p * 4 + 16 + b - 4)
                    dve.wait_ge(*c_act(f"tap{b}", p))
                    for k in range(2, -1, -1):
                        i = dve.scalar_tensor_tensor(y[:, b, :], pre[:, b, k:k + 512], cols[:, bass.ds(blk * 4 + V_CONV + k, 1)],
                                                     y[:, b, :], ALU.mult, ALU.add)
                        if k:
                            c_vec.link(dve, i, p)
                    c_vec.mark(i, f"conv{b}")
                    fill(FILL["conv"])
                fill(2 * FILL["conv"])
                for j in range(2):
                    h = p * 2 + j
                    prev = (lambda s, what: s(what + "0", p)) if j else (lambda s, what: s(what + "1", p - 1))
                    noprev = first and j == 0

                    def per_token(col):
                        return stN[:, :, bass.ds(h + col, 1)]
                    if j:
                        fill(FILL["norm"])
                    dve.wait_ge(*c_act(f"rootk{j}", p))
                    if not noprev:
                        dve.wait_ge(*prev(c_pe, "kN"))
                        dve.wait_ge(*prev(c_pool, "qeT"))
                    c_vec.mark(dve.tensor_tensor(kT, y[:, 2 + j, :], rinv[:, 1, :], ALU.mult), f"kT{j}")
                    dve.wait_ge(*c_act(f"rootq{j}", p))
                    c_vec.mark(dve.scalar_tensor_tensor(qT, y[:, j, :], float(A_DK ** -0.5), rinv[:, 0, :], ALU.mult, ALU.mult), f"qT{j}")
                    dve.wait_ge(*a_bc[j]("r2", p))
                    if not noprev:
                        dve.wait_ge(*prev(c_pe, "oT1"))
                    for t in range(NT):
                        i = dve.tensor_scalar(D[:, t, :], bc[:, j, 0, t * P:(t + 1) * P], stN[:, t, bass.ds(h, 1)], 0.0,
                                              ALU.subtract, ALU.min)
                    c_vec.mark(i, f"Dpre{j}")
                    dve.wait_ge(*c_pe(f"KK{j}", p))
                    dve.wait_ge(*c_pool(f"D{j}", p))
                    v4 = lambda b: psum[b][:, :].rearrange("p (t c) -> p t c", t=NT)
                    c_vec.mark(dve.tensor_tensor(LT, v4(4), D, ALU.mult), f"LT{j}")
                    dve.wait_ge(*c_pe(f"KQ{j}", p))
                    if not noprev:
                        dve.wait_ge(*prev(c_pe, "O3"))
                    c_vec.mark(dve.tensor_tensor(ATT, v4(5), D, ALU.mult), f"ATT{j}")
                    fill(FILL["scores"])
                    dve.wait_ge(*c_pe(f"kN{j}", p))
                    dve.wait_ge(*c_pe(f"ss{j}", p))
                    c_vec.mark(dve.tensor_tensor(kbeg, v4(2), begN[:, :, bass.ds(h, 1)].broadcast_to([P, NT, P]), ALU.mult), f"kbeg{j}")
                    c_vec.mark(dve.tensor_tensor(kdN, v4(2), per_token(64).broadcast_to([P, NT, P]), ALU.mult), f"kd{j}")
                    dve.wait_ge(*c_pe(f"vN{j}", p))
                    for q in range(2):
                        i = dve.tensor_tensor(vb[:, 2 * q:2 * q + 2, :], psum[3 + 4 * q][:, :].rearrange("p (t c) -> p t c", t=2),
                                              stN[:, 2 * q:2 * q + 2, bass.ds(h + 32, 1)].broadcast_to([P, 2, A_DV]), ALU.mult)
                    c_vec.mark(i, f"vb{j}")
                    eye = ident.unsqueeze(1).broadcast_to([P, NT, P])
                    dve.wait_ge(*c_pool(f"NM0_{j}", p))
                    if not noprev:
                        dve.wait_ge(*prev(c_pe, "V3_"))
                    c_vec.mark(dve.tensor_tensor(Y, NM[:, 0, :].rearrange("p (t c) -> p t c", t=NT), eye, ALU.add), f"Y0_{j}")
                    dve.wait_ge(*c_pe(f"P0_{j}", p))
                    if not noprev:
                        dve.wait_ge(*(oa_st[0]("o", p) if j else oa_st[1]("o", p - 1)))
                    c_vec.mark(dve.tensor_tensor(X, v4(6), eye, ALU.add), f"X0_{j}")
                    fill(FILL["tokens"] + FILL["inverse"])
                    for s in range(1, LEVELS):
                        if s < LEVELS - 1:
                            dve.wait_ge(*c_pe(f"X{s}_{j}", p))
                            dve.wait_ge(*c_vec(f"X{s - 1}_{j}", p))
                            c_vec.mark(dve.tensor_tensor(X, v4(5), X, ALU.add), f"X{s}_{j}")
                        dve.wait_ge(*c_pe(f"Y{s}_{j}", p))
                        dve.wait_ge(*c_vec(f"Y{s - 1}_{j}", p))
                        c_vec.mark(dve.tensor_tensor(Y, v4(6), Y, ALU.add), f"Y{s}_{j}")
                        fill(sum(FILL["level"]))
                    fill(FILL["w"])
                    for t in range(NT - 1):
                        dve.wait_ge(*c_pe(f"S{t}_{j}", p))
                        if t == 0:
                            if not noprev:
                                dve.wait_ge(*prev(c_pe, "O3"))
                            i = dve.tensor_copy(S, psum[3][:, 0:A_DV])
                        else:
                            dve.wait_ge(*c_pe(f"O{t}{j}", p))
                            dve.wait_ge(*c_vec(f"S{t - 1}_{j}", p))
                            i = dve.scalar_tensor_tensor(S, S, bc[:, j, 2, (t + 1) * P - 1:(t + 1) * P], psum[3][:, 0:A_DV],
                                                         ALU.mult, ALU.add)
                        c_vec.mark(i, f"S{t}_{j}" if t < NT - 2 else f"S{t}_{j}")
                        fill(sum(FILL["state"]))
                    fill(sum(FILL["state"]))
                    dve.wait_ge(*c_act(f"orms{j}", p))
                    c_vec.link(dve, dve.reciprocal(stat[:, 4:8], stat[:, 4:8]), p)
                    for t in range(NT):
                        i = dve.scalar_tensor_tensor(oN[:, t, :], psum[4 + t // 2][:, t % 2 * A_DV:(t % 2 + 1) * A_DV],
                                                     stat[:, 4 + t:5 + t], zs[:, t, j * A_DV:(j + 1) * A_DV], ALU.mult, ALU.mult)
                    c_vec.mark(i, f"gate{j}")
                    for d in range(2):
                        dve.wait_ge(*c_pe(f"oT{d}{j}", p))
                        c_vec.mark(dve.tensor_scalar(o_st[:, d:d + 1, :], psum[6 + d][:, :].unsqueeze(1),
                                                     cols[:, V_NA + d:V_NA + d + 1], None, ALU.mult), f"oT{d}{j}")

                    fill(FILL["out"])
                fill(99)

            def with_splits(p):
                ga_vec.start()
                for n in range(4):
                    split_a(p, n)
                at = [0]

                def fill(n):
                    for m in range(at[0], min(at[0] + n, 96)):
                        if m % KB == KB - 1 and m // KB < 8:
                            split_a(p, m // KB + 4)
                    at[0] += n
                chain_a(p - 1, fill)

            with_splits(1)
            with dve.Fori(2, PAIRS) as p:
                with_splits(p)
            def rope_q(h):
                dve.wait_ge(*bg_act("e1", h))
                if only(h) and h == 0:
                    dve.wait_ge(*b_tab("decay"))
                else:
                    dve.wait_ge(*b_pe("S3", h - 1))
                for o, (c0, c1, op) in enumerate(((cosT, sinT, ALU.subtract), (sinT, cosT, ALU.add))):
                    dve.tensor_tensor(rt[:, 0, :], qkr[:, 0, :], c0, ALU.mult)
                    b_rope.link(dve, dve.tensor_tensor(rt[:, 1, :], qkr[:, 1, :], c1, ALU.mult), h)
                    i = dve.tensor_tensor(qkT[:, o, :], rt[:, 0, :], rt[:, 1, :], op)
                    if o == 0:
                        b_rope.link(dve, i, h)
                b_rope.mark(i, "ropeq")

            def split_b(h, n):
                dve.wait_ge(*bg_act(f"w{n}", h))
                w, hi = (ring[0][:, :, n * P:(n + 1) * P], h_col[n]) if n < 4 else (ring[n // 4][:, n % 4 * 2:n % 4 * 2 + 2, :], h_row[n % 4])
                low(dve, bs_vec, w, w, hi, f"w{n}")

            def decay_b(h):
                b_vec.start()
                for m in range(NT):
                    dve.wait_ge(*b_pe(f"S{m}", h))
                    b_vec.mark(dve.tensor_tensor(PT[:, m, m * P:], psum[2 + m][:, m * P:],
                                                 dmask[:, bass.ds(h, 1), 0:512 - m * P].rearrange("p a n -> p (a n)"), ALU.mult), f"PT{m}")

            def gate_b(h):
                dve.wait_ge(*b_act("orms", h))
                b_vec.link(dve, dve.reciprocal(stat[:, 4:8], stat[:, 4:8]), h)
                dve.wait_ge(*bg_act("e11", h))
                for t in range(NT):
                    i = dve.scalar_tensor_tensor(bo[:, t, :], psum[(6, 7, 2, 3)[t]][:, :], stat[:, 4 + t:5 + t], bg[:, t, :], ALU.mult, ALU.mult)
                b_vec.mark(i, "gate")

            def out_b(h):
                if not only(h):
                    dve.wait_ge(*ob_st_s("o", h - 1))
                for d in range(4):
                    dve.wait_ge(*b_pe(f"oT{d}", h))
                    b_vec.mark(dve.tensor_scalar(ob_st[:, d, :], psum[4 + d][:, :],
                                                 cols[:, bass.ds(h * 4 + V_NB + d, 1)], None, ALU.mult), f"oT{d}")

            def step_b(h):
                bs_vec.start()
                b_rope.start()
                for n in range(4):
                    split_b(h, n)
                decay_b(h - 1)
                for n in range(4, 8):
                    split_b(h, n)
                rope_q(h)
                gate_b(h - 1)
                for n in range(8, 12):
                    split_b(h, n)
                out_b(h - 1)
            bs_vec.start()
            b_rope.start()
            for n in range(4):
                split_b(0, n)

            def ended_b(g):
                for n in pieces_b(g):
                    split_b(0, n)
            chain_a(PAIRS - 1, over_chain(ended_b))
            rope_q(0)
            with dve.Fori(1, B_HEADS) as h:
                step_b(h)
            decay_b(B_HEADS - 1)
            gate_b(B_HEADS - 1)
            out_b(B_HEADS - 1)

            def merge(x, c):
                m_vec[x].start()

                def split(n):
                    dve.wait_ge(*m_act[x](f"w{n}", c))
                    slot, q = (0, n) if n < 4 else (1 + n % 2, (n - 4) // 2)
                    w = ring[slot][:, :, q * P:(q + 1) * P]
                    low(dve, m_vec[x], w, w, h_col[n % 4], f"w{n}")
                for n in range(8):
                    split(n)
                if only(c) and c == 0:
                    for k in range(8):
                        dve.wait_ge(*ot_act[x](f"o{k}"))
                        o = oT[:, 2 * k:2 * k + 2, :]
                        low(dve, ot_vec[x], o, o, oT_hi[:, 2 * k:2 * k + 2, :], f"o{k}")
                for b in range(4):
                    if b < 2:
                        split(8 + 2 * b)
                        split(9 + 2 * b)
                    dve.wait_ge(*m_pe[x](f"y{b}", c))
                    dve.wait_ge(*m_act[x](f"sg{b}", c))
                    to = mixT[:, bass.ds(c * 4 + b, 1), :].rearrange("p a n -> p (a n)")
                    if x == 0:
                        m_vec[x].mark(dve.tensor_tensor(to, psum[2 + b][:, :], sg[:, b, :], ALU.mult), f"mix{b}")
                    else:
                        m_vec[x].link(dve, dve.tensor_tensor(ytmp[:, b % 2, :], psum[2 + b][:, :], sg[:, b, :], ALU.mult), c)
                        m_vec[x].mark(dve.tensor_tensor(to, to, ytmp[:, b % 2, :], ALU.add), f"mix{b}")
            merge(0, 0)
            with dve.Fori(1, 2) as c:
                merge(0, c)
            merge(1, 0)
            with dve.Fori(1, 2) as c:
                merge(1, c)

            def post_norm(act_s, vec_s, bank, rowsig, prenorm, pt_tmp, hN):
                for t in range(NT):
                    dve.wait_ge(*act_s(f"sq{t}1"))
                    vec_s.mark(dve.tensor_tensor(stat[:, 2 * t:2 * t + 1], stat[:, 2 * t:2 * t + 1], stat[:, 2 * t + 1:2 * t + 2], ALU.add), f"ss{t}")
                    dve.wait_ge(*act_s(f"rms{t}"))
                    vec_s.link(dve, dve.reciprocal(stat[:, 12:13], stat[:, 12:13]))
                    if t == 0:
                        dve.wait_ge(*rowsig)
                    for c in range(2):
                        i = dve.scalar_tensor_tensor(pt_tmp[:, t, c * 512:(c + 1) * 512], psum[bank(t, c)][:, :], stat[:, 12:13],
                                                     row[:, c * 512:(c + 1) * 512], ALU.mult, ALU.mult)
                    vec_s.link(dve, i)
                    vec_s.mark(dve.tensor_tensor(XR[:, t, :], XR[:, t, :], pt_tmp[:, t, :], ALU.add), f"x{t}")
                    if prenorm:
                        dve.wait_ge(*act_s(f"hrms{t}"))
                        vec_s.link(dve, dve.reciprocal(stat[:, 14:15], stat[:, 14:15]))
                        vec_s.mark(dve.tensor_scalar(hN[:, t, :], XR[:, t, :], stat[:, 14:15], None, ALU.mult), f"hn{t}")
            for n in range(8):
                if n % 2 == 0:
                    dve.wait_ge(*o_act(f"mix{n // 2}"))
                    low(dve, o_vec, mixT[:, n:n + 2, :], mixT[:, n:n + 2, :], mix_hi[:, n:n + 2, :], f"mix{n // 2}")
                dve.wait_ge(*o_act(f"w{n}"))
                w = ring[n % 2][:, n // 2 * 2:n // 2 * 2 + 2, :]
                low(dve, o_vec, w, w, h_row[n % 4], f"w{n}")
            dve.wait_ge(*x_back("x"))
            post_norm(o_act, o_vec, lambda t, c: 2 * t + c, o_row("row"), True, o_tmp, o_hN)

            def turned(pe_s, vec_s, bank, scale):
                for t in range(NT):
                    for q in range(2):
                        dve.wait_ge(*pe_s(f"T{t}{q}"))
                        to = AT[:, 4 * q:4 * q + 4, t * P:(t + 1) * P]
                        fr = psum[bank(t, q)][:, :].rearrange("p (b c) -> p b c", b=4)
                        if scale is None:
                            i = dve.tensor_copy(to, fr)
                        else:
                            i = dve.tensor_tensor(to, fr, cols[:, scale + 4 * q:scale + 4 * q + 4].unsqueeze(2).broadcast_to([P, 4, P]), ALU.mult)
                        vec_s.mark(i, f"AT{t}{q}")
            u_vec.start()
            for n in range(3):
                dve.wait_ge(*u_act(f"w{n}"))
                w = ring[0][:, :, n * P:(n + 1) * P]
                low(dve, u_vec, w, w, h_col[n], f"w{n}")
            turned(o_pe, o_vec, lambda t, q: 2 * t + q, V_MLPPRE)

            for q in range(4):
                dve.wait_ge(*o_act(f"ATh{q}"))
                a = AT[:, 2 * q:2 * q + 2, :]
                low(dve, o_vec, a, a, at_hi[:, 2 * q:2 * q + 2, :], f"ATl{q}")

            def mlp_up(i):
                if not only(i):
                    u_vec.start()
                for g in range(0 if only(i) else -3, 16):
                    n = g + 3
                    if n < 16:
                        dve.wait_ge(*u_act(f"w{n}", i))
                        w = ring[n // 4 % 2][:, :, n % 4 * P:(n % 4 + 1) * P]
                        low(dve, u_vec, w, w, h_col[n % 4], f"w{n}")
                    if g < 0:
                        continue
                    dve.wait_ge(*u_pe(f"g{g}", i))
                    u_vec.mark(dve.tensor_scalar(ffT[:, bass.ds(i * 16 + g, 1), :].rearrange("p a n -> p (a n)"), psum[g % 4][:, :], 0.0, None, ALU.max), f"relu{g}")
            mlp_up(0)
            with dve.Fori(1, 2) as i:
                mlp_up(i)

            def mlp_down(c):
                dn_vec.start()
                for n in range(16):
                    dve.wait_ge(*dn_act(f"w{n}", c))
                    w = ring[n // 4 % 2][:, n % 4 * 2:n % 4 * 2 + 2, :]
                    low(dve, dn_vec, w, w, h_row[n % 4], f"w{n}")
                    dve.wait_ge(*dn_act(f"ff{n}", c))
                    low(dve, dn_vec, ff_lo[:, n % 4, :, :], ffT[:, 2 * n:2 * n + 2, :], ff_hi[:, n % 4, :, :], f"ff{n}")
            mlp_down(0)
            with dve.Fori(1, 2) as c:
                mlp_down(c)
            post_norm(d_act, d_vec, lambda t, c: 4 * c + t, f_row("row"), False, pt_tmp, hN)
            def split2(p):
                dve.wait_ge(*p_act(f"w{p}"))
                w, hi = piece2(p)
                low(dve, p_vec, w, w, hi, f"w{p}")
            split2(0)
            turned(t2_pe, t2_vec, lambda t, q: 4 * q + t, None)
            for q in range(4):
                dve.wait_ge(*p_pe(f"memT{q}"))
                p_vec.mark(dve.tensor_copy(memT[:, 2 * q:2 * q + 2, :], psum[q][:, :].rearrange("p (k n) -> p k n", k=2)), f"memT{q}")

            for name, x, hi in (("m", memT, mem_hi), ("AT", AT, at_hi)):
                if name == "AT":
                    for p in range(1, 4):
                        split2(p)
                for q in range(4):
                    dve.wait_ge(*p_act(f"{name}h{q}"))
                    low(dve, p_vec, x[:, 2 * q:2 * q + 2, :], x[:, 2 * q:2 * q + 2, :], hi[:, 2 * q:2 * q + 2, :], f"{name}l{q}")
            for g in range(22):
                for p in pieces_after(g):
                    split2(p)

            def attend_body(kind, b):
                pe_s, act_s, vec_s = at_pe[kind], at_act[kind], at_vec[kind]
                vec_s.start()
                units, nk = (4, 256) if kind == "m" else (8, 256 if kind == "n" else 512)
                for n in range(units + 1):
                    if n < units:
                        e, u = n // 4, n % 4
                        dve.wait_ge(*pe_s(f"S{n}", b))
                        src = psum[n % 3][:, 0:nk]
                        if kind == "n":
                            if n >= 2:
                                dve.wait_ge(*act_s(f"ex{n - 2}", b))
                            if n == 0:
                                dve.wait_ge(*at_pool["n"]("bias", b))
                            vec_s.mark(dve.tensor_tensor(sc[:, n % 2, 0:nk], src, bias[:, e, (0, 1, 1, 2)[u], :], ALU.add), f"s{n}")
                            dve.wait_ge(*vec_s(f"s{n}", b))
                            src = sc[:, n % 2, 0:nk]
                        vec_s.mark(dve.tensor_reduce(nmax[:, n:n + 1], src, AX, ALU.max, negate=True), f"max{n}")
                    if n:
                        m = n - 1
                        dve.wait_ge(*act_s(f"ex{m}", b))
                        vec_s.link(dve, dve.reciprocal(pinv[:, m:m + 1], psums[:, m:m + 1]), b)
                        vec_s.mark(dve.tensor_scalar(pr[:, m % 3, 0:nk], pr[:, m % 3, 0:nk], pinv[:, m:m + 1], None, ALU.mult), f"n{m}")
                dve.wait_ge(*pe_s(f"AV{units - 1}", b))
                if not only(b):
                    dve.wait_ge(*y_sd[kind]("y", b - 1))
                elif kind != "n":
                    dve.wait_ge(*y_sd["n" if kind == "m" else "m"]("y", 3))
                to = y_st
                if kind == "n":
                    for cb in range(4):
                        i = dve.tensor_copy(to.rearrange("p (r c) -> p r c", r=8)[:, :, cb * 16:cb * 16 + 16],
                                            psum[5][:, cb * P:(cb + 1) * P].rearrange("p (r q) -> p r q", r=8))
                else:
                    i = dve.tensor_copy(to, psum[5][:, :])
                vec_s.mark(i, "y")

            def attend(kind):
                attend_body(kind, 0)
                with dve.Fori(1, 4) as b:
                    attend_body(kind, b)

            attend("n")
            for p in pieces_after(25):
                split2(p)
            for t in range(NT):
                dve.wait_ge(*r_pool(f"sq{t}"))
                i = dve.tensor_reduce(gst[:, t, :], ro[:, t, :].rearrange("p (h d) -> p h d", h=10), AX, ALU.add)
            r_vec.mark(i, "ss")
            attend("m")
            dve.wait_ge(*r_act("root"))
            r_vec.link(dve, dve.reciprocal(gst, gst))
            for t in range(NT):
                x = qkN[:, t, 0:640].rearrange("p (h d) -> p h d", h=10)
                r_vec.mark(dve.tensor_tensor(x, x, gst[:, t, :].unsqueeze(2).broadcast_to([P, 10, 64]), ALU.mult), f"scaled{t}")
            for t in range(NT):
                dve.wait_ge(*r_pool(f"gain{t}"))
                x = qkN[:, t, 0:640].rearrange("p (h d two) -> p h d two", h=10, two=2)
                o = ro[:, t, :].rearrange("p (h d two) -> p h d two", h=10, two=2)
                cb, sb_ = [v[:, t:t + 1, :].broadcast_to([P, 10, 32]) for v in (cosN, sinN)]
                a3, b3 = [v.rearrange("p (h d) -> p h d", h=10) for v in (ra, rb)]
                for out_at, (c0, c1, op) in enumerate(((cb, sb_, ALU.subtract), (sb_, cb, ALU.add))):
                    dve.tensor_tensor(a3, x[:, :, :, 0], c0, ALU.mult)
                    r_vec.link(dve, dve.tensor_tensor(b3, x[:, :, :, 1], c1, ALU.mult))
                    i = dve.tensor_tensor(o[:, :, :, out_at], a3, b3, op)
                    if out_at == 0 or t < 3:
                        r_vec.link(dve, i)
            r_vec.mark(i, "rope3")
            attend("g")

            def merge2(c):
                mg_vec.start()

                def split(i):
                    dve.wait_ge(*mg_act(f"w{i}", c))
                    w, hi = piece3(i)
                    low(dve, mg_vec, w, w, hi, f"w{i}")
                for i in range(4):
                    split(i)
                for g, b, part in events2:
                    if part == "br":
                        dve.wait_ge(*mg_pe(f"br{g}{b}", c))
                        dve.wait_ge(*mg_act(f"sg{g}{b}", c))
                        to = mgT[:, bass.ds(c * 4 + b, 1), :].rearrange("p a n -> p (a n)")
                        if g == 0:
                            i = dve.tensor_tensor(to, psum[4 + b][:, :], sg2[:, b, :], ALU.mult)
                        else:
                            mg_vec.link(dve, dve.tensor_tensor(mtmp[:, b % 2, :], psum[4 + b][:, :], sg2[:, b, :], ALU.mult), c)
                            i = dve.tensor_tensor(to, to, mtmp[:, b % 2, :], ALU.add)
                        mg_vec.mark(i, f"m{g}{b}")
                    i = piece_done(g, b, part)
                    if i is not None and i + 4 < 18:
                        split(i + 4)
                    if only(c) and (b, part) == (1, "gate"):
                        for k in range(2 * g, 2 * g + 2):
                            dve.wait_ge(*y_act(f"y{k}"))
                            y2 = yT[:, 2 * k:2 * k + 2, :]
                            low(dve, y_vec, y2, y2, yT_hi[:, 2 * k:2 * k + 2, :], f"y{k}")
            merge2(0)
            with dve.Fori(1, 2) as c:
                merge2(c)

            def normed(act_s, vec_s, src, rows, rows_sig):
                st6 = gst.rearrange("p t h -> p (t h)")
                for t in range(NT):
                    for c in range(2):
                        i = dve.bn_stats(st6[:, 6 * c:6 * c + 6], src[:, t, c * 512:(c + 1) * 512])
                    vec_s.link(dve, i)
                    i = dve.bn_aggr(stat[:, 2 * t:2 * t + 2], st6[:, 0:12])
                    if t < NT - 1:
                        vec_s.link(dve, i)
                vec_s.mark(i, "var")
                dve.wait_ge(*act_s("root"))
                vec_s.link(dve, dve.reciprocal(stat[:, 8:12], stat[:, 8:12]))
                dve.wait_ge(*rows_sig)
                for t in range(NT):
                    v = src[:, t, :]
                    vec_s.link(dve, dve.scalar_tensor_tensor(v, v, stat[:, 2 * t:2 * t + 1], rows[:, 0, :], ALU.subtract, ALU.mult))
                    vec_s.mark(dve.scalar_tensor_tensor(XR[:, t, :], v, stat[:, 8 + t:9 + t], rows[:, 1, :], ALU.mult, ALU.add), f"x{t}")
            for n in range(8):
                if n % 2 == 0:
                    dve.wait_ge(*l_act(f"mg{n // 2}"))
                    low(dve, l_vec, mgT[:, n:n + 2, :], mgT[:, n:n + 2, :], mg_hi[:, n:n + 2, :], f"mg{n // 2}")
                dve.wait_ge(*l_act(f"w{n}"))
                w = ring[n % 2][:, n // 2 * 2:n // 2 * 2 + 2, :]
                low(dve, l_vec, w, w, h_row[n % 4], f"w{n}")
            for t in range(NT):
                for c in range(2):
                    dve.wait_ge(*l_pe(f"m{t}{c}"))
                    i = dve.scalar_tensor_tensor(v2[:, t, c * 512:(c + 1) * 512], XR[:, t, c * 512:(c + 1) * 512], ALPHA, psum[2 * t + c][:, :],
                                                 ALU.mult, ALU.add)
            l_vec.link(dve, i)
            normed(l_act, l_vec, v2, lnrow, l_row("ln1_b_2"))
            turned(q_pe, q_vec, lambda t, q: 2 * t + q, None)
            for t in range(NT):
                i = dve.tensor_scalar(acc[:, t, :], XR[:, t, :], ALPHA, None, ALU.mult)
            q_vec.link(dve, dve.memset(affT[0:NE, :], 1.0))
            dve.wait_ge(*q_pe("logits"))
            lg = psum[0][:, 0:NT * NE].rearrange("p (t e) -> p t e", t=NT)
            q_vec.link(dve, dve.tensor_reduce(lmax, lg, AX, ALU.max))
            q_vec.mark(dve.tensor_tensor(affN, lg, lmax.unsqueeze(2).broadcast_to([P, NT, NE]), ALU.subtract), "less")
            dve.wait_ge(*q_act("exp"))
            q_vec.link(dve, dve.tensor_reduce(lsum, affN, AX, ALU.add))
            q_vec.link(dve, dve.reciprocal(lsum, lsum))
            q_vec.mark(dve.tensor_tensor(affN, affN, lsum.unsqueeze(2).broadcast_to([P, NT, NE]), ALU.mult), "aff")
            dve.wait_ge(*q_pe("affT"))
            q_vec.link(dve, dve.tensor_copy(wrk[0:NE, :], psum[1][0:NE, :]))
            for r in range(EC // 8):
                q_vec.link(dve, dve.max(m8[0:NE, :], wrk[0:NE, :]))
                q_vec.link(dve, dve.match_replace(wrk[0:NE, :], m8[0:NE, :], wrk[0:NE, :], -1.0))
            q_vec.link(dve, dve.tensor_scalar(wrk[0:NE, :], wrk[0:NE, :], 0.0, None, ALU.is_lt))
            q_vec.link(dve, dve.tensor_tensor_scan(cum[0:NE, :], affT[0:NE, :], wrk[0:NE, :], 0.0, ALU.mult, ALU.add))
            q_vec.mark(dve.tensor_tensor(cum[0:NE, :], cum[0:NE, :], wrk[0:NE, :], ALU.mult), "pos")
            dve.wait_ge(*q_pe("posN"))
            dve.wait_ge(*q_ld("wr"))
            q_vec.link(dve, dve.tensor_copy(posN, psum[2][:, 0:NT * NE].rearrange("p (t e) -> p t e", t=NT)))

            def experts(p):
                e_vec.start()
                four = [P, NT, 2, EC]
                v4 = lambda x: x.rearrange("p t (e j) -> p t e j", e=2)
                of = lambda x: x[:, :, bass.ds(p * 2, 2)].unsqueeze(3).broadcast_to(four)
                if not only(p):
                    dve.wait_ge(*e_pe("SGT", p - 1))
                e_vec.mark(dve.tensor_tensor(v4(SP), iota.unsqueeze(1).unsqueeze(1).broadcast_to(four), of(posN), ALU.is_equal), "SP")
                dve.wait_ge(*e_vec("SP", p))
                e_vec.mark(dve.tensor_tensor(v4(SG), v4(SP), of(affN), ALU.mult), "SG")
                dve.wait_ge(*e_pe("SGT", p))
                if not only(p):
                    dve.wait_ge(*e_pe("y7", p - 1))
                e_vec.mark(dve.tensor_copy(SGT, psum[2][:, :]), "SGT")
                for f in range(2):
                    dve.wait_ge(*e_pe(f"group{2 * f + 1}", p))
                    dve.wait_ge(*e_act(f"silu{f}", p))
                    e_vec.mark(dve.tensor_tensor(ga[:, f, :], psum[4 + 2 * f][:, :], ga[:, f, :], ALU.mult), f"ga{f}")
                for m in range(8):
                    t, n = m // 2, m % 2
                    dve.wait_ge(*e_pe(f"y{m}", p))
                    a = acc[:, t, n * 512:(n + 1) * 512]
                    e_vec.mark(dve.tensor_tensor(a, psum[(0, 1, 2, 6)[m % 4]][:, :], a, ALU.add), f"acc{m}")
            experts(0)
            with dve.Fori(1, NE // 2) as p:
                experts(p)
            dve.wait_ge(*e_vec("acc7", NE // 2 - 1))
            normed(f_act, f_vec, acc, lnrow2, f_rowl("ln2_b_2"))


def constants():
    i = np.arange(P)
    ident = np.eye(P)
    ones = np.ones((P, P))
    incl = (i[:, None] <= i[None, :]).astype(float)
    lv = []
    for s in range(LEVELS):
        w = 1 << s
        same = i[:, None] // (2 * w) == i[None, :] // (2 * w)
        lv.append(-(same & (i[:, None] // w % 2 == 0) & (i[None, :] // w % 2 == 1)).astype(float))
    return np.concatenate([ident, ones, incl] + lv, axis=1).astype(np.float32)


def retention_tables():
    inv = 10000.0 ** (-np.arange(0, B_DK, 2, dtype=np.float32) / B_DK)
    ang = np.arange(SEQ, dtype=np.float32)[None, :] * inv.astype(np.float32)[:, None]
    lg = np.log1p(-np.exp2(-5.0 - np.arange(B_HEADS)))
    m, c = np.arange(P)[:, None], np.arange(SEQ)[None, :]
    keep = c // 64 >= m // 64
    decay = [np.where(keep, np.exp(g * np.abs(c - m)), 0.0) * B_DK ** -0.5 for g in lg]
    return (np.concatenate([np.cos(ang), np.sin(ang)], axis=1).astype(np.float32),
            np.concatenate(decay, axis=1).astype(np.float32))


def rope_rows():
    t = np.arange(SEQ)
    inv = (10000.0 ** (-np.arange(0, 32, 2, dtype=np.float32) / 32)).astype(np.float32)
    ang = np.concatenate([(t // 64).astype(np.float32)[:, None] * inv, (t % 64).astype(np.float32)[:, None] * inv], axis=-1)
    by = lambda v: v.reshape(NT, P, 32).transpose(1, 0, 2).reshape(P, NT * 32)
    return np.concatenate([by(np.cos(ang)), by(np.sin(ang))], axis=1).astype(np.float32)


def neighbourhood(rpb):
    q, k = np.arange(P), np.arange(256)
    r, qq, kr, kk = q[:, None] // 16, q[:, None] % 16, k[None, :] // 32, k[None, :] % 32
    padded = np.pad(rpb, ((0, 0), (0, 0), (16, 17)))
    bias, mask = [], []
    for o, start in ((0, np.maximum(qq - 8, 0)), (-8, qq), (-16, np.minimum(qq + 8, 16))):
        bias.append(padded[:, kr - r + 7, kk - qq + 15 + o + 16])
        mask.append(np.where((kk >= start) & (kk < start + 16), 0.0, -1e30))
    bias = np.stack(bias, axis=1)
    bias = bias.reshape(4, 2, 3, P, 256).transpose(0, 3, 1, 2, 4).reshape(4, P, 1536)
    return np.ascontiguousarray(bias), np.concatenate(mask, axis=1).astype(np.float32)


def layout(inputs):
    g = {k: np.asarray(v) for k, v in inputs.items()}
    one = {k: np.ascontiguousarray(v[0]) for k, v in g.items()}

    def by_partition(v):
        return v.reshape(-1, P).T

    pad = lambda v: np.pad(v.reshape(-1, 1), ((0, P - v.size), (0, 0)))
    conv = one["conv_a"].reshape(4, 32, P).transpose(2, 1, 0).reshape(P, 128)
    cols = np.concatenate([
        by_partition(one["norm_mix_pre"]), by_partition(one["norm_mlp_pre"]), conv, by_partition(one["norm_a"]),
        by_partition(one["norm_b"]), by_partition(one["b_gate_2"]), pad(one["a_log"]), pad(one["dt_bias"]), np.repeat(np.eye(2, dtype=np.float32), 64, axis=0)], axis=1)
    t = {"cols": np.ascontiguousarray(cols), "consts": constants()}
    t["rope_b"], t["decay_b"] = retention_tables()
    for k in ("x", "w_in", "w_br_a", "w_br_b", "w_out", "w_up", "w_down"):
        t[k] = one[k]
    t["rope_g"] = rope_rows()
    t["na_bias"], t["na_mask"] = neighbourhood(one["na_rpb_2"])
    t["iota"] = np.broadcast_to(np.arange(1, EC + 1, dtype=np.float32), (P, EC)).copy()
    t["gains"] = np.concatenate([one["gqa_q_gain_2"], one["gqa_k_gain_2"]]).reshape(1, 128)
    t["mem_2"] = g["mem_2"][0]
    t["w_branch_2"] = one["w_branch_2"].reshape(3 * 512, DM)
    for k in ("w_in_2", "w_mem_kv_2", "w_out_2", "w_router_2", "w_gate_up_2", "w_down_2"):
        t[k] = one[k]
    for k in ("norm_mix_post", "norm_mlp_post", "ln1_g_2", "ln1_b_2", "ln2_g_2", "ln2_b_2"):
        t[k] = one[k].reshape(1, DM)
    return t


def kernel(**inputs):
    import concourse.bacc as bacc
    from concourse.bass_utils import run_bass_kernel_spmd

    t = layout(inputs)
    for _ in range(2):
        nc = bacc.Bacc("TRN2", target_bir_lowering=False, num_devices=1)
        aps = {k: nc.dram_tensor(k + "_in", v.shape, F32, kind="ExternalInput").ap() for k, v in t.items()}
        out = nc.dram_tensor("out", (SEQ, DM), F32, kind="ExternalOutput").ap()
        build(nc, aps, out)
    r = run_bass_kernel_spmd(nc, [{k + "_in": v for k, v in t.items()}], core_ids=[0])
    return r.results[0]["out"].reshape(1, SEQ, DM)
```
